# Optimizing a Trainium2 kernel written in Bass

```python
import math
import jax
import jax.numpy as jnp
from jax import lax
import numpy as np
import jax, jax.numpy as jnp

D_MODEL = 1024
BATCH = 1
SEQ = 256
DEPTH = 2

GRID_W = 64
CTX_LEN = 256
N_MIXERS = 2
N_MLA_LAYERS = (DEPTH + 1) // 2
N_GDN_LAYERS = DEPTH // 2
DEEPNORM_ALPHA = (2.0 * DEPTH) ** 0.25
DEEPNORM_BETA = (8.0 * DEPTH) ** -0.25
N_MOD = 6
LN_EPS = 1e-5
RMS_EPS = 1e-6

MLA_HEADS = D_MODEL // 128
MLA_Q_RANK = D_MODEL // 2
MLA_KV_RANK = D_MODEL // 4
MLA_NOPE = 128
MLA_ROPE = 64
MLA_V = 128
MLA_IN_W = MLA_Q_RANK + MLA_KV_RANK + MLA_ROPE
MLA_SCALE = (MLA_NOPE + MLA_ROPE) ** -0.5
Q_BLOCK = 128
ROPE_THETA = 10000.0

GDN_K_HEADS = D_MODEL // 128
GDN_V_HEADS = 2 * GDN_K_HEADS
GDN_DK = 128
GDN_DV = 128
GDN_KW = GDN_K_HEADS * GDN_DK
GDN_VW = GDN_V_HEADS * GDN_DV
GDN_QKV_W = 2 * GDN_KW + GDN_VW
GDN_IN_W = GDN_QKV_W + GDN_VW + 4 * GDN_V_HEADS
GDN_CONV = 5
CHUNK = 64

D_FF = int(math.ceil(8 * D_MODEL / 3 / 256)) * 256


def layer_norm(x, g, b):
    xf = x.astype(jnp.float32)
    mu = jnp.mean(xf, axis=-1, keepdims=True)
    var = jnp.mean(jnp.square(xf - mu), axis=-1, keepdims=True)
    return ((xf - mu) * lax.rsqrt(var + LN_EPS) * g + b).astype(x.dtype)

def rms_norm(x, g):
    xf = x.astype(jnp.float32)
    y = xf * lax.rsqrt(jnp.mean(jnp.square(xf), axis=-1, keepdims=True) + RMS_EPS) * g
    return y.astype(x.dtype)

def l2_norm(x):
    xf = x.astype(jnp.float32)
    return (xf * lax.rsqrt(jnp.sum(jnp.square(xf), axis=-1, keepdims=True) + RMS_EPS)).astype(x.dtype)

def modulate(h, shift, scale):
    return h * (1 + scale) + shift

def axial_rope_tables(n_tokens):
    rows = n_tokens // GRID_W
    row = jnp.broadcast_to(jnp.arange(rows)[:, None], (rows, GRID_W)).reshape(-1).astype(jnp.float32)
    col = jnp.broadcast_to(jnp.arange(GRID_W)[None, :], (rows, GRID_W)).reshape(-1).astype(jnp.float32)
    n_freq = MLA_ROPE // 4
    axis_dim = MLA_ROPE // 2
    inv_freq = ROPE_THETA ** (-(2.0 * jnp.arange(n_freq, dtype=jnp.float32)) / axis_dim)
    ang = jnp.concatenate([row[:, None] * inv_freq, col[:, None] * inv_freq], axis=-1)
    return jnp.cos(ang), jnp.sin(ang)

def apply_axial_rope(u, cos, sin):
    B, T, H, _ = u.shape
    f = MLA_ROPE // 4
    u = u.reshape(B, T, H, 2, 2, f)
    u1, u2 = u[..., 0, :], u[..., 1, :]
    cs = cos.reshape(1, T, 1, 2, f).astype(u.dtype)
    sn = sin.reshape(1, T, 1, 2, f).astype(u.dtype)
    out = jnp.stack([u1 * cs - u2 * sn, u2 * cs + u1 * sn], axis=-2)
    return out.reshape(B, T, H, MLA_ROPE)

def softmax_attend(q, k, v):
    s = jnp.einsum('bqhd,bkhd->bhqk', q, k).astype(jnp.float32) * MLA_SCALE
    p = jax.nn.softmax(s, axis=-1).astype(v.dtype)
    return jnp.einsum('bhqk,bkhd->bqhd', p, v)

def blockwise_attend(q, k, v):
    B, T, H, dq = q.shape
    qb = jnp.moveaxis(q.reshape(B, T // Q_BLOCK, Q_BLOCK, H, dq), 1, 0)
    o = lax.map(lambda blk: softmax_attend(blk, k, v), qb)
    return jnp.moveaxis(o, 0, 1).reshape(B, T, H, v.shape[-1])

def mla_project(h, w_in, q_norm, kv_norm, w_q_up, w_kv_up, rope):
    B, T, _ = h.shape
    lat = h @ w_in
    cq = rms_norm(lat[..., :MLA_Q_RANK], q_norm)
    ckv = rms_norm(lat[..., MLA_Q_RANK:MLA_Q_RANK + MLA_KV_RANK], kv_norm)
    k_rope = lat[..., MLA_Q_RANK + MLA_KV_RANK:][:, :, None, :]
    q = (cq @ w_q_up).reshape(B, T, MLA_HEADS, MLA_NOPE + MLA_ROPE)
    kv = (ckv @ w_kv_up).reshape(B, T, MLA_HEADS, MLA_NOPE + MLA_V)
    q_nope, q_rope = q[..., :MLA_NOPE], q[..., MLA_NOPE:]
    k_nope, v = kv[..., :MLA_NOPE], kv[..., MLA_NOPE:]
    if rope is not None:
        cos, sin = rope
        q_rope = apply_axial_rope(q_rope, cos, sin)
        k_rope = apply_axial_rope(k_rope, cos, sin)
    k_rope = jnp.broadcast_to(k_rope, (B, T, MLA_HEADS, MLA_ROPE))
    q = jnp.concatenate([q_nope, q_rope], axis=-1)
    k = jnp.concatenate([k_nope, k_rope], axis=-1)
    return q, k, v

def mla_mixer(h_ctx, h_lat, w_in, q_norm, kv_norm, w_q_up, w_kv_up, w_out, rope):
    q_c, k_c, v_c = mla_project(h_ctx, w_in, q_norm, kv_norm, w_q_up, w_kv_up, None)
    q_l, k_l, v_l = mla_project(h_lat, w_in, q_norm, kv_norm, w_q_up, w_kv_up, rope)
    o_c = softmax_attend(q_c, k_c, v_c)
    o_l = blockwise_attend(q_l, jnp.concatenate([k_c, k_l], axis=1), jnp.concatenate([v_c, v_l], axis=1))

    def out(o):
        B, T = o.shape[:2]
        return o.reshape(B, T, MLA_HEADS * MLA_V) @ w_out

    return out(o_c), out(o_l)

def short_conv(u, w):
    out = lax.conv_general_dilated(u, w[:, None, :], window_strides=(1,),
                                   padding=[(GDN_CONV // 2, GDN_CONV // 2)],
                                   dimension_numbers=('NWC', 'WIO', 'NWC'),
                                   feature_group_count=u.shape[-1])
    return jax.nn.silu(out)

def gated_delta_chunked(q, k, v, beta, g, s0):
    B, T, H, dk = q.shape
    dv = v.shape[-1]
    n = T // CHUNK
    f32 = jnp.float32

    def chunks(a):
        return jnp.moveaxis(a.astype(f32).reshape((B, n, CHUNK) + a.shape[2:]), 3, 1)

    qc, kc, vc, bc, gc = chunks(q), chunks(k), chunks(v), chunks(beta), chunks(g)
    gcum = jnp.cumsum(gc, axis=-1)
    idx = jnp.arange(CHUNK)
    incl = idx[:, None] >= idx[None, :]
    strict = idx[:, None] > idx[None, :]
    diff = gcum[..., :, None] - gcum[..., None, :]
    decay = jnp.where(incl, jnp.exp(jnp.where(incl, diff, 0.0)), 0.0)
    kb = kc * bc[..., None]
    lmat = jnp.where(strict, jnp.einsum('bhnid,bhnjd->bhnij', kb, kc) * decay, 0.0)
    a = lmat + jnp.eye(CHUNK, dtype=f32)
    rhs = jnp.concatenate([vc * bc[..., None], kb * jnp.exp(gcum)[..., None]], axis=-1)
    sol = lax.linalg.triangular_solve(a, rhs, left_side=True, lower=True, unit_diagonal=True)
    u, w = sol[..., :dv], sol[..., dv:]
    attn = jnp.einsum('bhnid,bhnjd->bhnij', qc, kc) * decay
    q_dec = qc * jnp.exp(gcum)[..., None]
    k_dec = kc * jnp.exp(gcum[..., -1:] - gcum)[..., None]
    g_last = jnp.exp(gcum[..., -1])
    xs = tuple(jnp.moveaxis(t, 2, 0) for t in (w, u, q_dec, k_dec, attn, g_last))

    def step(S, inp):
        w_i, u_i, qd_i, kd_i, a_i, gl_i = inp
        v_new = u_i - jnp.einsum('bhck,bhkv->bhcv', w_i, S)
        o_i = jnp.einsum('bhck,bhkv->bhcv', qd_i, S) + jnp.einsum('bhij,bhjv->bhiv', a_i, v_new)
        S = S * gl_i[..., None, None] + jnp.einsum('bhck,bhcv->bhkv', kd_i, v_new)
        return S, o_i

    s_final, o = lax.scan(step, s0, xs)
    o = jnp.transpose(o, (1, 0, 3, 2, 4)).reshape(B, T, H, dv)
    return o.astype(v.dtype), s_final

def gdn_project(h, w_in, conv_w, a_log, dt_bias):
    B, T, _ = h.shape
    proj = h @ w_in
    qkv = short_conv(proj[..., :GDN_QKV_W], conv_w)
    rep = GDN_V_HEADS // GDN_K_HEADS
    q = l2_norm(qkv[..., :GDN_KW].reshape(B, T, GDN_K_HEADS, GDN_DK)) * (GDN_DK ** -0.5)
    k = l2_norm(qkv[..., GDN_KW:2 * GDN_KW].reshape(B, T, GDN_K_HEADS, GDN_DK))
    q = jnp.repeat(q, rep, axis=2)
    k = jnp.repeat(k, rep, axis=2)
    v = qkv[..., 2 * GDN_KW:].reshape(B, T, GDN_V_HEADS, GDN_DV)
    z = proj[..., GDN_QKV_W:GDN_QKV_W + GDN_VW].reshape(B, T, GDN_V_HEADS, GDN_DV)
    ba = proj[..., GDN_QKV_W + GDN_VW:].astype(jnp.float32).reshape(B, T, 2, 2, GDN_V_HEADS)
    beta = jax.nn.sigmoid(ba[..., 0, :])
    g = -jnp.exp(a_log.astype(jnp.float32)) * jax.nn.softplus(ba[..., 1, :] + dt_bias.astype(jnp.float32))
    return q, k, v, z, beta, g

def gdn_mixer(h_ctx, h_lat, w_in, conv_w, a_log, dt_bias, norm_w, w_out):
    ctx_t = gdn_project(h_ctx, w_in, conv_w, a_log, dt_bias)
    lat_t = gdn_project(h_lat, w_in, conv_w, a_log, dt_bias)
    s0 = jnp.zeros((h_lat.shape[0], GDN_V_HEADS, GDN_DK, GDN_DV), jnp.float32)

    def one_direction(d):
        flip = (lambda a: jnp.flip(a, axis=1)) if d == 1 else (lambda a: a)

        def run(t, s_init):
            q, k, v, _, beta, g = t
            o, s_fin = gated_delta_chunked(flip(q), flip(k), flip(v), flip(beta[:, :, d]), flip(g[:, :, d]), s_init)
            return flip(o), s_fin

        o_ctx, s_ctx = run(ctx_t, s0)
        o_lat, _ = run(lat_t, s_ctx)
        return o_ctx, o_lat

    oc_f, ol_f = one_direction(0)
    oc_b, ol_b = one_direction(1)

    def finish(o, z):
        B, T = o.shape[:2]
        y = rms_norm(o, norm_w) * jax.nn.silu(z)
        return y.reshape(B, T, GDN_VW) @ w_out

    return finish(oc_f + oc_b, ctx_t[3]), finish(ol_f + ol_b, lat_t[3])

def swiglu(h, w_in, w_out):
    gate, up = jnp.split(h @ w_in, 2, axis=-1)
    return (jax.nn.silu(gate) * up) @ w_out

def first_inputs(seed: int = 0) -> dict:
    key = jax.random.key(seed)
    ks = jax.random.split(key, 24)
    f32 = jnp.float32

    def nrm(i, shape, std=1.0):
        return std * jax.random.normal(ks[i], shape, f32)

    D = D_MODEL
    nA, nB = N_MLA_LAYERS, N_GDN_LAYERS
    a_log = jnp.log(jax.random.uniform(ks[20], (nB, 2, GDN_V_HEADS), f32, 1.0, 16.0))
    dt = jnp.exp(jax.random.uniform(ks[21], (nB, 2, GDN_V_HEADS), f32, math.log(1e-3), math.log(1e-1)))
    dt_bias = dt + jnp.log(-jnp.expm1(-dt))
    return {
        'x': nrm(0, (BATCH, SEQ, D)),
        'c': nrm(1, (BATCH, D)),
        'ctx': nrm(2, (BATCH, CTX_LEN, D)),
        'c_ctx': nrm(3, (D,)),
        'w_mod': nrm(4, (DEPTH, D, N_MOD * D), D ** -0.5),
        'b_mod': nrm(5, (DEPTH, N_MOD * D), 0.01),
        'ln1_g': 1.0 + nrm(6, (DEPTH, D), 0.02),
        'ln1_b': nrm(7, (DEPTH, D), 0.01),
        'ln2_g': 1.0 + nrm(8, (DEPTH, D), 0.02),
        'ln2_b': nrm(9, (DEPTH, D), 0.01),
        'w_ffn_in': nrm(10, (DEPTH, D, 2 * D_FF), D ** -0.5),
        'w_ffn_out': nrm(11, (DEPTH, D_FF, D), DEEPNORM_BETA * D_FF ** -0.5),
        'mla_w_in': nrm(12, (nA, D, MLA_IN_W), D ** -0.5),
        'mla_q_norm': 1.0 + nrm(13, (nA, MLA_Q_RANK), 0.02),
        'mla_kv_norm': 1.0 + nrm(14, (nA, MLA_KV_RANK), 0.02),
        'mla_w_q_up': nrm(15, (nA, MLA_Q_RANK, MLA_HEADS * (MLA_NOPE + MLA_ROPE)), MLA_Q_RANK ** -0.5),
        'mla_w_kv_up': nrm(16, (nA, MLA_KV_RANK, MLA_HEADS * (MLA_NOPE + MLA_V)), MLA_KV_RANK ** -0.5),
        'mla_w_out': nrm(17, (nA, MLA_HEADS * MLA_V, D), DEEPNORM_BETA * (MLA_HEADS * MLA_V) ** -0.5),
        'gdn_w_in': nrm(18, (nB, D, GDN_IN_W), D ** -0.5),
        'gdn_conv': nrm(19, (nB, GDN_CONV, GDN_QKV_W), GDN_CONV ** -0.5),
        'gdn_a_log': a_log,
        'gdn_dt_bias': dt_bias,
        'gdn_norm': 1.0 + nrm(22, (nB, GDN_DV), 0.02),
        'gdn_w_out': nrm(23, (nB, GDN_VW, D), DEEPNORM_BETA * GDN_VW ** -0.5),
    }

def first_block(x, c, ctx, c_ctx, w_mod, b_mod, ln1_g, ln1_b, ln2_g, ln2_b, w_ffn_in, w_ffn_out,
              mla_w_in, mla_q_norm, mla_kv_norm, mla_w_q_up, mla_w_kv_up, mla_w_out,
              gdn_w_in, gdn_conv, gdn_a_log, gdn_dt_bias, gdn_norm, gdn_w_out):
    rope = axial_rope_tables(x.shape[1])
    h_lat, h_ctx = x, ctx
    for i in range(DEPTH):
        last = i == DEPTH - 1
        mod_lat = jnp.split((jax.nn.silu(c) @ w_mod[i] + b_mod[i])[:, None, :], N_MOD, axis=-1)
        mod_ctx = jnp.split(jax.nn.silu(c_ctx) @ w_mod[i] + b_mod[i], N_MOD, axis=-1)
        u_ctx = modulate(h_ctx, mod_ctx[0], mod_ctx[1])
        u_lat = modulate(h_lat, mod_lat[0], mod_lat[1])
        j = i // N_MIXERS
        if i % N_MIXERS == 0:
            y_ctx, y_lat = mla_mixer(u_ctx, u_lat, mla_w_in[j], mla_q_norm[j], mla_kv_norm[j],
                                     mla_w_q_up[j], mla_w_kv_up[j], mla_w_out[j], rope)
        else:
            y_ctx, y_lat = gdn_mixer(u_ctx, u_lat, gdn_w_in[j], gdn_conv[j], gdn_a_log[j],
                                     gdn_dt_bias[j], gdn_norm[j], gdn_w_out[j])
        h_lat = layer_norm(DEEPNORM_ALPHA * h_lat + mod_lat[2] * y_lat, ln1_g[i], ln1_b[i])
        f_lat = swiglu(modulate(h_lat, mod_lat[3], mod_lat[4]), w_ffn_in[i], w_ffn_out[i])
        h_lat = layer_norm(DEEPNORM_ALPHA * h_lat + mod_lat[5] * f_lat, ln2_g[i], ln2_b[i])
        if not last:
            h_ctx = layer_norm(DEEPNORM_ALPHA * h_ctx + mod_ctx[2] * y_ctx, ln1_g[i], ln1_b[i])
            f_ctx = swiglu(modulate(h_ctx, mod_ctx[3], mod_ctx[4]), w_ffn_in[i], w_ffn_out[i])
            h_ctx = layer_norm(DEEPNORM_ALPHA * h_ctx + mod_ctx[5] * f_ctx, ln2_g[i], ln2_b[i])
    return h_lat


D_MIX = D_MODEL
GLA_HEADS = 4
GLA_DV = 64
GLA_DK = GLA_DV // 2
GLA_GATE_RANK = 16
GLA_TAU = 16.0
GLA_CHUNK = 64
CONV_CH = D_MIX // 4
CONV_WIDTH = 31
SWA_Q_HEADS = 8
SWA_KV_HEADS = 2
SWA_HEAD_DIM = 64
SWA_WINDOW = 128
SWA_BLOCK = 128
D_FF_2 = 2816


def _in_proj_widths():
    return [
        GLA_HEADS * GLA_DK,
        GLA_HEADS * GLA_DK,
        GLA_HEADS * GLA_DV,
        GLA_HEADS * GLA_DV,
        GLA_GATE_RANK,
        CONV_CH,
        CONV_CH,
        SWA_Q_HEADS * SWA_HEAD_DIM,
        SWA_KV_HEADS * SWA_HEAD_DIM,
        SWA_KV_HEADS * SWA_HEAD_DIM,
    ]

def rmsnorm(x, g):
    x32 = x.astype(jnp.float32)
    y = x32 * lax.rsqrt(jnp.mean(x32 * x32, axis=-1, keepdims=True) + RMS_EPS)
    return (y * g.astype(jnp.float32)).astype(x.dtype)

def swiglu_ffn(h, w_gate, w_up, w_down):
    return (jax.nn.silu(h @ w_gate) * (h @ w_up)) @ w_down

def gla_group(q, k, v, glog, r, norm_g):
    B, S, H, DK = q.shape
    DV = v.shape[-1]
    C = GLA_CHUNK
    N = S // C
    f32 = jnp.float32

    def chunks(t):
        return t.astype(f32).reshape(B, N, C, H, t.shape[-1]).transpose(1, 0, 3, 2, 4)

    qc = chunks(q) * (DK ** -0.5)
    kc = chunks(k)
    vc = chunks(v)
    bc = jnp.cumsum(chunks(glog), axis=3)
    causal = jnp.tril(jnp.ones((C, C), dtype=bool))[:, :, None]

    def step(state, inp):
        qn, kn, vn, bn = inp
        diff = bn[:, :, :, None, :] - bn[:, :, None, :, :]
        decay = jnp.where(causal, jnp.exp(jnp.where(causal, diff, 0.0)), 0.0)
        attn = jnp.einsum('bhid,bhjd,bhijd->bhij', qn, kn, decay)
        o = jnp.einsum('bhij,bhjv->bhiv', attn, vn) \
            + jnp.einsum('bhid,bhdv->bhiv', qn * jnp.exp(bn), state)
        b_last = bn[:, :, -1:, :]
        state = jnp.exp(b_last[:, :, 0, :])[..., None] * state \
            + jnp.einsum('bhjd,bhjv->bhdv', kn * jnp.exp(b_last - bn), vn)
        return state, o

    s0 = jnp.zeros((B, H, DK, DV), f32)
    _, o = lax.scan(step, s0, (qc, kc, vc, bc))
    o = o.transpose(1, 0, 3, 2, 4).reshape(B, S, H, DV)
    o = o * lax.rsqrt(jnp.mean(o * o, axis=-1, keepdims=True) + RMS_EPS) * norm_g.astype(f32)
    o = o.reshape(B, S, H * DV) * jax.nn.silu(r.astype(f32))
    return o.astype(q.dtype)

def conv_group(a, g, conv_w, conv_b, ln_g, ln_b):
    u = a * jax.nn.sigmoid(g)
    y = lax.conv_general_dilated(
        u, conv_w[:, None, :].astype(u.dtype), window_strides=(1,),
        padding=[(CONV_WIDTH - 1, 0)], dimension_numbers=('NWC', 'WIO', 'NWC'),
        feature_group_count=CONV_CH) + conv_b
    y32 = y.astype(jnp.float32)
    mu = jnp.mean(y32, axis=-1, keepdims=True)
    var = jnp.mean(jnp.square(y32 - mu), axis=-1, keepdims=True)
    y32 = (y32 - mu) * lax.rsqrt(var + LN_EPS) * ln_g.astype(jnp.float32) + ln_b.astype(jnp.float32)
    return jax.nn.silu(y32).astype(a.dtype)

def swa_group(q, k, v, sinks):
    B, S, _ = q.shape
    BLK, HKV, DH = SWA_BLOCK, SWA_KV_HEADS, SWA_HEAD_DIM
    G = SWA_Q_HEADS // HKV
    nb = S // BLK
    qb = q.reshape(B, nb, BLK, HKV, G, DH)
    kb = k.reshape(B, nb, BLK, HKV, DH)
    vb = v.reshape(B, nb, BLK, HKV, DH)

    def with_prev(t):
        prev = jnp.pad(t, ((0, 0), (1, 0), (0, 0), (0, 0), (0, 0)))[:, :-1]
        return jnp.concatenate([prev, t], axis=2)

    kk, vv = with_prev(kb), with_prev(vb)
    s = jnp.einsum('bnqhgd,bnkhd->bnhgqk', qb, kk).astype(jnp.float32) * (DH ** -0.5)
    qi = jnp.arange(BLK)[:, None]
    kj = jnp.arange(2 * BLK)[None, :]
    dist = qi - kj + BLK
    blk = jnp.arange(nb)[:, None, None]
    valid = (dist >= 0) & (dist < SWA_WINDOW) & ((blk > 0) | (kj >= BLK))
    slopes = jnp.exp2(-8.0 * (jnp.arange(SWA_Q_HEADS, dtype=jnp.float32) + 1.0) / SWA_Q_HEADS)
    slopes = slopes.reshape(HKV, G)
    s = s - slopes[:, :, None, None] * dist.astype(jnp.float32)
    s = jnp.where(valid[None, :, None, None], s, -jnp.inf)
    sink = jnp.broadcast_to(sinks.astype(jnp.float32).reshape(HKV, G)[None, None, :, :, None, None],
                            s.shape[:-1] + (1,))
    p = jax.nn.softmax(jnp.concatenate([s, sink], axis=-1), axis=-1)[..., :-1]
    o = jnp.einsum('bnhgqk,bnkhd->bnqhgd', p.astype(v.dtype), vv)
    return o.reshape(B, S, SWA_Q_HEADS * DH)

def hybrid_mixer(h, w_in, gla_w_gate2, gla_b_gate, gla_norm_g, conv_w, conv_b,
                 conv_ln_g, conv_ln_b, swa_sinks, w_out):
    B, S, _ = h.shape
    p = h @ w_in
    offsets = np.cumsum(_in_proj_widths())[:-1].tolist()
    gq, gk, gv, gr, glr, ca, cg, sq, sk, sv = jnp.split(p, offsets, axis=-1)
    glog = jax.nn.log_sigmoid((glr @ gla_w_gate2 + gla_b_gate).astype(jnp.float32)) / GLA_TAU
    o_gla = gla_group(gq.reshape(B, S, GLA_HEADS, GLA_DK), gk.reshape(B, S, GLA_HEADS, GLA_DK),
                      gv.reshape(B, S, GLA_HEADS, GLA_DV), glog.reshape(B, S, GLA_HEADS, GLA_DK),
                      gr, gla_norm_g)
    o_conv = conv_group(ca, cg, conv_w, conv_b, conv_ln_g, conv_ln_b)
    o_swa = swa_group(sq, sk, sv, swa_sinks)
    return jnp.concatenate([o_gla, o_conv, o_swa], axis=-1) @ w_out

def second_inputs(seed: int = 0) -> dict:
    key = jax.random.key(seed)
    ks = jax.random.split(key, 16)
    f32 = jnp.float32
    d_in = sum(_in_proj_widths())
    nrm = lambda k, shape, scale: jax.random.normal(k, shape, f32) * scale
    return {
        "x": jax.random.normal(ks[0], (BATCH, SEQ, D_MODEL), f32),
        "norm_g": 1.0 + nrm(ks[1], (DEPTH, 6, D_MODEL), 0.05),
        "ffn_w_gate": nrm(ks[2], (DEPTH, 2, D_MODEL, D_FF_2), D_MODEL ** -0.5),
        "ffn_w_up": nrm(ks[3], (DEPTH, 2, D_MODEL, D_FF_2), D_MODEL ** -0.5),
        "ffn_w_down": nrm(ks[4], (DEPTH, 2, D_FF_2, D_MODEL), D_FF_2 ** -0.5),
        "w_in": nrm(ks[5], (DEPTH, D_MODEL, d_in), D_MODEL ** -0.5),
        "gla_w_gate2": nrm(ks[6], (DEPTH, GLA_GATE_RANK, GLA_HEADS * GLA_DK), GLA_GATE_RANK ** -0.5),
        "gla_b_gate": nrm(ks[7], (DEPTH, GLA_HEADS * GLA_DK), 0.1),
        "gla_norm_g": 1.0 + nrm(ks[8], (DEPTH, GLA_HEADS, GLA_DV), 0.05),
        "conv_w": nrm(ks[9], (DEPTH, CONV_WIDTH, CONV_CH), CONV_WIDTH ** -0.5),
        "conv_b": nrm(ks[10], (DEPTH, CONV_CH), 0.02),
        "conv_ln_g": 1.0 + nrm(ks[11], (DEPTH, CONV_CH), 0.05),
        "conv_ln_b": nrm(ks[12], (DEPTH, CONV_CH), 0.02),
        "swa_sinks": nrm(ks[13], (DEPTH, SWA_Q_HEADS), 0.5),
        "w_out": nrm(ks[14], (DEPTH, D_MIX, D_MODEL), D_MIX ** -0.5),
    }

def second_block(x, norm_g, ffn_w_gate, ffn_w_up, ffn_w_down, w_in, gla_w_gate2, gla_b_gate,
              gla_norm_g, conv_w, conv_b, conv_ln_g, conv_ln_b, swa_sinks, w_out):
    for l in range(DEPTH):
        g = norm_g[l]
        h = swiglu_ffn(rmsnorm(x, g[0]), ffn_w_gate[l, 0], ffn_w_up[l, 0], ffn_w_down[l, 0])
        x = x + 0.5 * rmsnorm(h, g[1])
        h = hybrid_mixer(rmsnorm(x, g[2]), w_in[l], gla_w_gate2[l], gla_b_gate[l], gla_norm_g[l],
                         conv_w[l], conv_b[l], conv_ln_g[l], conv_ln_b[l], swa_sinks[l], w_out[l])
        x = x + rmsnorm(h, g[3])
        h = swiglu_ffn(rmsnorm(x, g[4]), ffn_w_gate[l, 1], ffn_w_up[l, 1], ffn_w_down[l, 1])
        x = x + 0.5 * rmsnorm(h, g[5])
    return x


def setup_inputs(seed=0):
    out = dict(first_inputs(seed))
    for name, value in second_inputs(seed + 1).items():
        if name != "x":
            out[name + "_2"] = value
    return out


def reference(
    x, c, ctx, c_ctx, w_mod, b_mod, ln1_g, ln1_b, ln2_g, ln2_b, w_ffn_in, w_ffn_out, mla_w_in,
    mla_q_norm, mla_kv_norm, mla_w_q_up, mla_w_kv_up, mla_w_out, gdn_w_in, gdn_conv, gdn_a_log,
    gdn_dt_bias, gdn_norm, gdn_w_out, norm_g_2, ffn_w_gate_2, ffn_w_up_2, ffn_w_down_2, w_in_2,
    gla_w_gate2_2, gla_b_gate_2, gla_norm_g_2, conv_w_2, conv_b_2, conv_ln_g_2, conv_ln_b_2,
    swa_sinks_2, w_out_2,
):
    x = first_block(
        x, c, ctx, c_ctx, w_mod, b_mod, ln1_g, ln1_b, ln2_g, ln2_b, w_ffn_in, w_ffn_out,
        mla_w_in, mla_q_norm, mla_kv_norm, mla_w_q_up, mla_w_kv_up, mla_w_out, gdn_w_in,
        gdn_conv, gdn_a_log, gdn_dt_bias, gdn_norm, gdn_w_out,
    )
    return second_block(
        x, norm_g_2, ffn_w_gate_2, ffn_w_up_2, ffn_w_down_2, w_in_2, gla_w_gate2_2,
        gla_b_gate_2, gla_norm_g_2, conv_w_2, conv_b_2, conv_ln_g_2, conv_ln_b_2, swa_sinks_2,
        w_out_2,
    )


_drawn_inputs = setup_inputs


def setup_inputs(seed=0):
    import zlib

    import numpy as np

    out = dict(_drawn_inputs(seed))
    spreads = {}
    factors = {'b_mod': 3.17,
     'mla_q_norm': 8.0,
     'mla_kv_norm': 8.0,
     'gdn_norm': 8.0,
     'conv_ln_b_2': 3.702}
    for name, (base, spread) in spreads.items():
        noise = np.random.default_rng([zlib.crc32(name.encode()), seed]).standard_normal(out[name].shape)
        drawn = base * np.exp(spread * noise) if base else spread * noise
        out[name] = jnp.asarray(drawn.astype(out[name].dtype))
    for name, factor in factors.items():
        out[name] = (out[name] * factor).astype(out[name].dtype)
    return out
```

```python
from contextlib import ExitStack

import numpy as np

import concourse.bass as bass
from concourse import mybir

F32 = mybir.dt.float32
ACT = mybir.ActivationFunctionType
ALU = mybir.AluOpType
AX_X = mybir.AxisListType.X

P = 128
D = 1024
DC = D // P
SEQ = 256
CTX = 256
TOK = SEQ + CTX
DEPTH = 2
GRID_W = 64
ALPHA = (2.0 * DEPTH) ** 0.25
LN_EPS = 1e-5
RMS_EPS = 1e-6
N_MOD = 6
MB = N_MOD * DC

HEADS = 8
Q_RANK, KV_RANK = 512, 256
QC, KC = Q_RANK // P, KV_RANK // P
NOPE, ROPE, VDIM = 128, 64, 128
MLA_SCALE = (NOPE + ROPE) ** -0.5
ROPE_THETA = 10000.0

GK_HEADS, GV_HEADS = 8, 16
GROUPS = 4
GH = GV_HEADS // GROUPS
GKH = GK_HEADS // GROUPS
TAPS = 5
TILES = TOK // P
LT_TILES = SEQ // P
LEVELS = 7
GDN_VW = GV_HEADS * P

D_FF = 2816
FC = D_FF // P
PANEL = 4096
SLOTS = 3

GLA_HEADS, GLA_DK, GLA_DV, GLA_RANK, GLA_TAU = 4, 32, 64, 16, 16.0
CONV_W = 31
SWA_HEADS, SWA_KV, SWA_DH = 8, 2, 64
NEG = -1e30

SCAN = [[2, 3, 0, 1], [3, 2, 1, 0]]

PARAMS = [("b_mod", DEPTH * MB), ("ln1_g", DEPTH * DC), ("ln1_b", DEPTH * DC), ("ln2_g", DEPTH * DC),
          ("ln2_b", DEPTH * DC), ("q_norm", QC), ("kv_norm", KC), ("conv5", GROUPS * 8 * TAPS),
          ("gdn_norm", 1), ("a_log", 32), ("dt_bias", 32), ("w_ba", DC * 64), ("cvec", DC * 2), ("eps", 4)]
LPARAMS = [("norm_g", 6 * DC), ("glr", DC * GLA_RANK), ("gate2", P), ("b_gate", 1), ("gla_norm", 2),
           ("conv31", 2 * CONV_W), ("conv_b", 2), ("conv_ln_g", 2), ("conv_ln_b", 2), ("sinks", SWA_HEADS)]
CONSTS = [("ones", P), ("ones64", P), ("tri", 2 * P), ("ident", P), ("level", 2 * LEVELS * P),
          ("rope_cos", SEQ), ("rope_sin", SEQ), ("alibi", SWA_HEADS * 2 * P)]


def columns(table):
    at, out = 0, {}
    for name, n in table:
        out[name] = (at, n)
        at += n
    return out, at


PCOL, NPAR = columns(PARAMS)
LCOL, NLPAR = columns(LPARAMS)
CCOL, NCONST = columns(CONSTS)

SECTIONS = [("mod0", 12), ("mla", 7), ("ffn0", 11), ("down0", 8), ("mod1", 12), ("gdn", 12), ("gdn_out", 4),
            ("ffn1", 11), ("down1", 8)]
LAYER = [("ffnA", 11), ("downA", 8), ("mix_in", 4), ("mix_out", 2), ("ffnB", 11), ("downB", 8)]


class Plan:

    def __init__(self):
        self.base, self.first = {}, {}
        used = [0] * SLOTS
        at = {True: 0, False: 0}
        for name, n in SECTIONS:
            self._add(name, n, used, at)
        self.start = list(used)
        self.layer_first = dict(at)
        for name, n in LAYER:
            self._add(name, n, used, at)
        self.per_layer = [b - a for a, b in zip(self.start, used)]
        self.layer_panels = {k: at[k] - self.layer_first[k] for k in at}
        self.total = {k: self.layer_first[k] + DEPTH * self.layer_panels[k] for k in at}

    def _add(self, name, n, used, at):
        down = name.startswith("down")
        self.base[name], self.first[name] = list(used), at[down]
        for p in range(n):
            used[p % SLOTS] += 1
        at[down] += n

    def uses(self, name, slot, turn, layer=0):
        more = self.per_layer[slot] * layer if name in dict(LAYER) else 0
        return self.base[name][slot] + turn + more

    def panel(self, name, p, layer=0):
        down = name.startswith("down")
        more = self.layer_panels[down] * layer if name in dict(LAYER) else 0
        return self.first[name] + p + more


PLAN = Plan()

U_GDN, U_FFN1, U_BLOCK2 = 2 * DC, 3 * DC, 4 * DC


def U_MIX(l):
    return U_BLOCK2 + 3 * DC * l + DC



def build(nc, h_in, params, lparams, consts, panels, downs, out, stop=None):
    ctx = ExitStack()
    with ctx:
        def sb(name, shape):
            return ctx.enter_context(nc.sbuf_tensor(name, shape, F32))

        def sem(name):
            return ctx.enter_context(nc.semaphore(name))

        bank = ctx.enter_context(nc.psum_tensor("bank", [P, 8, 512], F32))

        ring = sb("ring", [P, SLOTS, PANEL])
        h = sb("h", [P, DC, TOK])
        u = sb("u", [P, DC, TOK])
        par = sb("par", [P, NPAR])
        lpar = sb("lpar", [P, NLPAR])
        con = sb("con", [P, NCONST])
        cond = sb("cond", [P, DC, 2])
        mod = sb("mod", [P, MB, 2])
        std = sb("std", [P, 2, TOK])
        ARENA = 25288
        arena = sb("arena", [P, ARENA])

        class Carve:

            def __init__(self, at=0):
                self.at = at

            def __call__(self, *shape):
                n = int(np.prod(shape))
                v = arena[:, self.at:self.at + n]
                self.at += n
                assert self.at <= ARENA, self.at
                names = "abcd"[:len(shape)]
                if len(shape) == 1:
                    return v
                return v.rearrange(f"p ({' '.join(names)}) -> p {' '.join(names)}", **dict(zip(names, shape)))

        def param(name, *shape):
            a, n = PCOL[name]
            return cut(par, a, n, shape)

        def lparam(name, *shape):
            a, n = LCOL[name]
            return cut(lpar, a, n, shape)

        def const(name, *shape):
            a, n = CCOL[name]
            return cut(con, a, n, shape)

        def cut(t, a, n, shape):
            v = t[:, a:a + n]
            if len(shape) < 2:
                return v
            names = "abcd"[:len(shape)]
            return v.rearrange(f"p ({' '.join(names)}) -> p {' '.join(names)}", **dict(zip(names, shape)))

        def wide(ap, n, at):
            shape = list(ap.shape)
            return ap.unsqueeze(at).to_broadcast(shape[:at] + [n] + shape[at:])

        ones, ident, ones64 = const("ones"), const("ident"), const("ones64")
        tri = const("tri", 2, P)
        level = const("level", 2, LEVELS, P)
        rope_cos, rope_sin = const("rope_cos"), const("rope_sin")
        alibi = const("alibi", SWA_HEADS, 2 * P)
        b_mod = param("b_mod", DEPTH, MB)
        ln_g = [param("ln1_g", DEPTH, DC), param("ln2_g", DEPTH, DC)]
        ln_b = [param("ln1_b", DEPTH, DC), param("ln2_b", DEPTH, DC)]
        q_norm, kv_norm = param("q_norm"), param("kv_norm")
        conv5 = param("conv5", GROUPS, 8 * TAPS)
        gdn_norm = param("gdn_norm")
        a_log, dt_bias = param("a_log"), param("dt_bias")
        w_ba = param("w_ba", DC, 64)
        cvec = param("cvec", DC, 2)
        eps = param("eps")
        norm_g = lparam("norm_g", 6, DC)
        w_glr = lparam("glr", DC, GLA_RANK)
        gate2 = lparam("gate2")
        b_gate, gla_norm = lparam("b_gate"), lparam("gla_norm")
        conv31 = lparam("conv31", 2, CONV_W)
        conv_b, conv_ln_g, conv_ln_b = lparam("conv_b"), lparam("conv_ln_g"), lparam("conv_ln_b")
        sinks = lparam("sinks")
        EPS_RMS, EPS_LN, EPS_RMS4, ONE = (eps[:, i:i + 1] for i in range(4))

        c = Carve()
        lat = c(QC + KC, TOK)
        krope = c(TOK)
        rope_t = c(2, SEQ)
        q_n, k_n = c(HEADS, TOK), c(HEADS, TOK)
        q_r = c(HEADS // 2, TOK)
        v_tm = c(TILES, HEADS * VDIM)
        probs = c(2, 3, 512)
        probs_t = c(TILES, SEQ)
        probs_tc = c(CTX // P, CTX)
        negmax, rowsum = c(2, 4), c(2, 4)
        lat_sq = q_n
        c = Carve()
        hidden = c(FC, TOK)
        silu_g = c(3, TOK)
        resid = c(DC, TOK)
        sq = hidden
        c = Carve()
        k_fm, q_fm, v_fm = c(GKH, TOK), c(GKH, SEQ), c(GH, TOK)
        k_tm, gv_tm = c(TILES, GKH, P), c(TILES, GH, P)
        state = c(2, GH, P)
        kq = c(2, LT_TILES, GKH, P)
        gdn_sq = Carve(c.at)(4, TOK)
        soft = Carve(c.at)(2, 2, TILES, GV_HEADS)
        X, XT = c(2, GH, P), c(2, GH, P)
        gdn_std = Carve(c.at)(4, TOK)
        KE, KD = c(2, GH, P), c(2, GH, P)
        Y, E, LT, QD, AT = (c(2, GH, P) for _ in range(5))
        cin = Carve(c.at)(2, 2, SEQ + TAPS - 1)
        ML = c(2, 2, GH, P)
        y_all = c(GV_HEADS, SEQ)
        gates = c(6, 2, TILES, GV_HEADS)
        gst = c(6, 2, TILES, GH)
        cst = c(8 * TAPS)
        kk = v_fm.rearrange("p a b -> p (a b)")[:, 0:TILES * GKH * P].rearrange("p (t j q) -> p t j q", t=TILES, j=GKH)
        o_acc, z_s = h[:, 0:GH, SEQ:TOK], h[:, GH:2 * GH, SEQ:TOK]
        BETA, G_, GCUM, EG, ED, ETOT = (gates[:, i] for i in range(6))
        S_BETA, S_G, S_GCUM, S_EG, S_ED, S_ETOT = (gst[:, i] for i in range(6))
        c = Carve(FC * TOK + 3 * TOK)
        yb, sq2 = c(DC, SEQ), c(DC, SEQ)
        end_norms = c.at
        c = Carve()
        dec, qe, ke = c(8, SEQ), c(8, SEQ), c(8, SEQ)
        swp, swt = c(SWA_HEADS, 3, P), c(SWA_HEADS, 3, P)
        att = c(GLA_HEADS, 3, P)
        att_l = c(2, 8, P)
        gqk, gr_s, sig_g = c(2, SEQ), c(2, SEQ), c(2, SEQ)
        conv_in = c(2, SEQ + CONV_W - 1)
        conv_y, cv_sq = c(2, SEQ), c(2, SEQ)
        s_q, s_k = c(4, SEQ), c(SEQ)
        g_v, s_v = c(2, GLA_HEADS * GLA_DV), c(2, SWA_KV * SWA_DH)
        glr_s, gl_y, gl_e, gl_c = c(SEQ), c(SEQ), c(SEQ), c(SEQ)
        og, og_sq = c(2, SEQ), c(2, SEQ)
        mix = c(DC, SEQ)
        swm, sws, swe = c(SWA_HEADS, 2), c(SWA_HEADS, 2), c(SWA_HEADS, 2)
        gmask = con[:, CCOL["ident"][0]:CCOL["ident"][0] + 8 * P].rearrange("p (l q) -> p l q", l=8)

        in_loaded, lpar_loaded, out_stored = sem("in_loaded"), sem("lpar_loaded"), sem("out_stored")
        slot_loaded = [sem(f"slot_loaded{s}") for s in range(SLOTS)]
        panel_done = [sem(f"panel_done{s}") for s in range(SLOTS)]
        names = """cond_ready mod_ready u_ready lat_done lat_copied lat_squared lat_ssq lat_std latn_ready krope_ready
            qn_done qn_ready qr_ready kn_done kn_ready v_done v_ready s_done max_ready exp_done p_ready pt_done
            pt_lat pt_ctx pv_done o_ready yg_ready r_ready mean_done cent_ready cent_sq var_done var_std norm_ready
            h_ready pair_done silu_ready pair_free
            yproj pad_ready zproj_done ba_done ax_ready sp_exp sp_ln beta_ready alog_ready g_ready gcum_done gcum_ready gexp_ready gst_ready
            proj_done cin_ready conv_done act_ready kq_sq kq_ssq kq_std kq_ready z_ready vt_done vt_ready kt_done
            kt_ready kk_done kk_ready kqm_ready oacc_sq oacc_ssq oacc_std y_ready
            yb_ready sq_ready ssq_done std_ready x_ready layer_done
            mixp_done gqk_ready gr_ready conv_u sig_ready swq_ready gv_ready glr_done glr_ready gate_done gy_ready
            ge_ready gln_ready gabs_ready gdec_ready gqe_ready gs_done att_ready go_done go_ready
            go_sq go_ssq go_std gla_ready cvy_ready cv_mean cv_cent cv_sq_ready cv_var cv_std cv_norm cv_ready
            sw_done swb_ready swm_ready swe_ready swp_ready swt_done swt_ready swo_done swo_ready""".split()
        s = {n: sem(n) for n in names}
        per_dir = """gtri_ready gbc_done diff_ready decay_ready eg_ready lt_ready ml_ready xt0_ready x0_done x0_ready
            y_done yc_ready xy_done xs_ready xt_done xt_ready kek_ready w_done w_ready vn_done vn_ready qd_ready
            at_ready od_done od_ready su_done su_ready""".split()
        sd = {n: sem(n) for n in per_dir}

        block = ctx.enter_context(nc.Block())

        def load_done(e, name, slot, turn, layer=0):
            e.wait_ge(slot_loaded[slot], 16 * PLAN.uses(name, slot, turn, layer) + 16)

        def panel_over(e, name, slot, turn, layer=0):
            e.wait_ge(panel_done[slot], PLAN.uses(name, slot, turn, layer) + 2)

        def mla_out_over(e, m):
            if m % 4 == 3:
                panel_over(e, "mla", 2 if m < 4 else 0, 1 if m < 4 else 2)
            else:
                e.wait_ge(s["yproj"], m + 1 - m // 4)

        def gdn_out_over(e, m):
            if m % 2:
                panel_over(e, "gdn_out", m // 2 % SLOTS, m // 2 // SLOTS)
            else:
                e.wait_ge(s["yproj"], 6 + m // 2 + 1)

        def mix_out_over(e, m, l):
            if m % 4 == 3:
                panel_over(e, "mix_out", m // 4, 0, l)
            else:
                e.wait_ge(s["yproj"], 10 + 6 * l + m + 1 - m // 4)

        @block.sync
        def _(sp):
            sp.dma_start(par[:], params).then_inc(in_loaded, 16)
            sp.dma_start(h[:], h_in).then_inc(in_loaded, 16)
            sp.dma_start(con[:], consts).then_inc(in_loaded, 16)

            def load(name, slot, turn, layer=0):
                sp.wait_ge(panel_done[slot], PLAN.uses(name, slot, turn, layer) + 1)
                at = PLAN.panel(name, turn * SLOTS + slot, layer)
                if name.startswith("down"):
                    sp.dma_start(ring[:, slot, 0:FC * P], downs[at]).then_inc(slot_loaded[slot], 16)
                else:
                    sp.dma_start(ring[:, slot, :], panels[at]).then_inc(slot_loaded[slot], 16)

            def section(name, layer=0):
                n = dict(SECTIONS + LAYER)[name]
                if n >= 2 * SLOTS:
                    with sp.Fori(0, n // SLOTS) as i:
                        for slot in range(SLOTS):
                            load(name, slot, i, layer)
                else:
                    for p in range(n // SLOTS * SLOTS):
                        load(name, p % SLOTS, p // SLOTS, layer)
                for p in range(n // SLOTS * SLOTS, n):
                    load(name, p % SLOTS, p // SLOTS, layer)

            for name, _ in SECTIONS:
                section(name)
            with sp.Fori(0, DEPTH) as l:
                sp.wait_ge(s["layer_done"], l + 1)
                sp.dma_start(lpar[:], lparams[l]).then_inc(lpar_loaded, 16)
                for name, _ in LAYER:
                    section(name, l)
            sp.wait_ge(s["layer_done"], DEPTH + 1)
            sp.dma_start(out, h[:, :, 0:SEQ]).then_inc(out_stored, 16)
            sp.wait_ge(out_stored, 16)

        @block.tensor
        def _(pe):
            def mm(o, w, x, first, last):
                return pe.matmul(o, w, x, start=first, stop=last)

            def slot_view(slot, k, n):
                return ring[:, slot, 0:k * n].rearrange("p (k n) -> p k n", k=k)

            for q in panel_done:
                pe.sem_inc(q, 1)
            pe.wait_ge(in_loaded, 48)

            def modulation(l):
                name = f"mod{l}"
                if l == 0:
                    pe.wait_ge(s["cond_ready"], 1)
                with pe.Fori(0, 12 // SLOTS) as i:
                    for slot in range(SLOTS):
                        load_done(pe, name, slot, i)
                        w = slot_view(slot, DC, 512)
                        for j in range(4):
                            o = bank[:, 7, bass.ds((i * (4 * SLOTS) + (4 * slot + j)) * 2, 2)]
                            for k in range(DC):
                                last = mm(o, w[:, k, j * P:(j + 1) * P], cond[:, k, :], k == 0, k == DC - 1)
                        last.then_inc(panel_done[slot], 1)

            def mla():
                for p in range(2):
                    load_done(pe, "mla", p, 0)
                    w = slot_view(p, DC, 512)
                    for j in range(4):
                        for k in range(DC):
                            if p == 0 and j == 0:
                                pe.wait_ge(s["u_ready"], k + 1)
                            last = mm(bank[:, 4 * p + j, :], w[:, k, j * P:(j + 1) * P], u[:, k, :], k == 0, k == DC - 1)
                        last.then_inc(s["lat_done"] if j < 3 else panel_done[p], 1)
                for b, (a, n) in enumerate([(0, QC), (QC, KC)]):
                    for k in range(n):
                        pe.wait_ge(s["lat_squared"], a + k + 1)
                        last = mm(bank[:, b, :], ones, lat_sq[:, a + k, :], k == 0, k == n - 1)
                    last.then_inc(s["lat_ssq"], 1)
                load_done(pe, "mla", 2, 0)
                w = slot_view(2, QC, HEADS * NOPE)
                pe.wait_ge(s["latn_ready"], QC)
                pe.wait_ge(s["lat_std"], 2)
                pe.wait_ge(s["krope_ready"], 1)
                for j in range(HEADS):
                    for k in range(QC):
                        last = mm(bank[:, j, :], w[:, k, j * P:(j + 1) * P], lat[:, k, :], k == 0, k == QC - 1)
                    last.then_inc(s["qn_done"] if j < HEADS - 1 else panel_done[2], 1)
                load_done(pe, "mla", 0, 1)
                w = slot_view(0, QC, 2 * HEADS * ROPE)
                for j in range(HEADS):
                    pe.wait_ge(s["qn_ready"], j + 1)
                    for k in range(QC):
                        last = mm(bank[:, j, :], w[:, k, j * P:(j + 1) * P], lat[:, k, :], k == 0, k == QC - 1)
                last.then_inc(panel_done[0], 1)
                load_done(pe, "mla", 1, 1)
                w = slot_view(1, KC, 2 * HEADS * P)
                pe.wait_ge(s["latn_ready"], QC + KC)
                pe.wait_ge(s["qr_ready"], HEADS // 2)
                for j in range(HEADS):
                    for k in range(KC):
                        last = mm(bank[:, j, :], w[:, k, j * P:(j + 1) * P], lat[:, QC + k, :], k == 0, k == KC - 1)
                    last.then_inc(s["kn_done"], 1)
                for t in range(TILES):
                    for half in range(2):
                        n = 2 * t + half
                        pe.wait_ge(s["kn_ready"], n + 1)
                        for k in range(KC):
                            a = HEADS * P + 512 * half
                            last = mm(bank[:, n, :], lat[:, QC + k, t * P:(t + 1) * P], w[:, k, a:a + 512],
                                      k == 0, k == KC - 1)
                        last.then_inc(s["v_done"] if n < 7 else panel_done[1], 1)
                pe.wait_ge(s["v_ready"], 8)

                def scores(hd):
                    r = slice(64 * (hd % 2), 64 * (hd % 2) + 64)
                    if hd:
                        pe.wait_ge(s["exp_done"], hd)
                    for t in range(LT_TILES):
                        cols = slice(t * P, (t + 1) * P)
                        mm(bank[:, t, :], q_n[:, hd, cols], k_n[:, hd, :], True, False)
                        last = mm(bank[:, t, :], q_r[r, hd // 2, cols], krope[r, :], False, True)
                    last.then_inc(s["s_done"], 1)
                    for t in range(CTX // P):
                        cols = slice(SEQ + t * P, SEQ + (t + 1) * P)
                        o = bank[:, 2, t * CTX:(t + 1) * CTX]
                        mm(o, q_n[:, hd, cols], k_n[:, hd, SEQ:TOK], True, False)
                        last = mm(o, q_r[r, hd // 2, cols], krope[r, SEQ:TOK], False, True)
                    last.then_inc(s["s_done"], 1)

                def turn(hd):
                    pe.wait_ge(s["p_ready"], hd + 1)
                    for b in range(3):
                        for j in range(4):
                            last = pe.transpose(bank[:, 3 + b, j * P:(j + 1) * P], probs[:, hd % 2, b, j * P:(j + 1) * P], ident)
                        last.then_inc(s["pt_done"], 1)

                def weigh(hd):
                    o = bank[:, 6 + hd % 2, :]
                    pe.wait_ge(s["pt_lat"], hd + 1)
                    if hd >= 2:
                        pe.wait_ge(s["o_ready"], hd - 1)
                    for t in range(TILES):
                        mm(o[:, 0:SEQ], v_tm[:, t, hd * P:(hd + 1) * P], probs_t[:, t, :], t == 0, t == TILES - 1)
                    pe.wait_ge(s["pt_ctx"], hd + 1)
                    for t in range(2):
                        last = mm(o[:, SEQ:TOK], v_tm[:, LT_TILES + t, hd * P:(hd + 1) * P], probs_tc[:, t, :], t == 0, t == 1)
                    last.then_inc(s["pv_done"], 1)

                scores(0)
                for hd in range(HEADS):
                    if hd + 1 < HEADS:
                        scores(hd + 1)
                    turn(hd)
                    weigh(hd)
                pe.wait_ge(s["o_ready"], HEADS)
                for p, (slot, trn) in enumerate([(2, 1), (0, 2)]):
                    load_done(pe, "mla", slot, trn)
                    w = slot_view(slot, DC, 512)
                    for j in range(4):
                        for k in range(DC):
                            last = mm(bank[:, 4 * p + j, :], w[:, k, j * P:(j + 1) * P], u[:, k, :], k == 0, k == DC - 1)
                        last.then_inc(s["yproj"] if j < 3 else panel_done[slot], 1)

            def layer_norm(n, T):
                for k in range(DC):
                    pe.wait_ge(s["r_ready"], DC * n + k + 1)
                    last = mm(bank[:, 0, 0:T], ones, resid[:, k, 0:T], k == 0, k == DC - 1)
                last.then_inc(s["mean_done"], 1)
                for k in range(DC):
                    pe.wait_ge(s["cent_sq"], DC * n + k + 1)
                    last = mm(bank[:, 1, 0:T], ones, sq[:, k, 0:T], k == 0, k == DC - 1)
                last.then_inc(s["var_done"], 1)

            def ffn(f, T, name, down, u_before, layer=0):
                def panel(slot, turn, first=False):
                    load_done(pe, name, slot, turn, layer)
                    w = slot_view(slot, DC, 512)
                    for half in range(2):
                        pe.wait_ge(s["pair_free"], FC * f + 2 * (SLOTS * turn + slot) + half + 1)
                        b = 2 * ((2 * slot + half) % 3)
                        for g in range(2):
                            j = 2 * half + g
                            for k in range(DC):
                                if first and j == 0:
                                    pe.wait_ge(s["u_ready"], u_before + k + 1)
                                last = mm(bank[:, b + g, 0:T], w[:, k, j * P:(j + 1) * P], u[:, k, 0:T], k == 0, k == DC - 1)
                        last.then_inc(panel_done[slot] if half else s["pair_done"], 1)

                panel(0, 0, True)
                panel(1, 0)
                with pe.Fori(0, 3) as i:
                    panel(2, i)
                    panel(0, i + 1)
                    panel(1, i + 1)
                pe.wait_ge(s["pair_free"], FC * (f + 1) + 3)
                for m in range(DC):
                    load_done(pe, down, m % SLOTS, m // SLOTS, layer)
                    w = slot_view(m % SLOTS, FC, P)
                    for k in range(FC):
                        last = mm(bank[:, m, 0:T], w[:, k, :], hidden[:, k, 0:T], k == 0, k == FC - 1)
                    last.then_inc(panel_done[m % SLOTS], 1)

            def gdn():
                pe.wait_ge(s["u_ready"], U_GDN + DC)
                for t in range(TILES):
                    for k in range(DC):
                        last = mm(bank[:, 2, t * 64:(t + 1) * 64], u[:, k, t * P:(t + 1) * P], w_ba[:, k, :], k == 0, k == DC - 1)
                last.then_inc(s["ba_done"], 1)
                pe.wait_ge(s["g_ready"], 1)
                for d in range(2):
                    mm(bank[:, 3, d * 64:(d + 1) * 64], tri[:, d, :], G_[:, d], True, True)
                    last = mm(bank[:, 3, 128 + d * 64:192 + d * 64], ones, G_[:, d], True, True)
                last.then_inc(s["gcum_done"], 1)
                with pe.Fori(0, GROUPS) as g:
                    gdn_group(g)
                pe.wait_ge(s["y_ready"], GROUPS + 1)
                for p in range(4):
                    load_done(pe, "gdn_out", p % SLOTS, p // SLOTS)
                    w = slot_view(p % SLOTS, GV_HEADS, 2 * P)
                    for j in range(2):
                        for k in range(GV_HEADS):
                            last = mm(bank[:, 2 * p + j, 0:SEQ], w[:, k, j * P:(j + 1) * P], y_all[:, k, :], k == 0, k == GV_HEADS - 1)
                        last.then_inc(panel_done[p % SLOTS] if j else s["yproj"], 1)

            def gdn_group(g):
                pe.wait_ge(s["y_ready"], g + 1)
                pe.wait_ge(s["gcum_ready"], 1)
                def project(slot, j, o, T):
                    w = slot_view(slot, DC, 512)
                    for k in range(DC):
                        last = mm(o, w[:, k, j * P:(j + 1) * P], u[:, k, 0:T], k == 0, k == DC - 1)
                    return last
                load_done(pe, "gdn", 0, g)
                project(0, 0, bank[:, 0, :], TOK).then_inc(s["proj_done"], 1)
                project(0, 1, bank[:, 1, :], TOK).then_inc(s["proj_done"], 1)
                project(0, 2, bank[:, 2, 0:SEQ], SEQ)
                project(0, 3, bank[:, 2, SEQ:TOK], SEQ).then_inc(panel_done[0], 1)
                load_done(pe, "gdn", 1, g)
                for j in range(GH):
                    project(1, j, bank[:, 3 + j, :], TOK).then_inc(s["proj_done"] if j < 3 else panel_done[1], 1)
                load_done(pe, "gdn", 2, g)
                project(2, 0, bank[:, 7, 0:SEQ], SEQ)
                project(2, 1, bank[:, 7, SEQ:TOK], SEQ).then_inc(s["zproj_done"], 1)
                pe.wait_ge(s["cin_ready"], 8 * g + 1)
                project(2, 2, bank[:, 0, 0:SEQ], SEQ)
                project(2, 3, bank[:, 0, SEQ:TOK], SEQ).then_inc(panel_done[2], 1)
                pe.wait_ge(s["cin_ready"], 8 * g + 8)
                for j in range(GH):
                    pe.wait_ge(s["act_ready"], 8 * g + 4 + j + 1)
                    for t in range(TILES):
                        last = pe.transpose(bank[:, 3 + j, t * P:(t + 1) * P], v_fm[:, j, t * P:(t + 1) * P], ident)
                    last.then_inc(s["vt_done"], 1)
                pe.wait_ge(s["kq_sq"], 3 * g + 1)
                mm(bank[:, 1, :], ones, gdn_sq[:, 0, :], True, True).then_inc(s["kq_ssq"], 1)
                pe.wait_ge(s["kq_sq"], 3 * g + 2)
                mm(bank[:, 2, :], ones, gdn_sq[:, 1, :], True, True).then_inc(s["kq_ssq"], 1)
                pe.wait_ge(s["kq_sq"], 3 * g + 3)
                pe.wait_ge(s["z_ready"], 2 * g + 1)
                mm(bank[:, 7, :], ones, gdn_sq[:, 2, :], True, True).then_inc(s["kq_ssq"], 1)
                pe.wait_ge(s["vt_ready"], 4 * g + 2)
                for j in range(GKH):
                    pe.wait_ge(s["kq_ready"], 3 * g + j + 1)
                    for t in range(TILES):
                        last = pe.transpose(bank[:, 3 + j, t * P:(t + 1) * P], k_fm[:, j, t * P:(t + 1) * P], ident)
                    last.then_inc(s["kt_done"], 1)
                pe.wait_ge(s["vt_ready"], 4 * g + 4)
                for t in range(TILES):
                    for j in range(GKH):
                        cols = slice(t * P, (t + 1) * P)
                        last = mm(bank[:, 5 + t // 2, (t % 2 * GKH + j) * P:(t % 2 * GKH + j + 1) * P], k_fm[:, j, cols], k_fm[:, j, cols], True, True)
                    if t % 2:
                        last.then_inc(s["kk_done"], 1)
                pe.wait_ge(s["kq_ready"], 3 * g + 3)
                for t in range(LT_TILES):
                    for j in range(GKH):
                        cols = slice(t * P, (t + 1) * P)
                        last = mm(bank[:, 7, (t * GKH + j) * P:(t * GKH + j + 1) * P], k_fm[:, j, cols], q_fm[:, j, cols], True, True)
                last.then_inc(s["kk_done"], 1)
                pe.wait_ge(s["z_ready"], 2 * g + 2)
                pe.wait_ge(s["kt_ready"], 2 * g + 2)
                pe.wait_ge(s["kk_ready"], 2 * g + 2)
                pe.wait_ge(s["kqm_ready"], g + 1)
                for st in range(4):
                    for d in range(2):
                        n = 4 * g + st
                        if st:
                            pe.wait_ge(sd["su_ready"], 2 * (3 * g + st) + d - 1)
                            if st > LT_TILES:
                                pe.wait_ge(sd["od_ready"], 2 * (2 * g + st - LT_TILES) + d - 1)
                        pe.wait_ge(sd["gtri_ready"], 2 * (n + 1) + d - 1)
                        mm(bank[:, 4 * d, :], ones, Y[:, d].rearrange("p a b -> p (a b)"), True, True).then_inc(sd["gbc_done"], 1)
                    for d in range(2):
                        pe.wait_ge(sd["xt0_ready"], 2 * (4 * g + st + 1) + d - 1)
                        for j in range(GH):
                            last = pe.transpose(bank[:, 4 * d + 2, j * P:(j + 1) * P], XT[:, d, j, :], ident)
                        last.then_inc(sd["x0_done"], 1)
                    for b in range(1, LEVELS):
                        for d in range(2):
                            n = 4 * g + st
                            pe.wait_ge(sd["ml_ready"], 2 * (LEVELS * n + b + 1) + d - 1)
                            if b == 1:
                                pe.wait_ge(sd["x0_ready"], 2 * (n + 1) + d - 1)
                                if st >= LT_TILES:
                                    pe.wait_ge(sd["eg_ready"], 2 * (2 * g + st - 1) + d - 1)
                            else:
                                pe.wait_ge(sd["xs_ready"], 2 * (6 * n + b - 1) + d - 1)
                            for j in range(GH):
                                last = mm(bank[:, 4 * d, j * P:(j + 1) * P], ML[:, d, b % 2, j, :], X[:, d, j, :], True, True)
                            last.then_inc(sd["y_done"], 1)
                        for d in range(2):
                            n = 4 * g + st
                            pe.wait_ge(sd["yc_ready"], 2 * (6 * n + b) + d - 1)
                            if b > 1:
                                pe.wait_ge(sd["xt_ready"], 2 * (6 * n + b - 1) + d - 1)
                            for j in range(GH):
                                last = mm(bank[:, 4 * d + 1, j * P:(j + 1) * P], XT[:, d, j, :], Y[:, d, j, :], True, True)
                            last.then_inc(sd["xy_done"], 1)
                        for d in range(2):
                            n = 4 * g + st
                            pe.wait_ge(sd["xs_ready"], 2 * (6 * n + b) + d - 1)
                            for j in range(GH):
                                last = pe.transpose(bank[:, 4 * d + 2, j * P:(j + 1) * P], X[:, d, j, :], ident)
                            last.then_inc(sd["xt_done"], 1)
                    for d in range(2):
                        n = 4 * g + st
                        t = SCAN[d][st]
                        if st:
                            pe.wait_ge(sd["xt_ready"], 2 * (6 * n + 6) + d - 1)
                            pe.wait_ge(sd["kek_ready"], 2 * (n + 1) + d - 1)
                            for j in range(GH):
                                last = mm(bank[:, 4 * d, j * P:(j + 1) * P], KE[:, d, j, :], XT[:, d, j, :], True, True)
                            last.then_inc(sd["w_done"], 1)
                    for d in range(2):
                        n = 4 * g + st
                        t = SCAN[d][st]
                        if st:
                            pe.wait_ge(sd["w_ready"], 2 * (3 * g + st) + d - 1)
                        else:
                            pe.wait_ge(sd["xt_ready"], 2 * (6 * n + 6) + d - 1)
                            pe.wait_ge(sd["kek_ready"], 2 * (n + 1) + d - 1)
                        for j in range(GH):
                            o = bank[:, 4 * d + 3, j * P:(j + 1) * P]
                            last = mm(o, XT[:, d, j, :], gv_tm[:, t, j, :], True, st == 0)
                            if st:
                                last = mm(o, LT[:, d, j, :], state[:, d, j, :], False, True)
                        last.then_inc(sd["vn_done"], 1)
                    for d in range(2):
                        n = 4 * g + st
                        t = SCAN[d][st]
                        pe.wait_ge(sd["vn_ready"], 2 * (n + 1) + d - 1)
                        if st >= LT_TILES:
                            pe.wait_ge(sd["qd_ready"], 2 * (2 * g + st - 1) + d - 1)
                            pe.wait_ge(sd["at_ready"], 2 * (2 * g + st - 1) + d - 1)
                            for j in range(GH):
                                o = bank[:, 4 * d + 1, j * P:(j + 1) * P]
                                mm(o, state[:, d, j, :], QD[:, d, j, :], True, False)
                                last = mm(o, E[:, d, j, :], AT[:, d, j, :], False, True)
                            last.then_inc(sd["od_done"], 1)
                        if st < 3:
                            for j in range(GH):
                                last = mm(bank[:, 4 * d + 3, j * P:(j + 1) * P], KD[:, d, j, :], E[:, d, j, :], True, True)
                            last.then_inc(sd["su_done"], 1)
                for half in range(2):
                    pe.wait_ge(s["oacc_sq"], 2 * g + half + 1)
                    mm(bank[:, half * 4, :], ones, gdn_sq[:, half, :], True, True).then_inc(s["oacc_ssq"], 1)

            def mean_square(i):
                for k in range(DC):
                    pe.wait_ge(s["sq_ready"], DC * i + k + 1)
                    last = mm(bank[:, 0, 0:SEQ], ones, sq2[:, k, :], k == 0, k == DC - 1)
                last.then_inc(s["ssq_done"], 1)

            def mixer(l):
                T = SEQ
                pe.wait_ge(s["u_ready"], U_MIX(l) + DC)
                for p in range(4):
                    load_done(pe, "mix_in", p % SLOTS, p // SLOTS, l)
                    w = slot_view(p % SLOTS, DC, 512)
                    for j in range(4 if p < 3 else 1):
                        o = bank[:, 2 * p + j // 2, j % 2 * T:(j % 2 + 1) * T]
                        for k in range(DC):
                            last = mm(o, w[:, k, j * P:(j + 1) * P], u[:, k, 0:T], k == 0, k == DC - 1)
                        if j == 1:
                            last.then_inc(s["mixp_done"], 1)
                        if j == 3:
                            last.then_inc(panel_done[p % SLOTS], 1)
                    if p == 3:
                        for k in range(DC):
                            last = mm(bank[0:GLA_RANK, 6, T:2 * T], w_glr[:, k, :], u[:, k, 0:T], k == 0, k == DC - 1)
                        last.then_inc(s["glr_done"], 1)
                        for t in range(2):
                            if t:
                                pe.wait_ge(s["gqk_ready"], l + 1)
                            o = bank[:, 7 if t == 0 else 0, 0:3 * P]
                            for k in range(DC):
                                last = mm(o, u[:, k, t * P:(t + 1) * P], w[:, k, P:4 * P], k == 0, k == DC - 1)
                            last.then_inc(panel_done[p % SLOTS] if t else s["mixp_done"], 1)
                pe.wait_ge(s["glr_ready"], l + 1)
                mm(bank[:, 6, 0:T], gate2[0:GLA_RANK, :], glr_s[0:GLA_RANK, :], True, True).then_inc(s["gate_done"], 1)
                pe.wait_ge(s["swq_ready"], 3 * l + 3)
                pe.wait_ge(s["gv_ready"], 2 * l + 2)
                pe.wait_ge(s["sig_ready"], l + 1)
                pe.wait_ge(s["gr_ready"], l + 1)
                pe.wait_ge(s["conv_u"], l + 1)
                pe.wait_ge(s["gy_ready"], l + 1)
                for hd in range(SWA_HEADS):
                    kv = hd // 4
                    r = slice(64 * kv, 64 * kv + 64)
                    mm(bank[:, hd, 0:P], s_q[r, hd % 4, 0:P], s_k[r, 0:P], True, True)
                    mm(bank[:, hd, P:3 * P], s_q[r, hd % 4, P:T], s_k[r, :], True, True).then_inc(s["sw_done"], 1)
                pe.wait_ge(s["gqe_ready"], l + 1)
                for t in range(3):
                    for hd in range(GLA_HEADS):
                        r = slice(GLA_DK * hd, GLA_DK * hd + GLA_DK)
                        if t == 0:
                            pe.wait_ge(s["swb_ready"], SWA_HEADS * l + 2 * hd + 2)
                        elif t == 1:
                            pe.wait_ge(s["att_ready"], 12 * l + hd + 1)
                        else:
                            pe.wait_ge(s["att_ready"], 12 * l + 4 + hd + 1)
                        if t < 2:
                            cols = slice(t * P, (t + 1) * P)
                            for lv in range(8):
                                o = bank[:, 2 * hd + lv // 4, lv % 4 * P:(lv % 4 + 1) * P]
                                kk_, qq_ = (gqk[r, 1, cols], gqk[r, 0, cols]) if lv == 0 else (ke[r, lv - 1, cols], qe[r, lv - 1, cols])
                                last = pe.matmul(o, kk_, qq_, start=True, stop=True)
                        else:
                            last = pe.matmul(bank[:, 2 * hd, 0:P], ke[r, 7, 0:P], qe[r, 7, P:T], start=True, stop=True)
                        last.then_inc(s["gs_done"], 1)
                pe.wait_ge(s["att_ready"], 12 * l + 12)
                for hd in range(GLA_HEADS):
                    r = slice(64 * (hd % 2), 64 * (hd % 2) + 64)
                    vc = slice(GLA_DV * hd, GLA_DV * hd + GLA_DV)
                    o = bank[r, hd // 2, :]
                    mm(o[:, 0:P], g_v[:, 0, vc], att[:, hd, 0, :], True, True)
                    mm(o[:, P:T], g_v[:, 0, vc], att[:, hd, 2, :], True, False)
                    last = mm(o[:, P:T], g_v[:, 1, vc], att[:, hd, 1, :], False, True)
                last.then_inc(s["go_done"], 1)
                pe.wait_ge(s["swp_ready"], l + 1)
                for b in range(6):
                    for j in range(4):
                        i = 4 * b + j
                        last = pe.transpose(bank[:, 2 + b, j * P:(j + 1) * P], swp[:, i // 3, i % 3, :], ident)
                    last.then_inc(s["swt_done"], 1)
                pe.wait_ge(s["go_sq"], l + 1)
                for b in range(2):
                    last = mm(bank[:, 0, b * T:(b + 1) * T], ones64, og_sq[:, b, :], True, True)
                last.then_inc(s["go_ssq"], 1)
                pe.wait_ge(s["cvy_ready"], l + 1)
                for b in range(2):
                    last = mm(bank[:, 1, 0:T], ones, conv_y[:, b, :], b == 0, b == 1)
                last.then_inc(s["cv_mean"], 1)
                pe.wait_ge(s["cv_sq_ready"], l + 1)
                for b in range(2):
                    last = mm(bank[:, 1, T:2 * T], ones, cv_sq[:, b, :], b == 0, b == 1)
                last.then_inc(s["cv_var"], 1)
                pe.wait_ge(s["swt_ready"], 6 * l + 6)
                for hd in range(SWA_HEADS):
                    kv = hd // 4
                    r = slice(64 * kv, 64 * kv + 64)
                    o = bank[r, 2 + hd % 4, :]
                    vc = slice(SWA_DH * kv, SWA_DH * kv + SWA_DH)
                    mm(o[:, 0:P], s_v[:, 0, vc], swt[:, hd, 0, :], True, True)
                    mm(o[:, P:T], s_v[:, 0, vc], swt[:, hd, 1, :], True, False)
                    last = mm(o[:, P:T], s_v[:, 1, vc], swt[:, hd, 2, :], False, True)
                last.then_inc(s["swo_done"], 1)
                pe.wait_ge(s["swo_ready"], l + 1)
                pe.wait_ge(s["gla_ready"], l + 1)
                pe.wait_ge(s["cv_ready"], l + 1)
                for p in range(2):
                    load_done(pe, "mix_out", p, 0, l)
                    w = slot_view(p, DC, 512)
                    for j in range(4):
                        for k in range(DC):
                            last = mm(bank[:, 4 * p + j, 0:T], w[:, k, j * P:(j + 1) * P], mix[:, k, :], k == 0, k == DC - 1)
                        last.then_inc(s["yproj"] if j < 3 else panel_done[p], 1)

            modulation(0)
            if stop == "mod":
                return
            mla()
            layer_norm(0, TOK)
            ffn(0, TOK, "ffn0", "down0", DC)
            layer_norm(1, TOK)
            modulation(1)
            gdn()
            layer_norm(2, SEQ)
            ffn(1, SEQ, "ffn1", "down1", U_FFN1)
            layer_norm(3, SEQ)
            with pe.Fori(0, DEPTH) as l:
                mean_square(6 * l)
                ffn(2 * l + 2, SEQ, "ffnA", "downA", U_BLOCK2 + 3 * DC * l, l)
                mean_square(6 * l + 1)
                mean_square(6 * l + 2)
                mixer(l)
                mean_square(6 * l + 3)
                mean_square(6 * l + 4)
                ffn(2 * l + 3, SEQ, "ffnB", "downB", U_BLOCK2 + 3 * DC * l + 2 * DC, l)
                mean_square(6 * l + 5)

        @block.scalar
        def _(act):
            act.wait_ge(in_loaded, 48)
            act.activation(cond[:], cvec, ACT.Silu).then_inc(s["cond_ready"], 1)

            def copy(o, i, scale=1.0):
                return act.activation(o, i, ACT.Copy, scale=scale)

            def mla():
                for b in range(QC + KC):
                    act.wait_ge(s["lat_copied"], b + 1)
                    act.activation(lat_sq[:, b, :], lat[:, b, :], ACT.Square).then_inc(s["lat_squared"], 1)
                for b, n in enumerate([Q_RANK, KV_RANK]):
                    act.wait_ge(s["lat_ssq"], b + 1)
                    act.activation(std[:, b, :], bank[:, b, :], ACT.Sqrt, bias=EPS_RMS, scale=1.0 / n).then_inc(s["lat_std"], 1)
                for j in range(HEADS):
                    if j < HEADS - 1:
                        act.wait_ge(s["qn_done"], j + 1)
                    else:
                        panel_over(act, "mla", 2, 0)
                    copy(q_n[:, j, :], bank[:, j, :]).then_inc(s["qn_ready"], 1)
                for j in range(HEADS):
                    act.wait_ge(s["kn_done"], j + 1)
                    copy(k_n[:, j, :], bank[:, j, :]).then_inc(s["kn_ready"], 1)
                for n in range(8):
                    if n < 7:
                        act.wait_ge(s["v_done"], n + 1)
                    else:
                        panel_over(act, "mla", 1, 1)
                    copy(v_tm[:, n // 2, n % 2 * 512:n % 2 * 512 + 512], bank[:, n, :]).then_inc(s["v_ready"], 1)
                for hd in range(HEADS):
                    act.wait_ge(s["max_ready"], hd + 1)
                    d = hd % 2
                    for i in range(4):
                        b, cols = (i, slice(0, 512)) if i < 2 else (2, slice((i - 2) * CTX, (i - 1) * CTX))
                        last = act.activation(probs[:, d, b, cols], bank[:, b, cols], ACT.Exp, bias=negmax[:, d, i:i + 1],
                                              scale=MLA_SCALE, accum_out=rowsum[:, d, i:i + 1])
                    last.then_inc(s["exp_done"], 1)
                    if hd:
                        act.wait_ge(s["pv_done"], hd)
                    for t in range(LT_TILES):
                        act.wait_ge(s["pt_done"], 3 * hd + t + 1)
                        last = copy(probs_t[:, :, t * P:(t + 1) * P], bank[:, 3 + t, :].rearrange("p (k q) -> p k q", k=TILES))
                    last.then_inc(s["pt_lat"], 1)

            def gated(n, T, row, over):
                for m in range(DC):
                    over(act, m)
                    for seg in range(T // SEQ):
                        cols = slice(seg * SEQ, (seg + 1) * SEQ)
                        last = copy(resid[:, m, cols], bank[:, m, cols], scale=mod[:, row * DC + m, seg:seg + 1])
                    last.then_inc(s["yg_ready"], 1)

            def layer_norm(n, l, T):
                for k in range(DC):
                    act.wait_ge(s["cent_ready"], DC * n + k + 1)
                    act.activation(sq[:, k, 0:T], resid[:, k, 0:T], ACT.Square).then_inc(s["cent_sq"], 1)
                act.wait_ge(s["var_done"], n + 1)
                act.activation(std[:, 0, 0:T], bank[:, 1, 0:T], ACT.Sqrt, bias=EPS_LN, scale=1.0 / D).then_inc(s["var_std"], 1)
                for k in range(DC):
                    act.wait_ge(s["norm_ready"], DC * n + k + 1)
                    act.activation(h[:, k, 0:T], resid[:, k, 0:T], ACT.Identity, bias=ln_b[n % 2][:, l, k:k + 1]).then_inc(s["h_ready"], 1)

            def ffn(f, T, name, layer=0):
                def pair(slot, turn, half):
                    if half:
                        panel_over(act, name, slot, turn, layer)
                    else:
                        act.wait_ge(s["pair_done"], 11 * f + SLOTS * turn + slot + 1)
                    q = (2 * slot + half) % 3
                    act.activation(silu_g[:, q, 0:T], bank[:, 2 * q, 0:T], ACT.Silu).then_inc(s["silu_ready"], 1)

                with act.Fori(0, 11 // SLOTS) as i:
                    for slot in range(SLOTS):
                        for half in range(2):
                            pair(slot, i, half)
                for p in range(11 // SLOTS * SLOTS, 11):
                    for half in range(2):
                        pair(p % SLOTS, p // SLOTS, half)

            def gdn_gates():
                act.wait_ge(s["ba_done"], 1)
                ba = bank[:, 2, 0:TILES * 64].rearrange("p (t d w h) -> p t d w h", t=TILES, d=2, w=2)
                for d in range(2):
                    last = act.activation(BETA[:, d], ba[:, :, d, 0, :], ACT.Sigmoid)
                last.then_inc(s["beta_ready"], 1)
                act.activation(a_log, a_log, ACT.Exp).then_inc(s["alog_ready"], 1)
                act.wait_ge(s["ax_ready"], 1)
                act.activation(soft[:, 1], soft[:, 1], ACT.Exp).then_inc(s["sp_exp"], 1)
                act.wait_ge(s["sp_exp"], 1)
                act.activation(soft[:, 1], soft[:, 1], ACT.Ln, bias=ONE).then_inc(s["sp_ln"], 1)
                act.wait_ge(s["gcum_ready"], 1)
                act.activation(EG, GCUM, ACT.Exp)
                act.activation(ED, ED, ACT.Exp)
                act.activation(ETOT, ETOT, ACT.Exp).then_inc(s["gexp_ready"], 1)

            def gdn_group(g):
                raw = [k_fm[:, 0, :], k_fm[:, 1, :], q_fm[:, 0, :], q_fm[:, 1, :]] + [v_fm[:, j, :] for j in range(GH)]

                def silu(b):
                    act.wait_ge(s["conv_done"], 8 * g + b + 3)
                    act.activation(raw[b], raw[b], ACT.Silu).then_inc(s["act_ready"], 1)

                for b in range(8):
                    if b in (0, 1):
                        act.wait_ge(s["proj_done"], 5 * g + b + 1)
                    elif b < 4:
                        panel_over(act, "gdn", 0, g)
                    elif b < 7:
                        act.wait_ge(s["proj_done"], 5 * g + b - 1)
                    else:
                        panel_over(act, "gdn", 1, g)
                    act.wait_ge(s["conv_done"], 8 * g + b + 1)
                    if 2 <= b < 4:
                        i = bank[:, 2, (b - 2) * SEQ:(b - 1) * SEQ]
                        copy(cin[:, b % 2, 0, 2:2 + SEQ], i).then_inc(s["cin_ready"], 1)
                    else:
                        i = bank[:, b if b < 2 else b - 1, :].rearrange("p (s t) -> p s t", s=2)
                        copy(cin[:, b % 2, :, 2:2 + SEQ], i).then_inc(s["cin_ready"], 1)
                    if b:
                        silu(b - 1)
                silu(7)
                for i, b in enumerate([7, 0]):
                    if i == 0:
                        act.wait_ge(s["zproj_done"], g + 1)
                    else:
                        panel_over(act, "gdn", 2, g)
                    act.activation(z_s[:, 2 * i:2 * i + 2, :], bank[:, b, :].rearrange("p (a t) -> p a t", a=2), ACT.Silu).then_inc(s["z_ready"], 1)
                act.drain()
                for j in range(GKH):
                    act.activation(gdn_sq[:, j, :], k_fm[:, j, :], ACT.Square).then_inc(s["kq_sq"], 1)
                act.activation(gdn_sq[:, 2, :], q_fm.rearrange("p a t -> p (a t)"), ACT.Square).then_inc(s["kq_sq"], 1)
                for j in range(GH):
                    act.wait_ge(s["vt_done"], GH * g + j + 1)
                    copy(gv_tm[:, :, j, :], bank[:, 3 + j, :].rearrange("p (t q) -> p t q", t=TILES)).then_inc(s["vt_ready"], 1)
                for j, b in enumerate([1, 2, 7]):
                    act.wait_ge(s["kq_ssq"], 3 * g + j + 1)
                    act.activation(gdn_std[:, j, :], bank[:, b, :], ACT.Sqrt, bias=EPS_RMS).then_inc(s["kq_std"], 1)
                for i in range(2):
                    act.wait_ge(s["kk_done"], 3 * g + i + 1)
                    copy(kk[:, 2 * i:2 * i + 2], bank[:, 5 + i, :].rearrange("p (t j q) -> p t j q", t=2, j=GKH)).then_inc(s["kk_ready"], 1)
                for st in range(4):
                    n = 4 * g + st
                    for d in range(2):
                        act.wait_ge(sd["diff_ready"], 2 * (n + 1) + d - 1)
                        act.activation(E[:, d], E[:, d], ACT.Exp).then_inc(sd["decay_ready"], 1)
                        if st >= LT_TILES:
                            act.activation(QD[:, d], bank[:, 4 * d, :].rearrange("p (j q) -> p j q", j=GH), ACT.Exp).then_inc(sd["eg_ready"], 1)
                    for d in range(2):
                        act.wait_ge(sd["x0_done"], 2 * (n + 1) + d - 1)
                        copy(X[:, d], bank[:, 4 * d + 2, :].rearrange("p (j q) -> p j q", j=GH)).then_inc(sd["x0_ready"], 1)
                    for b in range(1, LEVELS):
                        for d in range(2):
                            act.wait_ge(sd["y_done"], 2 * (6 * n + b) + d - 1)
                            copy(Y[:, d], bank[:, 4 * d, :].rearrange("p (j q) -> p j q", j=GH)).then_inc(sd["yc_ready"], 1)
                        for d in range(2):
                            act.wait_ge(sd["xt_done"], 2 * (6 * n + b) + d - 1)
                            copy(XT[:, d], bank[:, 4 * d + 2, :].rearrange("p (j q) -> p j q", j=GH)).then_inc(sd["xt_ready"], 1)
                    if st:
                        for d in range(2):
                            act.wait_ge(sd["w_done"], 2 * (3 * g + st) + d - 1)
                            copy(LT[:, d], bank[:, 4 * d, :].rearrange("p (j q) -> p j q", j=GH), scale=-1.0).then_inc(sd["w_ready"], 1)
                for half in range(2):
                    if half == 0:
                        act.wait_ge(sd["od_ready"], 2 * (2 * g + 2))
                    act.activation(gdn_sq[:, half, :].rearrange("p (a t) -> p a t", a=2), o_acc[:, 2 * half:2 * half + 2, :], ACT.Square).then_inc(s["oacc_sq"], 1)
                for half in range(2):
                    act.wait_ge(s["oacc_ssq"], 2 * g + half + 1)
                    act.activation(gdn_std[:, half, :], bank[:, 4 * half, :], ACT.Sqrt, bias=EPS_RMS, scale=1.0 / P).then_inc(s["oacc_std"], 1)

            def root(i, twice):
                act.wait_ge(s["ssq_done"], i + 1)
                act.activation(std[:, 0, 0:SEQ], bank[:, 0, 0:SEQ], ACT.Sqrt, bias=EPS_RMS4 if twice else EPS_RMS,
                               scale=(4.0 if twice else 1.0) / D).then_inc(s["std_ready"], 1)

            def squares_of_x(batch):
                for k in range(DC):
                    act.wait_ge(s["x_ready"], DC * batch + k + 1)
                    act.activation(sq2[:, k, :], h[:, k, 0:SEQ], ACT.Square).then_inc(s["sq_ready"], 1)

            def squares_of_y(batch):
                for k in range(DC):
                    act.wait_ge(s["yb_ready"], DC * batch + k + 1)
                    act.activation(sq2[:, k, :], yb[:, k, :], ACT.Square).then_inc(s["sq_ready"], 1)

            def mixer(l):
                T = SEQ
                act.wait_ge(s["mixp_done"], 4 * l + 1)
                copy(gqk[:, 0, :], bank[:, 0, 0:T], scale=GLA_DK ** -0.5)
                copy(gqk[:, 1, :], bank[:, 0, T:2 * T]).then_inc(s["gqk_ready"], 1)
                two = lambda b: bank[:, b, :].rearrange("p (a t) -> p a t", a=2)
                panel_over(act, "mix_in", 0, 0, l)
                act.activation(gr_s, two(1), ACT.Silu).then_inc(s["gr_ready"], 1)
                panel_over(act, "mix_in", 1, 0, l)
                act.activation(sig_g, two(3), ACT.Sigmoid).then_inc(s["sig_ready"], 1)
                act.wait_ge(s["mixp_done"], 4 * l + 3)
                copy(s_q[:, 0:2, :], two(4), scale=SWA_DH ** -0.5).then_inc(s["swq_ready"], 1)
                panel_over(act, "mix_in", 2, 0, l)
                copy(s_q[:, 2:4, :], two(5), scale=SWA_DH ** -0.5).then_inc(s["swq_ready"], 1)
                act.wait_ge(s["glr_done"], l + 1)
                copy(s_k, bank[:, 6, 0:T]).then_inc(s["swq_ready"], 1)
                copy(glr_s[0:GLA_RANK, :], bank[0:GLA_RANK, 6, T:2 * T]).then_inc(s["glr_ready"], 1)
                for t in range(2):
                    if t == 0:
                        act.wait_ge(s["mixp_done"], 4 * l + 4)
                    else:
                        panel_over(act, "mix_in", 0, 1, l)
                    b = 7 if t == 0 else 0
                    copy(g_v[:, t, :], bank[:, b, 0:2 * P])
                    copy(s_v[:, t, :], bank[:, b, 2 * P:3 * P]).then_inc(s["gv_ready"], 1)
                act.wait_ge(s["ge_ready"], l + 1)
                act.activation(gl_e, gl_e, ACT.Exp)
                act.drain()
                act.activation(gl_e, gl_e, ACT.Ln, bias=ONE).then_inc(s["gln_ready"], 1)
                act.wait_ge(s["swm_ready"], l + 1)
                for hd in range(SWA_HEADS):
                    act.activation(swp[:, hd, 0, :], swp[:, hd, 0, :], ACT.Exp, bias=swm[:, hd, 0:1], accum_out=sws[:, hd, 0:1])
                    act.activation(swp[:, hd, 1:3, :], swp[:, hd, 1:3, :], ACT.Exp, bias=swm[:, hd, 1:2], accum_out=sws[:, hd, 1:2])
                act.activation(swe, swe, ACT.Exp).then_inc(s["swe_ready"], 1)
                act.wait_ge(s["gabs_ready"], l + 1)
                act.activation(dec, dec, ACT.Exp, scale=1.0 / GLA_TAU).then_inc(s["gdec_ready"], 1)
                act.wait_ge(s["go_ready"], 2 * l + 2)
                act.activation(og_sq, og, ACT.Square).then_inc(s["go_sq"], 1)
                flat = swt.rearrange("p h k q -> p (h k q)")
                for b in range(6):
                    act.wait_ge(s["swt_done"], 6 * l + b + 1)
                    copy(flat[:, 512 * b:512 * b + 512], bank[:, 2 + b, :]).then_inc(s["swt_ready"], 1)
                act.wait_ge(s["go_ssq"], l + 1)
                act.activation(std[:, 0, :], bank[:, 0, :], ACT.Sqrt, bias=EPS_RMS, scale=1.0 / GLA_DV).then_inc(s["go_std"], 1)
                act.wait_ge(s["cv_cent"], l + 1)
                act.activation(cv_sq, conv_y, ACT.Square).then_inc(s["cv_sq_ready"], 1)
                act.wait_ge(s["cv_var"], l + 1)
                act.activation(gl_e, bank[:, 1, T:2 * T], ACT.Sqrt, bias=EPS_LN, scale=1.0 / (2 * P)).then_inc(s["cv_std"], 1)
                act.wait_ge(s["cv_norm"], l + 1)
                for b in range(2):
                    last = act.activation(mix[:, 2 + b, :], conv_y[:, b, :], ACT.Silu, bias=conv_ln_b[:, b:b + 1])
                last.then_inc(s["cv_ready"], 1)
                act.wait_ge(s["swo_done"], l + 1)
                for b in range(4):
                    last = copy(mix[:, 4 + b, :], bank[:, 2 + b, 0:T])
                last.then_inc(s["swo_ready"], 1)

            def over_down(name, layer=0):
                return lambda e, m: panel_over(e, name, m % SLOTS, m // SLOTS, layer)

            act.wait_ge(s["mod_ready"], 1)
            mla()
            gated(0, TOK, 2, mla_out_over)
            layer_norm(0, 0, TOK)
            ffn(0, TOK, "ffn0")
            gated(1, TOK, 5, over_down("down0"))
            layer_norm(1, 0, TOK)
            act.wait_ge(s["mod_ready"], 2)
            gdn_gates()
            with act.Fori(0, GROUPS) as g:
                gdn_group(g)
            gated(2, SEQ, 2, gdn_out_over)
            layer_norm(2, 1, SEQ)
            ffn(1, SEQ, "ffn1")
            gated(3, SEQ, 5, over_down("down1"))
            layer_norm(3, 1, SEQ)
            with act.Fori(0, DEPTH) as l:
                act.wait_ge(lpar_loaded, 16 * l + 16)
                squares_of_x(3 * l)
                root(6 * l, False)
                ffn(2 * l + 2, SEQ, "ffnA", l)
                squares_of_y(3 * l)
                root(6 * l + 1, True)
                squares_of_x(3 * l + 1)
                root(6 * l + 2, False)
                mixer(l)
                squares_of_y(3 * l + 1)
                root(6 * l + 3, False)
                squares_of_x(3 * l + 2)
                root(6 * l + 4, False)
                ffn(2 * l + 3, SEQ, "ffnB", l)
                squares_of_y(3 * l + 2)
                root(6 * l + 5, True)

        @block.gpsimd
        def _(pool):
            def gdn_group(g):
                pool.wait_ge(s["gst_ready"], g + 1)
                pool.wait_ge(s["kt_ready"], 2 * g + 2)
                pool.wait_ge(s["kq_ready"], 3 * g + 3)
                for st in range(4):
                    n = 4 * g + st
                    for d in range(2):
                        t = SCAN[d][st]
                        if st:
                            pool.wait_ge(sd["xy_done"], 2 * (6 * n) + d - 1)
                            pool.wait_ge(sd["su_done"], 2 * (3 * g + st) + d - 1)
                        pool.tensor_tensor(Y[:, d], wide(tri[:, d, :], GH, 1), wide(S_G[:, d, t, :], P, 2), ALU.mult).then_inc(sd["gtri_ready"], 1)
                    for d in range(2):
                        t = SCAN[d][st]
                        for j in range(GH):
                            if st:
                                last = pool.tensor_scalar(KE[:, d, j, :], k_tm[:, t, j // 2, :], S_EG[:, d, t, j:j + 1], 1.0, ALU.mult, ALU.mult)
                            if st < 3:
                                last = pool.tensor_scalar(KD[:, d, j, :], k_tm[:, t, j // 2, :], S_ED[:, d, t, j:j + 1], 1.0, ALU.mult, ALU.mult)
                        last.then_inc(sd["kek_ready"], 1)
                    for b in range(LEVELS):
                        for d in range(2):
                            t = SCAN[d][st]
                            if b == 0:
                                pool.wait_ge(sd["lt_ready"], 2 * (n + 1) + d - 1)
                            if b == 2:
                                pool.wait_ge(sd["xt0_ready"], 2 * (n + 1) + d - 1)
                            if b > 2:
                                pool.wait_ge(sd["y_done"], 2 * (6 * n + b - 2) + d - 1)
                            pool.tensor_tensor(ML[:, d, b % 2], LT[:, d], wide(level[:, d, b, :], GH, 1), ALU.mult).then_inc(sd["ml_ready"], 1)
                            if b == 1 and st >= LT_TILES:
                                if st == 3:
                                    pool.wait_ge(sd["od_done"], 2 * (2 * g + 1) + d - 1)
                                pair = "p (a r) q -> p a r q"
                                pool.tensor_tensor(AT[:, d].rearrange(pair, r=2), E[:, d].rearrange(pair, r=2),
                                                   wide(kq[:, d, t], 2, 2), ALU.mult).then_inc(sd["at_ready"], 1)

            with pool.Fori(0, GROUPS) as g:
                gdn_group(g)

        @block.vector
        def _(dve):
            dve.sem_inc(s["pair_free"], 3)
            dve.sem_inc(s["conv_done"], 2)
            dve.sem_inc(s["y_ready"], 1)
            dve.sem_inc(s["layer_done"], 1)
            dve.wait_ge(in_loaded, 48)

            def modulation(l):
                panel_over(dve, f"mod{l}", 2, 3)
                dve.tensor_tensor(mod[:], bank[:, 7, 0:2 * MB].rearrange("p (m s) -> p m s", s=2),
                                  wide(b_mod[:, l, :], 2, 2), ALU.add)
                dve.drain()
                for row in (1, 4):
                    rows = mod[:, row * DC:(row + 1) * DC, :]
                    last = dve.tensor_scalar(rows, rows, 1.0, None, ALU.add)
                last.then_inc(s["mod_ready"], 1)
                dve.drain()

            def modulate(shift, scale, T, n=None):
                for k in range(DC):
                    if n is not None:
                        dve.wait_ge(s["h_ready"], DC * n + k + 1)
                    for seg in range(T // SEQ):
                        cols = slice(seg * SEQ, (seg + 1) * SEQ)
                        last = dve.tensor_scalar(u[:, k, cols], h[:, k, cols], mod[:, scale * DC + k, seg:seg + 1],
                                                 mod[:, shift * DC + k, seg:seg + 1], ALU.mult, ALU.add)
                    last.then_inc(s["u_ready"], 1)

            def rope(o, nat, swapped):
                dve.tensor_tensor(rope_t[:, 0, :], nat, rope_cos, ALU.mult)
                dve.tensor_tensor(rope_t[:, 1, :], swapped, rope_sin, ALU.mult)
                dve.drain()
                dve.tensor_tensor(o, rope_t[:, 0, :], rope_t[:, 1, :], ALU.add)
                dve.drain()

            def mla():
                for b in range(QC + KC):
                    if b % 4 == 3:
                        panel_over(dve, "mla", 0, 0)
                    else:
                        dve.wait_ge(s["lat_done"], b + 1 - b // 4)
                    dve.tensor_copy(lat[:, b, :], bank[:, b, :]).then_inc(s["lat_copied"], 1)
                panel_over(dve, "mla", 1, 0)
                rope(krope[:, 0:SEQ], bank[:, 6, 0:SEQ], bank[:, 7, 0:SEQ])
                dve.tensor_copy(krope[:, SEQ:TOK], bank[:, 6, SEQ:TOK]).then_inc(s["krope_ready"], 1)
                for b, (a, n, g) in enumerate([(0, QC, q_norm), (QC, KC, kv_norm)]):
                    dve.wait_ge(s["lat_std"], b + 1)
                    dve.reciprocal(std[:, b, :], std[:, b, :])
                    dve.drain()
                    for k in range(n):
                        dve.scalar_tensor_tensor(lat[:, a + k, :], lat[:, a + k, :], g[:, k:k + 1], std[:, b, :],
                                                 ALU.mult, ALU.mult).then_inc(s["latn_ready"], 1)
                panel_over(dve, "mla", 0, 1)
                for j in range(HEADS // 2):
                    rope(q_r[:, j, 0:SEQ], bank[:, j, 0:SEQ], bank[:, 4 + j, 0:SEQ])
                    dve.tensor_copy(q_r[:, j, SEQ:TOK], bank[:, j, SEQ:TOK]).then_inc(s["qr_ready"], 1)

                def maxima(hd):
                    d = hd % 2
                    dve.wait_ge(s["s_done"], 2 * hd + 1)
                    for t in range(LT_TILES):
                        dve.tensor_reduce(negmax[:, d, t:t + 1], bank[:, t, :], AX_X, ALU.max, negate=True)
                    dve.wait_ge(s["s_done"], 2 * hd + 2)
                    dve.tensor_reduce(negmax[:, d, 2:4], bank[:, 2, :].rearrange("p (t k) -> p t k", t=2), AX_X, ALU.max, negate=True)
                    dve.drain()
                    dve.tensor_scalar(negmax[:, d, :], negmax[:, d, :], MLA_SCALE, None, ALU.mult).then_inc(s["max_ready"], 1)

                def normed(hd):
                    d = hd % 2
                    dve.wait_ge(s["exp_done"], hd + 1)
                    dve.reciprocal(rowsum[:, d, :], rowsum[:, d, :])
                    dve.drain()
                    for i in range(4):
                        b, cols = (i, slice(0, 512)) if i < 2 else (2, slice((i - 2) * CTX, (i - 1) * CTX))
                        p = probs[:, d, b, cols]
                        last = dve.tensor_scalar(p, p, rowsum[:, d, i:i + 1], None, ALU.mult)
                    last.then_inc(s["p_ready"], 1)

                maxima(0)
                for hd in range(HEADS):
                    normed(hd)
                    if hd + 1 < HEADS:
                        maxima(hd + 1)
                    if hd:
                        dve.wait_ge(s["pv_done"], hd)
                    dve.wait_ge(s["pt_done"], 3 * hd + 3)
                    dve.tensor_copy(probs_tc.rearrange("p k (t q) -> p t k q", t=2),
                                    bank[:, 5, :].rearrange("p (t k q) -> p t k q", t=2, k=2)).then_inc(s["pt_ctx"], 1)
                    dve.wait_ge(s["pv_done"], hd + 1)
                    dve.tensor_copy(u[:, hd, :], bank[:, 6 + hd % 2, :]).then_inc(s["o_ready"], 1)

            def layer_norm(n, l, T):
                for m in range(DC):
                    dve.wait_ge(s["yg_ready"], DC * n + m + 1)
                    dve.scalar_tensor_tensor(resid[:, m, 0:T], h[:, m, 0:T], ALPHA, resid[:, m, 0:T],
                                             ALU.mult, ALU.add).then_inc(s["r_ready"], 1)
                dve.wait_ge(s["mean_done"], n + 1)
                for k in range(DC):
                    dve.scalar_tensor_tensor(resid[:, k, 0:T], bank[:, 0, 0:T], -1.0 / D, resid[:, k, 0:T],
                                             ALU.mult, ALU.add).then_inc(s["cent_ready"], 1)
                dve.wait_ge(s["var_std"], n + 1)
                dve.reciprocal(std[:, 1, 0:T], std[:, 0, 0:T])
                dve.drain()
                for k in range(DC):
                    dve.scalar_tensor_tensor(resid[:, k, 0:T], resid[:, k, 0:T], ln_g[n % 2][:, l, k:k + 1], std[:, 1, 0:T],
                                             ALU.mult, ALU.mult).then_inc(s["norm_ready"], 1)

            def ffn(f, T):
                def pair(q, b):
                    dve.wait_ge(s["silu_ready"], FC * f + q + 1)
                    dve.tensor_tensor(hidden[:, q, 0:T], silu_g[:, b, 0:T], bank[:, 2 * b + 1, 0:T],
                                      ALU.mult).then_inc(s["pair_free"], 1)

                with dve.Fori(0, 11 // SLOTS) as i:
                    for j in range(2 * SLOTS):
                        pair(i * (2 * SLOTS) + j, j % 3)
                for q in range(11 // SLOTS * SLOTS * 2, FC):
                    pair(q, q % 3)

            def gdn_gates():
                dve.wait_ge(s["beta_ready"], 1)
                ba = bank[:, 2, 0:TILES * 64].rearrange("p (t d w h) -> p t d w h", t=TILES, d=2, w=2)
                for d in range(2):
                    dve.tensor_tensor(soft[:, 0, d], ba[:, :, d, 1, :], wide(dt_bias[:, 16 * d:16 * d + 16], TILES, 1), ALU.add)
                dve.drain()
                dve.scalar_tensor_tensor(soft[:, 1], soft[:, 0], -1.0, soft[:, 0], ALU.mult, ALU.min).then_inc(s["ax_ready"], 1)
                dve.wait_ge(s["sp_ln"], 1)
                dve.scalar_tensor_tensor(soft[:, 0], soft[:, 0], 0.0, soft[:, 1], ALU.max, ALU.add)
                dve.drain()
                dve.wait_ge(s["alog_ready"], 1)
                for d in range(2):
                    last = dve.scalar_tensor_tensor(G_[:, d], soft[:, 0, d], -1.0, wide(a_log[:, 16 * d:16 * d + 16], TILES, 1),
                                                    ALU.mult, ALU.mult)
                last.then_inc(s["g_ready"], 1)
                dve.wait_ge(s["gcum_done"], 1)
                half = bank[:, 3, 0:256].rearrange("p (w d t h) -> p w d t h", w=2, d=2, t=TILES)
                dve.tensor_copy(GCUM, half[:, 0])
                dve.tensor_copy(ETOT, half[:, 1])
                dve.drain()
                dve.tensor_tensor(ED, ETOT, GCUM, ALU.subtract).then_inc(s["gcum_ready"], 1)

            def gdn_group(g):
                raw = [k_fm[:, 0, :], k_fm[:, 1, :], q_fm[:, 0, :], q_fm[:, 1, :]] + [v_fm[:, j, :] for j in range(GH)]
                dve.memset(cin[:, :, :, 0:2], 0.0)
                dve.memset(cin[:, :, :, 2 + SEQ:4 + SEQ], 0.0).then_inc(s["pad_ready"], 1)
                dve.wait_ge(s["gexp_ready"], 1)
                dve.tensor_copy(gst.rearrange("p k d t h -> p (k d t) h"),
                                gates.rearrange("p k d t h -> p (k d t) h")[:, :, bass.ds(g * GH, GH)]).then_inc(s["gst_ready"], 1)
                dve.tensor_copy(cst, conv5[:, g, :])
                dve.drain()
                for b in range(8):
                    dve.wait_ge(s["cin_ready"], 8 * g + b + 1)
                    segs = slice(0, 1) if 2 <= b < 4 else slice(0, 2)
                    o = raw[b].rearrange("p (s t) -> p s t", t=SEQ)
                    for j in range(TAPS):
                        tap, w = cin[:, b % 2, segs, j:j + SEQ], cst[:, b * TAPS + j:b * TAPS + j + 1]
                        if j == 0:
                            last = dve.tensor_scalar(o, tap, w, None, ALU.mult)
                        else:
                            last = dve.scalar_tensor_tensor(o, tap, w, o, ALU.mult, ALU.add)
                        if j < TAPS - 1:
                            dve.drain()
                    last.then_inc(s["conv_done"], 1)
                for j in range(3):
                    dve.wait_ge(s["kq_std"], 3 * g + j + 1)
                    dve.reciprocal(gdn_std[:, j, :], gdn_std[:, j, :])
                    dve.drain()
                    if j < 2:
                        dve.tensor_tensor(k_fm[:, j, :], k_fm[:, j, :], gdn_std[:, j, :], ALU.mult).then_inc(s["kq_ready"], 1)
                    else:
                        qf = q_fm.rearrange("p a t -> p (a t)")
                        dve.scalar_tensor_tensor(qf, qf, P ** -0.5, gdn_std[:, j, :], ALU.mult, ALU.mult).then_inc(s["kq_ready"], 1)
                for j in range(GKH):
                    dve.wait_ge(s["kt_done"], GKH * g + j + 1)
                    dve.tensor_copy(k_tm[:, :, j, :], bank[:, 3 + j, :].rearrange("p (t q) -> p t q", t=TILES)).then_inc(s["kt_ready"], 1)
                dve.wait_ge(s["kk_done"], 3 * g + 3)
                for d in range(2):
                    last = dve.tensor_tensor(kq[:, d].rearrange("p t j q -> p (t j) q"), bank[:, 7, :].rearrange("p (n q) -> p n q", n=4),
                                             wide(tri[:, d, :], 4, 1), ALU.mult)
                last.then_inc(s["kqm_ready"], 1)
                dve.wait_ge(s["kk_ready"], 2 * g + 2)
                heads = lambda b: bank[:, b, :].rearrange("p (j q) -> p j q", j=GH)
                for st in range(4):
                    n = 4 * g + st
                    for d in range(2):
                        t = SCAN[d][st]
                        dve.wait_ge(sd["gbc_done"], 2 * (n + 1) + d - 1)
                        for j in range(GH):
                            last = dve.tensor_scalar(E[:, d, j, :], bank[:, 4 * d, j * P:(j + 1) * P], S_GCUM[:, d, t, j:j + 1], 0.0,
                                                     ALU.subtract, ALU.min)
                        last.then_inc(sd["diff_ready"], 1)
                    for d in range(2):
                        t = SCAN[d][st]
                        dve.wait_ge(sd["decay_ready"], 2 * (n + 1) + d - 1)
                        for j in range(GH):
                            last = dve.scalar_tensor_tensor(LT[:, d, j, :], E[:, d, j, :], S_BETA[:, d, t, j:j + 1], kk[:, t, j // 2, :],
                                                            ALU.mult, ALU.mult)
                        last.then_inc(sd["lt_ready"], 1)
                    for d in range(2):
                        dve.wait_ge(sd["ml_ready"], 2 * (LEVELS * n + 1) + d - 1)
                        dve.tensor_tensor(XT[:, d], wide(ident, GH, 1), ML[:, d, 0], ALU.subtract).then_inc(sd["xt0_ready"], 1)
                    if st >= LT_TILES:
                        for d in range(2):
                            t = SCAN[d][st]
                            dve.wait_ge(sd["eg_ready"], 2 * (2 * g + st - 1) + d - 1)
                            pair = "p (a r) q -> p a r q"
                            dve.tensor_tensor(QD[:, d].rearrange(pair, r=2), QD[:, d].rearrange(pair, r=2),
                                              wide(q_fm[:, :, t * P:(t + 1) * P], 2, 2), ALU.mult).then_inc(sd["qd_ready"], 1)
                    for b in range(1, LEVELS):
                        for d in range(2):
                            if b == 1:
                                dve.wait_ge(sd["x0_ready"], 2 * (n + 1) + d - 1)
                            dve.wait_ge(sd["xy_done"], 2 * (6 * n + b) + d - 1)
                            dve.tensor_tensor(X[:, d], X[:, d], heads(4 * d + 1), ALU.subtract).then_inc(sd["xs_ready"], 1)
                    for d in range(2):
                        t = SCAN[d][st]
                        dve.wait_ge(sd["vn_done"], 2 * (n + 1) + d - 1)
                        if st >= LT_TILES:
                            dve.wait_ge(sd["at_ready"], 2 * (2 * g + st - 1) + d - 1)
                        for j in range(GH):
                            last = dve.tensor_scalar(E[:, d, j, :], bank[:, 4 * d + 3, j * P:(j + 1) * P], S_BETA[:, d, t, j:j + 1], None, ALU.mult)
                        last.then_inc(sd["vn_ready"], 1)
                    for d in range(2):
                        t = SCAN[d][st]
                        if st >= LT_TILES:
                            dve.wait_ge(sd["od_done"], 2 * (2 * g + st - 1) + d - 1)
                            o = o_acc[:, :, t * P:(t + 1) * P]
                            if st == LT_TILES:
                                dve.tensor_copy(o, heads(4 * d + 1)).then_inc(sd["od_ready"], 1)
                            else:
                                dve.tensor_tensor(o, o, heads(4 * d + 1), ALU.add).then_inc(sd["od_ready"], 1)
                        if st < 3:
                            dve.wait_ge(sd["su_done"], 2 * (3 * g + st + 1) + d - 1)
                            if st == 0:
                                dve.tensor_copy(state[:, d], heads(4 * d + 3)).then_inc(sd["su_ready"], 1)
                            else:
                                for j in range(GH):
                                    last = dve.scalar_tensor_tensor(state[:, d, j, :], state[:, d, j, :], S_ETOT[:, d, t, j:j + 1],
                                                                    bank[:, 4 * d + 3, j * P:(j + 1) * P], ALU.mult, ALU.add)
                                last.then_inc(sd["su_ready"], 1)
                for half in range(2):
                    two = slice(2 * half, 2 * half + 2)
                    dve.wait_ge(s["oacc_std"], 2 * g + half + 1)
                    dve.reciprocal(gdn_std[:, half, :], gdn_std[:, half, :])
                    dve.drain()
                    dve.scalar_tensor_tensor(o_acc[:, two, :], o_acc[:, two, :], gdn_norm, gdn_std[:, half, :].rearrange("p (a t) -> p a t", a=2),
                                             ALU.mult, ALU.mult)
                dve.drain()
                dve.tensor_tensor(y_all[:, bass.ds(g * GH, GH), :], o_acc, z_s, ALU.mult).then_inc(s["y_ready"], 1)

            def inverse_root(i):
                dve.wait_ge(s["std_ready"], i + 1)
                dve.reciprocal(std[:, 1, 0:SEQ], std[:, 0, 0:SEQ])
                dve.drain()

            def pre_norm(i, j):
                inverse_root(i)
                for k in range(DC):
                    dve.scalar_tensor_tensor(u[:, k, 0:SEQ], h[:, k, 0:SEQ], norm_g[:, j, k:k + 1], std[:, 1, 0:SEQ],
                                             ALU.mult, ALU.mult).then_inc(s["u_ready"], 1)

            def post_norm(i, j, over):
                for m in range(DC):
                    over(dve, m)
                    dve.tensor_copy(yb[:, m, :], bank[:, m, 0:SEQ]).then_inc(s["yb_ready"], 1)
                inverse_root(i)
                for k in range(DC):
                    dve.scalar_tensor_tensor(yb[:, k, :], yb[:, k, :], norm_g[:, j, k:k + 1], std[:, 1, 0:SEQ], ALU.mult, ALU.mult)
                dve.drain()
                for k in range(DC):
                    dve.tensor_tensor(h[:, k, 0:SEQ], h[:, k, 0:SEQ], yb[:, k, :], ALU.add).then_inc(s["x_ready"], 1)
                dve.drain()

            def mixer(l):
                T = SEQ
                two = lambda b: bank[:, b, :].rearrange("p (a t) -> p a t", a=2)
                dve.memset(conv_in[:, :, 0:CONV_W - 1], 0.0)
                dve.wait_ge(s["sig_ready"], l + 1)
                dve.tensor_tensor(conv_in[:, :, CONV_W - 1:], two(2), sig_g, ALU.mult).then_inc(s["conv_u"], 1)
                dve.wait_ge(s["gate_done"], l + 1)
                dve.tensor_scalar(gl_y, bank[:, 6, 0:T], b_gate, None, ALU.add).then_inc(s["gy_ready"], 1)
                dve.drain()
                dve.scalar_tensor_tensor(gl_e, gl_y, -1.0, gl_y, ALU.mult, ALU.min).then_inc(s["ge_ready"], 1)
                for hd in range(SWA_HEADS):
                    dve.wait_ge(s["sw_done"], SWA_HEADS * l + hd + 1)
                    dve.tensor_tensor(swp[:, hd, 0, :], bank[:, hd, 0:P], alibi[:, hd, P:2 * P], ALU.add)
                    dve.tensor_tensor(swp[:, hd, 1:3, :], bank[:, hd, P:3 * P].rearrange("p (a q) -> p a q", a=2),
                                      alibi[:, hd, :].rearrange("p (a q) -> p a q", a=2), ALU.add).then_inc(s["swb_ready"], 1)
                dve.drain()
                dve.tensor_reduce(swm[:, :, 0], swp[:, :, 0, :], AX_X, ALU.max)
                dve.tensor_reduce(swm[:, :, 1], swp[:, :, 1:3, :].rearrange("p h a q -> p h (a q)"), AX_X, ALU.max)
                dve.drain()
                dve.tensor_tensor(swm, swm, wide(sinks, 2, 2), ALU.max)
                dve.drain()
                dve.tensor_scalar(swm, swm, -1.0, None, ALU.mult)
                dve.drain()
                dve.tensor_tensor(swe, swm, wide(sinks, 2, 2), ALU.add).then_inc(s["swm_ready"], 1)
                dve.wait_ge(s["gln_ready"], l + 1)
                dve.scalar_tensor_tensor(gl_y, gl_y, 0.0, gl_e, ALU.min, ALU.subtract)
                dve.drain()
                dve.tensor_tensor_scan(gl_c, gl_y, gl_y, 0.0, ALU.add, ALU.bypass)
                dve.drain()
                for lv in range(8):
                    n = 2 << lv
                    cum = gl_c.rearrange("p (b n) -> p b n", n=n)
                    mid = cum[:, :, n // 2 - 1:n // 2].to_broadcast([P, T // n, n])
                    dve.tensor_tensor(dec[:, lv, :].rearrange("p (b n) -> p b n", n=n), cum, mid, ALU.subtract)
                dve.drain()
                dve.scalar_tensor_tensor(dec, dec, -1.0, dec, ALU.mult, ALU.min).then_inc(s["gabs_ready"], 1)
                for j in range(CONV_W):
                    for b in range(2):
                        tap, w = conv_in[:, b, j:j + T], conv31[:, b, j:j + 1]
                        if j == 0:
                            last = dve.tensor_scalar(conv_y[:, b, :], tap, w, conv_b[:, b:b + 1], ALU.mult, ALU.add)
                        else:
                            last = dve.scalar_tensor_tensor(conv_y[:, b, :], tap, w, conv_y[:, b, :], ALU.mult, ALU.add)
                    if j < CONV_W - 1:
                        dve.drain()
                last.then_inc(s["cvy_ready"], 1)
                dve.wait_ge(s["swe_ready"], l + 1)
                dve.tensor_tensor(sws, sws, swe, ALU.add)
                dve.drain()
                dve.reciprocal(sws, sws)
                dve.drain()
                for hd in range(SWA_HEADS):
                    dve.tensor_scalar(swp[:, hd, 0, :], swp[:, hd, 0, :], sws[:, hd, 0:1], None, ALU.mult)
                    last = dve.tensor_scalar(swp[:, hd, 1:3, :], swp[:, hd, 1:3, :], sws[:, hd, 1:2], None, ALU.mult)
                last.then_inc(s["swp_ready"], 1)
                dve.wait_ge(s["gdec_ready"], l + 1)
                dve.tensor_tensor(qe, dec, wide(gqk[:, 0, :], 8, 1), ALU.mult)
                dve.tensor_tensor(ke, dec, wide(gqk[:, 1, :], 8, 1), ALU.mult).then_inc(s["gqe_ready"], 1)
                for t in range(2):
                    for hd in range(GLA_HEADS):
                        dve.wait_ge(s["gs_done"], 12 * l + 4 * t + hd + 1)
                        for b in range(2):
                            dve.tensor_tensor(att_l[:, hd % 2, 4 * b:4 * b + 4, :], bank[:, 2 * hd + b, :].rearrange("p (v q) -> p v q", v=4),
                                              gmask[:, 4 * b:4 * b + 4, :], ALU.mult)
                        dve.drain()
                        dve.tensor_reduce(att[:, hd, t, :], att_l[:, hd % 2].rearrange("p v q -> p q v"), AX_X, ALU.add).then_inc(s["att_ready"], 1)
                for hd in range(GLA_HEADS):
                    dve.wait_ge(s["gs_done"], 12 * l + 8 + hd + 1)
                    dve.tensor_copy(att[:, hd, 2, :], bank[:, 2 * hd, 0:P]).then_inc(s["att_ready"], 1)
                dve.wait_ge(s["go_done"], l + 1)
                for b in range(2):
                    dve.tensor_copy(og[:, b, :], bank[:, b, 0:T]).then_inc(s["go_ready"], 1)
                dve.wait_ge(s["go_std"], l + 1)
                dve.reciprocal(std[:, 1, :], std[:, 0, :])
                dve.drain()
                for b in range(2):
                    dve.scalar_tensor_tensor(og[:, b, :], og[:, b, :], gla_norm[:, b:b + 1], std[:, 1, b * T:(b + 1) * T], ALU.mult, ALU.mult)
                dve.drain()
                dve.tensor_tensor(mix[:, 0:2, :], og, gr_s, ALU.mult).then_inc(s["gla_ready"], 1)
                dve.wait_ge(s["cv_mean"], l + 1)
                for b in range(2):
                    last = dve.scalar_tensor_tensor(conv_y[:, b, :], bank[:, 1, 0:T], -1.0 / (2 * P), conv_y[:, b, :], ALU.mult, ALU.add)
                last.then_inc(s["cv_cent"], 1)
                dve.wait_ge(s["cv_std"], l + 1)
                dve.reciprocal(gl_y, gl_e)
                dve.drain()
                for b in range(2):
                    last = dve.scalar_tensor_tensor(conv_y[:, b, :], conv_y[:, b, :], conv_ln_g[:, b:b + 1], gl_y, ALU.mult, ALU.mult)
                last.then_inc(s["cv_norm"], 1)

            def over_down(name, layer=0):
                return lambda e, m: panel_over(e, name, m % SLOTS, m // SLOTS, layer)

            modulation(0)
            modulate(0, 1, TOK)
            mla()
            layer_norm(0, 0, TOK)
            modulate(3, 4, TOK, 0)
            ffn(0, TOK)
            layer_norm(1, 0, TOK)
            modulation(1)
            modulate(0, 1, TOK, 1)
            gdn_gates()
            with dve.Fori(0, GROUPS) as g:
                gdn_group(g)
            layer_norm(2, 1, SEQ)
            modulate(3, 4, SEQ, 2)
            ffn(1, SEQ)
            layer_norm(3, 1, SEQ)
            dve.wait_ge(s["h_ready"], 4 * DC)
            dve.sem_inc(s["x_ready"], DC)
            with dve.Fori(0, DEPTH) as l:
                dve.wait_ge(lpar_loaded, 16 * l + 16)
                pre_norm(6 * l, 0)
                ffn(2 * l + 2, SEQ)
                post_norm(6 * l + 1, 1, over_down("downA", l))
                pre_norm(6 * l + 2, 2)
                mixer(l)
                post_norm(6 * l + 3, 3, lambda e, m: mix_out_over(e, m, l))
                pre_norm(6 * l + 4, 4)
                ffn(2 * l + 3, SEQ)
                post_norm(6 * l + 5, 5, over_down("downB", l))
                dve.sem_inc(s["layer_done"], 1)


def chunks(w):
    k, n = w.shape
    return w.reshape(k // P, P, n).transpose(1, 0, 2)


def vec(v):
    v = v.reshape(-1, P)
    return v.T


def constants():
    t = np.arange(P)
    c = {"ones": np.ones((P, P)), "ident": np.eye(P), "ones64": (t[:, None] // 64 == t[None, :] // 64) * 1.0}
    c["tri"] = np.concatenate([t[:, None] <= t[None, :], t[:, None] >= t[None, :]], 1) * 1.0
    levels = []
    for d in range(2):
        for b in range(LEVELS):
            same = t[:, None] >> (b + 1) == t[None, :] >> (b + 1)
            first, second = (t >> b) % 2 == 0, (t >> b) % 2 == 1
            levels.append((same & first[:, None] & second[None, :]) if d == 0 else (same & second[:, None] & first[None, :]))
    c["level"] = np.concatenate(levels, 1) * 1.0
    f32 = np.float32
    tok = np.arange(SEQ)
    n_freq = ROPE // 4
    inv = f32(ROPE_THETA) ** (-(f32(2.0) * np.arange(n_freq, dtype=f32)) / f32(ROPE // 2))
    ang = np.stack([(tok // GRID_W).astype(f32)[:, None] * inv, (tok % GRID_W).astype(f32)[:, None] * inv], 1)
    cos, sin = np.cos(ang), np.sin(ang)
    f = np.arange(P) % ROPE
    axis, half, i = f // 32, f // 16 % 2, f % 16
    c["rope_cos"] = cos[:, axis, i].T
    c["rope_sin"] = (sin[:, axis, i] * np.where(half == 0, -1, 1)).T
    slopes = np.exp2(-8.0 * (np.arange(SWA_HEADS) + 1.0) / SWA_HEADS)
    dist = t[:, None] - np.arange(2 * P)[None, :] + P
    valid = (dist >= 0) & (dist < P)
    c["alibi"] = np.concatenate([np.where(valid, -sl * dist, NEG) for sl in slopes], 1)
    return np.ascontiguousarray(np.concatenate([c[n] for n, _ in CONSTS], 1), np.float32)


def panel(blocks):
    w = np.concatenate(blocks, 2).reshape(P, -1)
    assert w.shape[1] == PANEL, w.shape
    return w


def ffn_panels(gate, up):
    g, v = chunks(gate), chunks(up)
    col = lambda w, b: w[:, :, b * P:(b + 1) * P]
    return [panel([col(g, 2 * p), col(v, 2 * p), col(g, 2 * p + 1), col(v, 2 * p + 1)]) for p in range(FC // 2)]


def down_panels(w):
    w = chunks(w)
    return [w[:, :, m * P:(m + 1) * P].reshape(P, -1) for m in range(DC)]


def wide_panels(w, n):
    w = chunks(w)
    return [panel([w[:, :, a:a + n]]) for a in range(0, w.shape[2], n)]


def layout(a):
    tokens = np.concatenate([a["x"][0], a["ctx"][0]], 0)
    h_in = np.ascontiguousarray(tokens.T.reshape(DC, P, TOK).transpose(1, 0, 2))

    spread = lambda v: np.broadcast_to(v.reshape(1, -1), (P, v.size))
    conv = a["gdn_conv"][0]
    def taps(g):
        heads = [2 * g, 2 * g + 1]
        starts = [D + hd * P for hd in heads] + [hd * P for hd in heads] + [2 * D + (GH * g + j) * P for j in range(GH)]
        return np.concatenate([conv[:, st:st + P].T for st in starts], 1)
    pieces = {
        "b_mod": vec(a["b_mod"]), "ln1_g": vec(a["ln1_g"]), "ln1_b": vec(a["ln1_b"]), "ln2_g": vec(a["ln2_g"]),
        "ln2_b": vec(a["ln2_b"]), "q_norm": vec(a["mla_q_norm"]), "kv_norm": vec(a["mla_kv_norm"]),
        "conv5": np.concatenate([taps(g) for g in range(GROUPS)], 1), "gdn_norm": vec(a["gdn_norm"]),
        "a_log": spread(a["gdn_a_log"]), "dt_bias": spread(a["gdn_dt_bias"]),
        "w_ba": chunks(a["gdn_w_in"][0][:, 4 * D + GDN_VW:]).reshape(P, -1),
        "cvec": np.stack([vec(a["c"]), vec(a["c_ctx"])], 2).reshape(P, -1),
        "eps": spread(np.array([RMS_EPS, LN_EPS, 4 * RMS_EPS, 1.0], np.float32)),
    }
    params = np.ascontiguousarray(np.concatenate([pieces[n] for n, _ in PARAMS], 1))
    lparams = []
    for l in range(DEPTH):
        rank = a["gla_w_gate2_2"][l]
        cw = a["conv_w_2"][l].T.reshape(2, P, CONV_W).transpose(1, 0, 2).reshape(P, -1)
        q = {
            "norm_g": vec(a["norm_g_2"][l]), "glr": chunks(a["w_in_2"][l][:, 768:768 + GLA_RANK]).reshape(P, -1),
            "gate2": np.concatenate([rank, np.zeros((P - GLA_RANK, P), rank.dtype)], 0), "b_gate": vec(a["gla_b_gate_2"][l]),
            "gla_norm": vec(a["gla_norm_g_2"][l]), "conv31": cw, "conv_b": vec(a["conv_b_2"][l]),
            "conv_ln_g": vec(a["conv_ln_g_2"][l]), "conv_ln_b": vec(a["conv_ln_b_2"][l]), "sinks": spread(a["swa_sinks_2"][l]),
        }
        lparams.append(np.concatenate([q[n] for n, _ in LPARAMS], 1))
    lparams = np.ascontiguousarray(np.stack(lparams))

    rows = {True: [], False: []}
    def add(name, more):
        rows[name.startswith("down")] += more
    swap = np.arange(ROPE).reshape(2, 2, 16)[:, ::-1].reshape(-1)
    w_in = chunks(a["mla_w_in"][0])
    kr = w_in[:, :, Q_RANK + KV_RANK:]
    krs = kr[:, :, swap]
    q_up = chunks(a["mla_w_q_up"][0]).reshape(P, QC, HEADS, NOPE + ROPE)
    q_rope = q_up[..., NOPE:]
    kv_up = chunks(a["mla_w_kv_up"][0]).reshape(P, KC, HEADS, NOPE + VDIM)
    flat = lambda w: w.reshape(w.shape[0], w.shape[1], -1)
    add("mod0", wide_panels(a["w_mod"][0], 512))
    add("mla", [panel([w_in[:, :, 0:512]]), panel([w_in[:, :, 512:Q_RANK + KV_RANK], kr, kr, krs, krs]),
                panel([flat(q_up[..., :NOPE])]), panel([flat(q_rope), flat(q_rope[..., swap])]),
                panel([flat(kv_up[..., :NOPE]), flat(kv_up[..., NOPE:])])] + wide_panels(a["mla_w_out"][0], 512))
    for l in range(DEPTH):
        w = a["w_ffn_in"][l]
        if l == 1:
            add("mod1", wide_panels(a["w_mod"][1], 512))
            gw = chunks(a["gdn_w_in"][0])
            for g in range(GROUPS):
                two = lambda at: gw[:, :, at + 2 * P * g:at + 2 * P * g + 2 * P]
                four = lambda at: gw[:, :, at + 4 * P * g:at + 4 * P * g + 4 * P]
                add("gdn", [panel([two(D), two(0)]), panel([four(2 * D)]), panel([four(4 * D)])])
            add("gdn_out", wide_panels(a["gdn_w_out"][0], 2 * P))
        add(f"ffn{l}", ffn_panels(w[:, :D_FF], w[:, D_FF:]))
        add(f"down{l}", down_panels(a["w_ffn_out"][l]))
    for l in range(DEPTH):
        w = chunks(a["w_in_2"][l])
        swq = w[:, :, 1296:1808].reshape(P, DC, 2, 4, SWA_DH).transpose(0, 1, 3, 2, 4).reshape(P, DC, 512)
        wo = a["w_out_2"][l]
        wo = np.concatenate([wo[:512], wo[512:].reshape(2, 4, SWA_DH, D).transpose(1, 0, 2, 3).reshape(512, D)], 0)
        add("ffnA", ffn_panels(a["ffn_w_gate_2"][l, 0], a["ffn_w_up_2"][l, 0]))
        add("downA", down_panels(a["ffn_w_down_2"][l, 0]))
        add("mix_in", [panel([w[:, :, 0:256], w[:, :, 512:768]]), panel([w[:, :, 784:1296]]), panel([swq]),
                       panel([w[:, :, 1808:1936], w[:, :, 256:512], w[:, :, 1936:2064]])])
        add("mix_out", wide_panels(wo, 512))
        add("ffnB", ffn_panels(a["ffn_w_gate_2"][l, 1], a["ffn_w_up_2"][l, 1]))
        add("downB", down_panels(a["ffn_w_down_2"][l, 1]))
    panels, downs = np.stack(rows[False]), np.stack(rows[True])

    return {"h_in": h_in, "params": params, "lparams": lparams, "consts": constants(), "panels": panels, "downs": downs}


def kernel(**inputs):
    import concourse.bacc as bacc
    from concourse.bass_utils import run_bass_kernel_spmd

    arrays = layout({k: np.asarray(v) for k, v in inputs.items()})
    nc = bacc.Bacc("TRN2", target_bir_lowering=False, num_devices=1)
    args = [nc.dram_tensor(n, v.shape, F32, kind="ExternalInput").ap() for n, v in arrays.items()]
    args.append(nc.dram_tensor("out", (P, DC, SEQ), F32, kind="ExternalOutput").ap())
    build(nc, *args)
    r = run_bass_kernel_spmd(nc, [arrays], core_ids=[0])
    got = r.results[0]["out"]
    return np.ascontiguousarray(got.transpose(2, 1, 0).reshape(1, SEQ, D))
```

```python
from contextlib import ExitStack

import numpy as np

import concourse.bass as bass
from concourse import mybir

F32 = mybir.dt.float32
F32R = mybir.dt.float32r
ACT = mybir.ActivationFunctionType
ALU = mybir.AluOpType
AX_X = mybir.AxisListType.X

P = 128
D = 1024
DC = D // P
SEQ = 256
CTX = 256
TOK = SEQ + CTX
DEPTH = 2
GRID_W = 64
ALPHA = (2.0 * DEPTH) ** 0.25
LN_EPS = 1e-5
RMS_EPS = 1e-6
N_MOD = 6
MB = N_MOD * DC

HEADS = 8
Q_RANK, KV_RANK = 512, 256
QC, KC = Q_RANK // P, KV_RANK // P
NOPE, ROPE, VDIM = 128, 64, 128
MLA_SCALE = (NOPE + ROPE) ** -0.5
ROPE_THETA = 10000.0

GK_HEADS, GV_HEADS = 8, 16
GROUPS = 4
GH = GV_HEADS // GROUPS
GKH = GK_HEADS // GROUPS
TAPS = 5
TILES = TOK // P
LT_TILES = SEQ // P
LEVELS = 7
GDN_VW = GV_HEADS * P

D_FF = 2816
FC = D_FF // P
PANEL = 4096
SLOTS = 3
PAIR = DC * 2 * P
HALF = FC // 2 * P
PARTS = FC + 2 * DC
HALVES = FC // 2 + DC

GLA_HEADS, GLA_DK, GLA_DV, GLA_RANK, GLA_TAU = 4, 32, 64, 16, 16.0
CONV_W = 31
SWA_HEADS, SWA_KV, SWA_DH = 8, 2, 64
NEG = -1e30

SCAN = [[2, 3, 0, 1], [3, 2, 1, 0]]

PARAMS = [("b_mod", DEPTH * MB), ("ln1_g", DEPTH * DC), ("ln1_b", DEPTH * DC), ("ln2_g", DEPTH * DC),
          ("ln2_b", DEPTH * DC), ("q_norm", QC), ("kv_norm", KC), ("conv5", GROUPS * 8 * TAPS),
          ("gdn_norm", 1), ("a_log", 32), ("dt_bias", 32), ("w_ba", DC * 64), ("cvec", DC * 2), ("eps", 4)]
LPARAMS = [("norm_g", 6 * DC), ("glr", DC * GLA_RANK), ("gate2", P), ("b_gate", 1), ("gla_norm", 2),
           ("conv31", 2 * CONV_W), ("conv_b", 2), ("conv_ln_g", 2), ("conv_ln_b", 2), ("sinks", SWA_HEADS)]
CONSTS = [("ones", P), ("ones64", P), ("tri", 2 * P), ("ident", P), ("level", 2 * LEVELS * P),
          ("rope_cos", SEQ), ("rope_sin", SEQ)]


def columns(table):
    at, out = 0, {}
    for name, n in table:
        out[name] = (at, n)
        at += n
    return out, at


PCOL, NPAR = columns(PARAMS)
LCOL, NLPAR = columns(LPARAMS)
CCOL, NCONST = columns(CONSTS)

SECTIONS = [("mod0", 10), ("mla", 7), ("mod0b", 2), ("ffn0", 11), ("down0", 8), ("mod1", 3),
            ("ffn0c", 11), ("down0c", 8), ("mod1b", 9), ("gdn", 12), ("gdn_out", 4),
            ("ffn1", 11), ("down1", 8)]
AGAIN = {"ffn0c": "ffn0", "down0c": "down0"}
START = {"mod0": 2, "mod0b": 1, "down0": 2, "mod1": 1, "ffn0c": 1, "mod1b": 2, "ffn1": 1, "downA": 2, "ffnB": 2, "downB": 1}
LAYER = [("ffnA", 11), ("downA", 8), ("mix_in", 4), ("mix_out", 2), ("ffnB", 11), ("downB", 8)]


class Plan:

    def __init__(self):
        self.base, self.first = {}, {}
        used = [0] * SLOTS
        at = {True: 0, False: 0}
        for name, n in SECTIONS:
            self._add(name, n, used, at)
        self.start = list(used)
        self.layer_first = dict(at)
        for name, n in LAYER:
            self._add(name, n, used, at)
        self.per_layer = [b - a for a, b in zip(self.start, used)]
        self.layer_panels = {k: at[k] - self.layer_first[k] for k in at}
        self.total = {k: self.layer_first[k] + DEPTH * self.layer_panels[k] for k in at}

    def _add(self, name, n, used, at):
        down = name.startswith("down")
        self.base[name], self.first[name] = list(used), self.first[AGAIN[name]] if name in AGAIN else at[down]
        for p in range(n):
            used[self.slot(name, p)] += 1
        if name not in AGAIN:
            at[down] += n

    def slot(self, name, p):
        return (START.get(name, 0) + p) % SLOTS

    def uses(self, name, p, turn, layer=0):
        slot = self.slot(name, p)
        more = self.per_layer[slot] * layer if name in dict(LAYER) else 0
        return self.base[name][slot] + turn + more

    def panel(self, name, p, layer=0):
        down = name.startswith("down")
        more = self.layer_panels[down] * layer if name in dict(LAYER) else 0
        return self.first[name] + p + more


PLAN = Plan()

MLA_Q = QC + KC + 2 - 2
MLA_K = MLA_Q + HEADS - 1
MLA_V = MLA_K + HEADS
BLOCKS = 12
SPLITS = DC // 2 + BLOCKS
U_GDN, U_FFN1, U_BLOCK2 = 3 * DC, 4 * DC, 5 * DC
NORMS = 5


def U_MIX(l):
    return U_BLOCK2 + 3 * DC * l + DC



def build(nc, h_in, params, lparams, consts, slopes, panels, downs, out):
    ctx = ExitStack()
    with ctx:
        def sb(name, shape):
            return ctx.enter_context(nc.sbuf_tensor(name, shape, F32))

        def sem(name):
            return ctx.enter_context(nc.semaphore(name))

        bank = ctx.enter_context(nc.psum_tensor("bank", [P, 8, 512], F32))

        with nc.sbuf_tensor("ring", [P, SLOTS, PANEL], F32) as ring:
            pass
        ring_lo = sb("ring_lo", [P, SLOTS, PANEL])
        h = sb("h", [P, DC, TOK])
        par = sb("par", [P, NPAR])
        lpar = sb("lpar", [P, NLPAR])
        with nc.sbuf_tensor("alibi", [P, SWA_HEADS, 2 * P], F32) as alibi:
            pass
        gw_parts = sb("gw_parts", [P, SWA_HEADS * 2 * P])
        warm = sb("warm", [P, 1])
        con = sb("con", [P, NCONST])
        cond = sb("cond", [P, DC, 2])
        mod = sb("mod", [P, MB, 2])
        with nc.sbuf_tensor("std", [P, 2, TOK], F32) as std:
            pass
        gw_parts2 = sb("gw_parts2", [P, 2 * TOK])
        with nc.sbuf_tensor("u", [P, DC, TOK], F32) as u:
            pass
        u_parts = sb("u_parts", [P, DC, 2, SEQ])
        ARENA = 25272
        with nc.sbuf_tensor("arena", [P, ARENA], F32) as arena:
            pass
        with nc.sbuf_tensor("gdn_parts", [P, ARENA], F32) as gdn_parts:
            pass
        gated = sb("gated", [P, 2, 3, SEQ])
        with nc.sbuf_tensor("tokens", [P, DC, SEQ], F32) as tokens:
            pass
        ffn_arena = sb("ffn_arena", [P, ARENA - 6 * SEQ])

        class Carve:

            def __init__(self, at=0, mem=None):
                self.at, self.mem = at, arena if mem is None else mem

            def __call__(self, *shape):
                n = int(np.prod(shape))
                v = self.mem[:, self.at:self.at + n]
                self.at += n
                assert self.at <= self.mem.shape[1], self.at
                names = "abcd"[:len(shape)]
                if len(shape) == 1:
                    return v
                return v.rearrange(f"p ({' '.join(names)}) -> p {' '.join(names)}", **dict(zip(names, shape)))

        def param(name, *shape):
            a, n = PCOL[name]
            return cut(par, a, n, shape)

        def lparam(name, *shape):
            a, n = LCOL[name]
            return cut(lpar, a, n, shape)

        def const(name, *shape):
            a, n = CCOL[name]
            return cut(con, a, n, shape)

        def cut(t, a, n, shape):
            v = t[:, a:a + n]
            if len(shape) < 2:
                return v
            names = "abcd"[:len(shape)]
            return v.rearrange(f"p ({' '.join(names)}) -> p {' '.join(names)}", **dict(zip(names, shape)))

        def wide(ap, n, at):
            shape = list(ap.shape)
            return ap.unsqueeze(at).to_broadcast(shape[:at] + [n] + shape[at:])

        ones, ident, ones64 = const("ones"), const("ident"), const("ones64")
        tri = const("tri", 2, P)
        level = const("level", 2, LEVELS, P)
        rope_cos, rope_sin = const("rope_cos"), const("rope_sin")
        b_mod = param("b_mod", DEPTH, MB)
        ln_g = [param("ln1_g", DEPTH, DC), param("ln2_g", DEPTH, DC)]
        ln_b = [param("ln1_b", DEPTH, DC), param("ln2_b", DEPTH, DC)]
        q_norm, kv_norm = param("q_norm"), param("kv_norm")
        conv5 = param("conv5", GROUPS, 8 * TAPS)
        gdn_norm = param("gdn_norm")
        a_log, dt_bias = param("a_log"), param("dt_bias")
        w_ba = param("w_ba", DC, 64)
        cvec = param("cvec", DC, 2)
        eps = param("eps")
        norm_g = lparam("norm_g", 6, DC)
        w_glr = lparam("glr", DC, GLA_RANK)
        gate2 = lparam("gate2")
        b_gate, gla_norm = lparam("b_gate"), lparam("gla_norm")
        conv31 = lparam("conv31", 2, CONV_W)
        conv_b, conv_ln_g, conv_ln_b = lparam("conv_b"), lparam("conv_ln_g"), lparam("conv_ln_b")
        sinks = lparam("sinks")
        EPS_RMS, EPS_LN, EPS_RMS4, ONE = (eps[:, i:i + 1] for i in range(4))

        c = Carve()
        lat = c(QC + KC, TOK)
        krope = c(TOK)
        rope_t = c(2, SEQ)
        q_n, k_n = c(HEADS, TOK), c(HEADS, TOK)
        q_r = c(HEADS // 2, TOK)
        v_tm = c(TILES, HEADS * VDIM)
        probs = c(2, 3, 512)
        probs_t = c(TILES, SEQ)
        probs_tc = c(CTX // P, CTX)
        negmax, rowsum = c(2, 4), c(2, 4)
        lat_sq = q_n
        mod_rows = Carve()(N_MOD * D)[0:2]
        early_rows = alibi.rearrange("p h q -> p (h q)")[0:2]

        def rows_at(l, a, n):
            return (early_rows if l and a < 3 * 512 else mod_rows)[:, a:a + n]

        c = Carve(mem=ffn_arena)
        hidden = c(FC, 2, SEQ)
        silu_g, whole = gated[:, 0], gated[:, 1]
        w_hi, w_lo = c(3, PAIR), c(3, PAIR)
        sq, yb, sq2 = u, u[:, :, 0:SEQ], u[:, :, SEQ:TOK]

        def r(ap):
            return ap.bitcast(F32R)

        c = Carve()
        k_fm, q_fm, v_fm = c(GKH, TOK), c(GKH, SEQ), c(GH, TOK)
        parts_at = [c.at]
        k_tm, gv_tm = c(TILES, GKH, P), c(TILES, GH, P)
        state = c(2, GH, P)
        kq = c(2, LT_TILES, GKH, P)
        gdn_sq = Carve(c.at)(4, TOK)
        soft = Carve(c.at)(2, 2, TILES, GV_HEADS)
        X, XT = c(2, GH, P), c(2, GH, P)
        gdn_std = Carve(c.at)(4, TOK)
        R, KD = c(2, GH, P), c(2, GH, P)
        parts_at.append(c.at)
        Y, E, LT, QD, AT = (c(2, GH, P) for _ in range(5))
        G, V = (Carve(2 * GH * P * i, alibi.rearrange("p h q -> p (h q)"))(2, GH, P) for i in range(2))
        QDS = [QD, Carve(0, std.rearrange("p a t -> p (a t)"))(2, GH, P)]
        cin = Carve(c.at)(2, 2, SEQ + TAPS - 1)
        ML = c(2, 2, GH, P)
        parts = [Carve(at, gdn_parts) for at in parts_at]
        gu_hi, gu_lo = (p(DC, TOK) for p in parts)
        gw_hi = [p(DC, P) for p in parts + [Carve(2 * GH * P, gw_parts), Carve(0, gw_parts2)]]
        assert all(p.at <= at + 5 * 2 * GH * P for p, at in zip(parts, parts_at))
        y_all = c(GV_HEADS, SEQ)
        gates = c(6, 2, TILES, GV_HEADS)
        gst = c(6, 2, TILES, GH)
        cst = c(8 * TAPS)
        kk = v_fm.rearrange("p a b -> p (a b)")[:, 0:TILES * GKH * P].rearrange("p (t j q) -> p t j q", t=TILES, j=GKH)
        o_acc, z_s = h[:, 0:GH, SEQ:TOK], h[:, GH:2 * GH, SEQ:TOK]
        BETA, G_, GCUM, EG, ED, ETOT = (gates[:, i] for i in range(6))
        S_BETA, S_G, S_GCUM, S_EG, S_ED, S_ETOT = (gst[:, i] for i in range(6))
        c = Carve()
        dec, qe, ke = c(8, SEQ), c(8, SEQ), c(8, SEQ)
        swp, swt = c(SWA_HEADS, 3, P), c(SWA_HEADS, 3, P)
        att = c(GLA_HEADS, 3, P)
        att_l = c(2, 8, P)
        gqk, gr_s, sig_g = c(2, SEQ), c(2, SEQ), c(2, SEQ)
        conv_in = c(2, SEQ + CONV_W - 1)
        conv_y, cv_sq = c(2, SEQ), c(2, SEQ)
        s_q, s_k = c(4, SEQ), c(SEQ)
        g_v, s_v = c(2, GLA_HEADS * GLA_DV), c(2, SWA_KV * SWA_DH)
        glr_s, gl_y, gl_e, gl_c = c(SEQ), c(SEQ), c(SEQ), c(SEQ)
        og, og_sq = c(2, SEQ), c(2, SEQ)
        mix = c(DC, SEQ)
        swm, sws, swe = c(SWA_HEADS, 2), c(SWA_HEADS, 2), c(SWA_HEADS, 2)
        gmask = con[:, CCOL["ident"][0]:CCOL["ident"][0] + 8 * P].rearrange("p (l q) -> p l q", l=8)

        VT_BANK = [1, 2, 0, 6]

        par_loaded, in_loaded, lpar_loaded, alibi_loaded, out_stored = (
            sem(n) for n in ("par_loaded", "in_loaded", "lpar_loaded", "alibi_loaded", "out_stored"))
        slot_loaded = [sem(f"slot_loaded{s}") for s in range(SLOTS)]
        panel_done = [sem(f"panel_done{s}") for s in range(SLOTS)]
        names = """cond_ready mod_ready u_ready mla_done mla_copied lat_copied lat_squared lat_ssq lat_std latn_ready mod_copied rows_turned hi_ready lo_ready hid_hi hid_ready whole_ready uhi_ready krope_ready
            qr_ready s_done max_ready exp_done p_ready pt_done
            pt_lat pt_ctx pv_done o_ready r_ready mean_done cent_ready cent_sq var_done var_std norm_ready
            h_ready pair_done silu_ready pair_free
            yproj gate_sums ax_ready gate_acts g_ready gcum_ready gexp_ready gst_ready
            parts_split parts_lo odd_lo
            proj_done cin_ready conv_done act_ready kq_sq kq_ssq kq_std kq_ready z_ready vt_done vt_ready kt_done
            kt_ready kk_done kk_ready kqm_ready oacc_sq oacc_ssq oacc_std y_ready
            yb_ready sq_ready ssq_done std_ready x_ready layer_done
            mixp_done gqk_ready gr_ready conv_u sig_ready swq_ready gv_ready glr_done glr_ready gate_done gy_ready
            ge_ready gln_ready gabs_ready gdec_ready gqe_ready gs_done att_ready go_done go_ready
            go_sq go_ssq go_std gla_ready cvy_ready cv_mean cv_cent cv_sq_ready cv_var cv_std cv_norm cv_ready
            sw_done swb_ready swm_ready swe_ready swp_ready swt_done swt_ready swo_done swo_ready""".split()
        s = {n: sem(n) for n in names}
        per_dir = """gtri_ready gbc_done diff_ready decay_ready eg_ready lt_ready ml_ready xt0_ready x0_done x0_ready
            y_done yc_ready xy_done xs_ready xt_done xt_ready kd_ready ks_done rest_ready vn_done vn_ready qd_ready
            at_ready od_done od_ready su_done su_ready""".split()
        sd = {n: sem(n) for n in per_dir}

        block = ctx.enter_context(nc.Block())

        def load_done(e, name, slot, turn, layer=0):
            e.wait_ge(slot_loaded[PLAN.slot(name, slot)], 16 * PLAN.uses(name, slot, turn, layer) + 16)

        def panel_over(e, name, slot, turn, layer=0):
            e.wait_ge(panel_done[PLAN.slot(name, slot)], PLAN.uses(name, slot, turn, layer) + 2)

        def mla_out_over(e, m):
            if m % 4 == 3:
                panel_over(e, "mla", 2 if m < 4 else 0, 1 if m < 4 else 2)
            else:
                e.wait_ge(s["yproj"], m + 1 - m // 4)

        def gdn_out_over(e, m):
            if m % 2:
                panel_over(e, "gdn_out", m // 2 % SLOTS, m // 2 // SLOTS)
            else:
                e.wait_ge(s["yproj"], 6 + m // 2 + 1)

        def mix_out_over(e, m, l):
            if m % 4 == 3:
                panel_over(e, "mix_out", m // 4, 0, l)
            else:
                e.wait_ge(s["yproj"], 10 + 6 * l + m + 1 - m // 4)

        @block.sync
        def _(sp):
            sp.dma_start(par[:], params).then_inc(par_loaded, 16)

            def load(name, slot, turn, layer=0):
                sp.wait_ge(panel_done[PLAN.slot(name, slot)], PLAN.uses(name, slot, turn, layer) + 1)
                at = PLAN.panel(name, turn * SLOTS + slot, layer)
                slot = PLAN.slot(name, slot)
                if name.startswith("down"):
                    sp.dma_start(ring[:, slot, 0:FC * P], downs[at]).then_inc(slot_loaded[slot], 16)
                else:
                    sp.dma_start(ring[:, slot, :], panels[at]).then_inc(slot_loaded[slot], 16)

            def section(name, layer=0):
                n = dict(SECTIONS + LAYER)[name]
                if n >= 2 * SLOTS:
                    with sp.Fori(0, n // SLOTS) as i:
                        for slot in range(SLOTS):
                            load(name, slot, i, layer)
                else:
                    for p in range(n // SLOTS * SLOTS):
                        load(name, p % SLOTS, p // SLOTS, layer)
                for p in range(n // SLOTS * SLOTS, n):
                    load(name, p % SLOTS, p // SLOTS, layer)

            for p in range(SLOTS):
                load("mod0", p, 0)
            sp.dma_start(con[:], consts).then_inc(in_loaded, 16)
            sp.dma_start(h[:], h_in).then_inc(in_loaded, 16)
            with sp.Fori(1, 3) as i:
                for p in range(SLOTS):
                    load("mod0", p, i)
            load("mod0", 0, 3)
            for name, _ in SECTIONS[1:]:
                section(name)
            sp.wait_ge(s["layer_done"], 1)
            sp.dma_start(alibi[:], slopes).then_inc(alibi_loaded, 16)
            with sp.Fori(0, DEPTH) as l:
                sp.wait_ge(s["layer_done"], l + 1)
                sp.dma_start(lpar[:], lparams[l]).then_inc(lpar_loaded, 16)
                for name, _ in LAYER:
                    section(name, l)
            sp.wait_ge(s["layer_done"], DEPTH + 1)
            sp.dma_start(out, h[:, :, 0:SEQ]).then_inc(out_stored, 16)
            sp.wait_ge(out_stored, 16)

        @block.tensor
        def _(pe):
            def mm(o, w, x, first, last):
                return pe.matmul(o, w, x, start=first, stop=last)

            def slot_view(slot, k, n):
                return ring[:, slot, 0:k * n].rearrange("p (k n) -> p k n", k=k)

            for q in panel_done:
                pe.sem_inc(q, 1)

            def modulation(l, name, first, panels):
                for i in panels:
                    slot = i % SLOTS
                    if i >= SLOTS:
                        pe.wait_ge(s["mod_copied"], 12 * l + first + i - SLOTS + 1)
                    load_done(pe, name, slot, i // SLOTS)
                    w = slot_view(PLAN.slot(name, slot), DC, 512)
                    for k in range(DC):
                        last = mm(bank[0:2, 3 + slot, :], cond[:, k, :], w[:, k, :], k == 0, k == DC - 1)
                    last.then_inc(panel_done[PLAN.slot(name, slot)], 1)

            def turn_rows(l, a, b):
                pe.wait_ge(s["mod_copied"], 12 * l + b // 4)
                for m in range(a, b):
                    last = pe.transpose(bank[:, 7, 2 * m:2 * m + 2], rows_at(l, m * P, P), ident[0:2, 0:2])
                last.then_inc(s["rows_turned"], 1)

            def mla():
                for p in range(2):
                    load_done(pe, "mla", p, 0)
                    w = slot_view(p, DC, 512)
                    for j in range(4):
                        for k in range(DC):
                            if p == 0 and j == 0:
                                pe.wait_ge(s["u_ready"], k + 1)
                            last = mm(bank[:, 4 * p + j, :], w[:, k, j * P:(j + 1) * P], u[:, k, :], k == 0, k == DC - 1)
                        last.then_inc(s["mla_done"] if j < 3 else panel_done[p], 1)
                for b, (a, n) in enumerate([(0, QC), (QC, KC)]):
                    for k in range(n):
                        pe.wait_ge(s["lat_squared"], a + k + 1)
                        last = mm(bank[:, b, :], ones, lat_sq[:, a + k, :], k == 0, k == n - 1)
                    last.then_inc(s["lat_ssq"], 1)
                load_done(pe, "mla", 2, 0)
                w = slot_view(2, QC, HEADS * NOPE)
                pe.wait_ge(s["latn_ready"], QC)
                pe.wait_ge(s["lat_std"], 2)
                pe.wait_ge(s["krope_ready"], 1)
                for j in range(HEADS):
                    for k in range(QC):
                        last = mm(bank[:, j, :], w[:, k, j * P:(j + 1) * P], lat[:, k, :], k == 0, k == QC - 1)
                    last.then_inc(s["mla_done"] if j < HEADS - 1 else panel_done[2], 1)
                load_done(pe, "mla", 0, 1)
                w = slot_view(0, QC, 2 * HEADS * ROPE)
                for j in range(HEADS):
                    pe.wait_ge(s["mla_copied"], j + 1)
                    for k in range(QC):
                        last = mm(bank[:, j, :], w[:, k, j * P:(j + 1) * P], lat[:, k, :], k == 0, k == QC - 1)
                last.then_inc(panel_done[0], 1)
                load_done(pe, "mla", 1, 1)
                w = slot_view(1, KC, 2 * HEADS * P)
                pe.wait_ge(s["latn_ready"], QC + KC)
                for j in range(HEADS):
                    if j < HEADS // 2:
                        pe.wait_ge(s["qr_ready"], j + 1)
                    for k in range(KC):
                        last = mm(bank[:, j, :], w[:, k, j * P:(j + 1) * P], lat[:, QC + k, :], k == 0, k == KC - 1)
                    last.then_inc(s["mla_done"], 1)
                for t in range(TILES):
                    for half in range(2):
                        n = 2 * t + half
                        pe.wait_ge(s["mla_copied"], HEADS + n + 1)
                        for k in range(KC):
                            a = HEADS * P + 512 * half
                            last = mm(bank[:, n, :], lat[:, QC + k, t * P:(t + 1) * P], w[:, k, a:a + 512],
                                      k == 0, k == KC - 1)
                        last.then_inc(s["mla_done"] if n < 7 else panel_done[1], 1)
                pe.wait_ge(s["mla_copied"], 3 * HEADS)

                def scores(hd):
                    r = slice(64 * (hd % 2), 64 * (hd % 2) + 64)
                    if hd:
                        pe.wait_ge(s["exp_done"], hd)
                    for t in range(LT_TILES):
                        cols = slice(t * P, (t + 1) * P)
                        mm(bank[:, t, :], q_n[:, hd, cols], k_n[:, hd, :], True, False)
                        last = mm(bank[:, t, :], q_r[r, hd // 2, cols], krope[r, :], False, True)
                    last.then_inc(s["s_done"], 1)
                    for t in range(CTX // P):
                        cols = slice(SEQ + t * P, SEQ + (t + 1) * P)
                        o = bank[:, 2, t * CTX:(t + 1) * CTX]
                        mm(o, q_n[:, hd, cols], k_n[:, hd, SEQ:TOK], True, False)
                        last = mm(o, q_r[r, hd // 2, cols], krope[r, SEQ:TOK], False, True)
                    last.then_inc(s["s_done"], 1)

                def turn(hd):
                    pe.wait_ge(s["p_ready"], hd + 1)
                    for b in range(3):
                        for j in range(4):
                            last = pe.transpose(bank[:, 3 + b, j * P:(j + 1) * P], probs[:, hd % 2, b, j * P:(j + 1) * P], ident)
                        last.then_inc(s["pt_done"], 1)

                def weigh(hd):
                    o = bank[:, 6 + hd % 2, :]
                    pe.wait_ge(s["pt_lat"], hd + 1)
                    if hd >= 2:
                        pe.wait_ge(s["o_ready"], hd - 1)
                    for t in range(TILES):
                        mm(o[:, 0:SEQ], v_tm[:, t, hd * P:(hd + 1) * P], probs_t[:, t, :], t == 0, t == TILES - 1)
                    pe.wait_ge(s["pt_ctx"], hd + 1)
                    for t in range(2):
                        last = mm(o[:, SEQ:TOK], v_tm[:, LT_TILES + t, hd * P:(hd + 1) * P], probs_tc[:, t, :], t == 0, t == 1)
                    last.then_inc(s["pv_done"], 1)

                scores(0)
                for hd in range(HEADS):
                    if hd + 1 < HEADS:
                        scores(hd + 1)
                    turn(hd)
                    weigh(hd)
                pe.wait_ge(s["o_ready"], HEADS)
                for p, (slot, trn) in enumerate([(2, 1), (0, 2)]):
                    load_done(pe, "mla", slot, trn)
                    w = slot_view(slot, DC, 512)
                    for j in range(4):
                        for k in range(DC):
                            last = mm(bank[:, 4 * p + j, :], w[:, k, j * P:(j + 1) * P], u[:, k, :], k == 0, k == DC - 1)
                        last.then_inc(s["yproj"] if j < 3 else panel_done[slot], 1)

            def norm_mean(n, cols):
                for k in range(DC):
                    pe.wait_ge(s["r_ready"], DC * n + k + 1)
                    last = mm(bank[:, 0, 0:cols.stop - cols.start], ones, h[:, k, cols], k == 0, k == DC - 1)
                last.then_inc(s["mean_done"], 1)

            def norm_variance(n, T):
                for k in range(DC):
                    pe.wait_ge(s["cent_sq"], DC * n + k + 1)
                    last = mm(bank[:, 1, 0:T], ones, sq[:, k, 0:T], k == 0, k == DC - 1)
                last.then_inc(s["var_done"], 1)

            def mm3(o, wh, wl, x, first, last):
                mm(o, r(wh), r(x[:, 0, :]), first, False)
                mm(o, r(wh), r(x[:, 1, :]), False, False)
                return mm(o, r(wl), r(x[:, 0, :]), False, last)

            def ffn(f, name, down, u_before, layer=0):
                def panel(slot, turn, first=False):
                    for half in range(2):
                        i = 2 * (SLOTS * turn + slot) + half
                        pe.wait_ge(s["lo_ready"], PARTS * f + i + 1)
                        pe.wait_ge(s["pair_free"], FC * f + i + 1)
                        q = (2 * slot + half) % 3
                        wh, wl = (w[:, q, :].rearrange("p (k n) -> p k n", k=DC) for w in (w_hi, w_lo))
                        for g in range(2):
                            cols = slice(g * P, (g + 1) * P)
                            for k in range(DC):
                                if first and half == 0 and g == 0:
                                    pe.wait_ge(s["u_ready"], u_before + k + 1)
                                last = mm3(bank[:, 2 * q + g, 0:SEQ], wh[:, k, cols], wl[:, k, cols], u_parts[:, k], k == 0, k == DC - 1)
                        last.then_inc(panel_done[PLAN.slot(name, slot)] if half else s["pair_done"], 1)

                def down_panel(slot, turn):
                    m = SLOTS * turn + slot
                    for half in range(2):
                        pe.wait_ge(s["lo_ready"], PARTS * f + FC + 2 * m + half + 1)
                        q = (FC + 2 * slot + half) % 3
                        wh, wl = (w[:, q, 0:HALF].rearrange("p (k n) -> p k n", n=P) for w in (w_hi, w_lo))
                        for j in range(FC // 2):
                            k = FC // 2 * half + j
                            last = mm3(bank[:, m, 0:SEQ], wh[:, j, :], wl[:, j, :], hidden[:, k], k == 0, k == FC - 1)
                        last.then_inc(panel_done[PLAN.slot(down, slot)] if half else s["pair_done"], 1)

                panel(0, 0, True)
                panel(1, 0)
                with pe.Fori(0, 3) as i:
                    panel(2, i)
                    panel(0, i + 1)
                    panel(1, i + 1)
                pe.wait_ge(s["hid_ready"], FC * (f + 1))
                down_panel(0, 0)
                down_panel(1, 0)
                with pe.Fori(0, 2) as i:
                    down_panel(2, i)
                    down_panel(0, i + 1)
                    down_panel(1, i + 1)

            def gdn():
                pe.wait_ge(s["u_ready"], U_GDN + DC)
                for t in range(TILES):
                    for k in range(DC):
                        last = mm(bank[:, 2, t * 64:(t + 1) * 64], u[:, k, t * P:(t + 1) * P], w_ba[:, k, :], k == 0, k == DC - 1)
                last.then_inc(s["gate_sums"], 1)
                pe.wait_ge(s["g_ready"], 1)
                for d in range(2):
                    mm(bank[:, 3, d * 64:(d + 1) * 64], tri[:, d, :], G_[:, d], True, True)
                    last = mm(bank[:, 3, 128 + d * 64:192 + d * 64], ones, G_[:, d], True, True)
                last.then_inc(s["gate_sums"], 1)
                with pe.Fori(0, GROUPS) as g:
                    gdn_group(g)
                pe.wait_ge(s["y_ready"], GROUPS)
                for p in range(4):
                    load_done(pe, "gdn_out", p % SLOTS, p // SLOTS)
                    w = slot_view(p % SLOTS, GV_HEADS, 2 * P)
                    for j in range(2):
                        for k in range(GV_HEADS):
                            last = mm(bank[:, 2 * p + j, 0:SEQ], w[:, k, j * P:(j + 1) * P], y_all[:, k, :], k == 0, k == GV_HEADS - 1)
                        last.then_inc(panel_done[p % SLOTS] if j else s["yproj"], 1)

            def gdn_group(g):
                pe.wait_ge(s["oacc_std"], 2 * g + 2)
                pe.wait_ge(s["gcum_ready"], 1)
                def project(slot, j, o, T):
                    n = 4 * slot + j
                    wh = gw_hi[n % 4]
                    wl = ring_lo[:, slot, :].rearrange("p (k n) -> p k n", k=DC)[:, :, j * P:(j + 1) * P]
                    pe.wait_ge(s["parts_split"], SPLITS * g + DC // 2 + n + 1)
                    for k in range(DC):
                        if n == 0:
                            if k % 2:
                                pe.wait_ge(s["odd_lo"], DC // 2 * g + k // 2 + 1)
                            else:
                                pe.wait_ge(s["parts_lo"], SPLITS * g + k // 2 + 1)
                        mm(o, r(wh[:, k, :]), r(gu_hi[:, k, 0:T]), k == 0, False)
                        mm(o, r(wh[:, k, :]), r(gu_lo[:, k, 0:T]), False, False)
                    pe.wait_ge(s["parts_lo"], SPLITS * g + DC // 2 + n + 1)
                    for k in range(DC):
                        last = mm(o, r(wl[:, k, :]), r(gu_hi[:, k, 0:T]), False, k == DC - 1)
                    return last
                project(0, 0, bank[:, 0, :], TOK).then_inc(s["proj_done"], 1)
                project(0, 1, bank[:, 1, :], TOK).then_inc(s["proj_done"], 1)
                project(0, 2, bank[:, 2, 0:SEQ], SEQ).then_inc(s["proj_done"], 1)
                project(0, 3, bank[:, 2, SEQ:TOK], SEQ).then_inc(panel_done[0], 1)
                for j in range(GH):
                    project(1, j, bank[:, 3 + j, :], TOK).then_inc(s["proj_done"] if j < 3 else panel_done[1], 1)
                    if j < 2:
                        for i, b in [[(0, 1), (1, 2)], [(2, 0)]][j]:
                            pe.wait_ge(s["kq_sq"], 3 * g + i + 1)
                            mm(bank[:, b, :], ones, gdn_sq[:, i, :], True, True).then_inc(s["kq_ssq"], 1)
                project(2, 0, bank[:, 7, 0:SEQ], SEQ)
                project(2, 1, bank[:, 7, SEQ:TOK], SEQ).then_inc(s["proj_done"], 1)
                pe.wait_ge(s["kq_std"], 3 * g + 3)
                project(2, 2, bank[:, 0, 0:SEQ], SEQ)
                project(2, 3, bank[:, 0, SEQ:TOK], SEQ).then_inc(panel_done[2], 1)
                def prepare(st):
                    for d in range(2):
                        n = 4 * g + st
                        if st > 1:
                            pe.wait_ge(sd["rest_ready"], 2 * (3 * g + st - 1) + d - 1)
                        pe.wait_ge(sd["gtri_ready"], 2 * (n + 1) + d - 1)
                        mm(bank[:, 4 * d + 3, :], ones, G[:, d].rearrange("p a b -> p (a b)"), True, True).then_inc(sd["gbc_done"], 1)

                pe.wait_ge(s["cin_ready"], 8 * g + 8)
                pe.wait_ge(s["z_ready"], 2 * g + 1)
                prepare(0)
                for j in range(GKH):
                    pe.wait_ge(s["kq_ready"], 3 * g + j + 1)
                    for t in range(TILES):
                        last = pe.transpose(bank[:, 1 + j, t * P:(t + 1) * P], k_fm[:, j, t * P:(t + 1) * P], ident)
                    last.then_inc(s["kt_done"], 1)
                for t in range(TILES):
                    for j in range(GKH):
                        cols = slice(t * P, (t + 1) * P)
                        last = mm(bank[:, 4 + t // 2, (t % 2 * GKH + j) * P:(t % 2 * GKH + j + 1) * P], k_fm[:, j, cols], k_fm[:, j, cols], True, True)
                    if t % 2:
                        last.then_inc(s["kk_done"], 1)
                pe.wait_ge(s["kq_ready"], 3 * g + 3)
                for t in range(LT_TILES):
                    for j in range(GKH):
                        cols = slice(t * P, (t + 1) * P)
                        last = mm(bank[:, 6, (t * GKH + j) * P:(t * GKH + j + 1) * P], k_fm[:, j, cols], q_fm[:, j, cols], True, True)
                last.then_inc(s["kk_done"], 1)
                for j in range(GH):
                    pe.wait_ge(s["act_ready"], 8 * g + 4 + j + 1)
                    if j < 2:
                        pe.wait_ge(s["kt_ready"], 2 * g + j + 1)
                    elif j == 2:
                        pe.wait_ge(s["z_ready"], 2 * g + 2)
                    else:
                        pe.wait_ge(s["kqm_ready"], g + 1)
                    for t in range(TILES):
                        last = pe.transpose(bank[:, VT_BANK[j], t * P:(t + 1) * P], v_fm[:, j, t * P:(t + 1) * P], ident)
                    last.then_inc(s["vt_done"], 1)
                pe.wait_ge(s["vt_ready"], 4 * g + 4)
                pe.wait_ge(s["z_ready"], 2 * g + 2)
                pe.wait_ge(s["kt_ready"], 2 * g + 2)
                pe.wait_ge(s["kk_ready"], 2 * g + 2)
                pe.wait_ge(s["kqm_ready"], g + 1)
                for st in range(4):
                    for d in range(2):
                        pe.wait_ge(sd["xt0_ready"], 2 * (4 * g + st + 1) + d - 1)
                        for j in range(GH):
                            last = pe.transpose(bank[:, 4 * d + 2, j * P:(j + 1) * P], XT[:, d, j, :], ident)
                        last.then_inc(sd["x0_done"], 1)
                    for b in range(1, LEVELS):
                        for d in range(2):
                            n = 4 * g + st
                            pe.wait_ge(sd["ml_ready"], 2 * (LEVELS * n + b + 1) + d - 1)
                            if b == 1:
                                pe.wait_ge(sd["x0_ready"], 2 * (n + 1) + d - 1)
                            else:
                                pe.wait_ge(sd["xs_ready"], 2 * (6 * n + b - 1) + d - 1)
                            for j in range(GH):
                                last = mm(bank[:, 4 * d, j * P:(j + 1) * P], ML[:, d, b % 2, j, :], X[:, d, j, :], True, True)
                            last.then_inc(sd["y_done"], 1)
                        for d in range(2):
                            n = 4 * g + st
                            pe.wait_ge(sd["yc_ready"], 2 * (6 * n + b) + d - 1)
                            if b > 1:
                                pe.wait_ge(sd["xt_ready"], 2 * (6 * n + b - 1) + d - 1)
                            elif st > LT_TILES:
                                pe.wait_ge(sd["od_ready"], 2 * (2 * g + st - LT_TILES) + d - 1)
                            for j in range(GH):
                                last = mm(bank[:, 4 * d + 1, j * P:(j + 1) * P], XT[:, d, j, :], Y[:, d, j, :], True, True)
                            last.then_inc(sd["xy_done"], 1)
                        if b == 1 and st:
                            for d in range(2):
                                t = SCAN[d][st]
                                pe.wait_ge(sd["su_ready"], 2 * (3 * g + st) + d - 1)
                                for j in range(GH):
                                    last = mm(bank[:, 4 * d + 3, j * P:(j + 1) * P], k_fm[:, j // 2, t * P:(t + 1) * P], state[:, d, j, :], True, True)
                                last.then_inc(sd["ks_done"], 1)
                        if b == 3 and st < 3:
                            prepare(st + 1)
                        for d in range(2):
                            n = 4 * g + st
                            pe.wait_ge(sd["xs_ready"], 2 * (6 * n + b) + d - 1)
                            for j in range(GH):
                                last = pe.transpose(bank[:, 4 * d + 2, j * P:(j + 1) * P], X[:, d, j, :], ident)
                            last.then_inc(sd["xt_done"], 1)
                    for d in range(2):
                        n = 4 * g + st
                        t = SCAN[d][st]
                        pe.wait_ge(sd["xt_ready"], 2 * (6 * n + 6) + d - 1)
                        if st < 3:
                            pe.wait_ge(sd["diff_ready"], 2 * (n + 2) + d - 1)
                            if st + 1 >= LT_TILES:
                                pe.wait_ge(sd["eg_ready"], 2 * (2 * g + st) + d - 1)
                        if st:
                            pe.wait_ge(sd["rest_ready"], 2 * (3 * g + st) + d - 1)
                        for j in range(GH):
                            last = mm(bank[:, 4 * d + 3, j * P:(j + 1) * P], XT[:, d, j, :], R[:, d, j, :] if st else gv_tm[:, t, j, :], True, True)
                        last.then_inc(sd["vn_done"], 1)
                    for d in range(2):
                        n = 4 * g + st
                        t = SCAN[d][st]
                        pe.wait_ge(sd["vn_ready"], 2 * (n + 1) + d - 1)
                        if st < 3:
                            pe.wait_ge(sd["kd_ready"], 2 * (3 * g + st + 1) + d - 1)
                            for j in range(GH):
                                last = mm(bank[:, 4 * d + 3, j * P:(j + 1) * P], KD[:, d, j, :], V[:, d, j, :], True, True)
                            last.then_inc(sd["su_done"], 1)
                        if st >= LT_TILES:
                            pe.wait_ge(sd["qd_ready"], 2 * (2 * g + st - 1) + d - 1)
                            pe.wait_ge(sd["at_ready"], 2 * (2 * g + st - 1) + d - 1)
                            for j in range(GH):
                                o = bank[:, 4 * d + 1, j * P:(j + 1) * P]
                                mm(o, state[:, d, j, :], QDS[st % 2][:, d, j, :], True, False)
                                last = mm(o, V[:, d, j, :], AT[:, d, j, :], False, True)
                            last.then_inc(sd["od_done"], 1)
                for half in range(2):
                    pe.wait_ge(s["oacc_sq"], 2 * g + half + 1)
                    mm(bank[:, half * 4, :], ones, gdn_sq[:, half, :], True, True).then_inc(s["oacc_ssq"], 1)

            def mean_square(i):
                for k in range(DC):
                    pe.wait_ge(s["sq_ready"], DC * i + k + 1)
                    last = mm(bank[:, 0, 0:SEQ], ones, sq2[:, k, :], k == 0, k == DC - 1)
                last.then_inc(s["ssq_done"], 1)

            def mixer(l):
                T = SEQ
                pe.wait_ge(s["u_ready"], U_MIX(l) + DC)
                for k in range(DC):
                    last = mm(bank[0:GLA_RANK, 7, T:2 * T], w_glr[:, k, :], u[:, k, 0:T], k == 0, k == DC - 1)
                last.then_inc(s["glr_done"], 1)
                for p in range(4):
                    load_done(pe, "mix_in", p % SLOTS, p // SLOTS, l)
                    w = slot_view(p % SLOTS, DC, 512)
                    for j in range(4 if p < 3 else 1):
                        o = bank[:, 2 * (p if p > 1 else 1 - p) + j // 2, j % 2 * T:(j % 2 + 1) * T]
                        for k in range(DC):
                            last = mm(o, w[:, k, j * P:(j + 1) * P], u[:, k, 0:T], k == 0, k == DC - 1)
                        if j == 1:
                            last.then_inc(s["mixp_done"], 1)
                        if j == 3:
                            last.then_inc(panel_done[p % SLOTS], 1)
                    if p == 0:
                        pe.wait_ge(s["glr_ready"], l + 1)
                        mm(bank[:, 7, 0:T], gate2[0:GLA_RANK, :], glr_s[0:GLA_RANK, :], True, True).then_inc(s["gate_done"], 1)
                    if p == 3:
                        last.then_inc(s["mixp_done"], 1)
                        pe.wait_ge(s["gy_ready"], l + 1)
                        for t in range(2):
                            if t:
                                pe.wait_ge(s["gqk_ready"], l + 1)
                            o = bank[:, 7 if t == 0 else 0, 0:3 * P]
                            for k in range(DC):
                                last = mm(o, u[:, k, t * P:(t + 1) * P], w[:, k, P:4 * P], k == 0, k == DC - 1)
                            last.then_inc(panel_done[p % SLOTS] if t else s["mixp_done"], 1)
                pe.wait_ge(s["swq_ready"], 3 * l + 3)
                pe.wait_ge(s["gv_ready"], 2 * l + 2)
                pe.wait_ge(s["sig_ready"], l + 1)
                pe.wait_ge(s["gr_ready"], l + 1)
                pe.wait_ge(s["conv_u"], l + 1)
                for hd in range(SWA_HEADS):
                    kv = hd // 4
                    r = slice(64 * kv, 64 * kv + 64)
                    mm(bank[:, hd, 0:P], s_q[r, hd % 4, 0:P], s_k[r, 0:P], True, True)
                    mm(bank[:, hd, P:3 * P], s_q[r, hd % 4, P:T], s_k[r, :], True, True).then_inc(s["sw_done"], 1)
                pe.wait_ge(s["gqe_ready"], l + 1)
                for t in range(3):
                    for hd in range(GLA_HEADS):
                        r = slice(GLA_DK * hd, GLA_DK * hd + GLA_DK)
                        if t == 0:
                            pe.wait_ge(s["swb_ready"], SWA_HEADS * l + 2 * hd + 2)
                        elif t == 1:
                            pe.wait_ge(s["att_ready"], 12 * l + hd + 1)
                        else:
                            pe.wait_ge(s["att_ready"], 12 * l + 4 + hd + 1)
                        if t < 2:
                            cols = slice(t * P, (t + 1) * P)
                            for lv in range(8):
                                o = bank[:, 2 * hd + lv // 4, lv % 4 * P:(lv % 4 + 1) * P]
                                kk_, qq_ = (gqk[r, 1, cols], gqk[r, 0, cols]) if lv == 0 else (ke[r, lv - 1, cols], qe[r, lv - 1, cols])
                                last = pe.matmul(o, kk_, qq_, start=True, stop=True)
                        else:
                            last = pe.matmul(bank[:, 2 * hd, 0:P], ke[r, 7, 0:P], qe[r, 7, P:T], start=True, stop=True)
                        last.then_inc(s["gs_done"], 1)
                pe.wait_ge(s["att_ready"], 12 * l + 8)
                pe.wait_ge(s["cvy_ready"], l + 1)
                for b in range(2):
                    last = mm(bank[:, 7, 0:T], ones, conv_y[:, b, :], b == 0, b == 1)
                last.then_inc(s["cv_mean"], 1)
                pe.wait_ge(s["att_ready"], 12 * l + 12)
                for hd in range(GLA_HEADS):
                    r = slice(64 * (hd % 2), 64 * (hd % 2) + 64)
                    vc = slice(GLA_DV * hd, GLA_DV * hd + GLA_DV)
                    o = bank[r, hd // 2, :]
                    mm(o[:, 0:P], g_v[:, 0, vc], att[:, hd, 0, :], True, True)
                    mm(o[:, P:T], g_v[:, 0, vc], att[:, hd, 2, :], True, False)
                    last = mm(o[:, P:T], g_v[:, 1, vc], att[:, hd, 1, :], False, True)
                last.then_inc(s["go_done"], 1)
                pe.wait_ge(s["cv_sq_ready"], l + 1)
                for b in range(2):
                    last = mm(bank[:, 7, T:2 * T], ones, cv_sq[:, b, :], b == 0, b == 1)
                last.then_inc(s["cv_var"], 1)
                pe.wait_ge(s["swp_ready"], l + 1)
                for b in range(6):
                    if b == 5:
                        pe.wait_ge(s["cv_std"], l + 1)
                    for j in range(4):
                        i = 4 * b + j
                        last = pe.transpose(bank[:, 2 + b, j * P:(j + 1) * P], swp[:, i // 3, i % 3, :], ident)
                    last.then_inc(s["swt_done"], 1)
                pe.wait_ge(s["go_sq"], l + 1)
                for b in range(2):
                    last = mm(bank[:, 0, b * T:(b + 1) * T], ones64, og_sq[:, b, :], True, True)
                last.then_inc(s["go_ssq"], 1)
                pe.wait_ge(s["swt_ready"], 6 * l + 6)
                for hd in range(SWA_HEADS):
                    kv = hd // 4
                    r = slice(64 * kv, 64 * kv + 64)
                    o = bank[r, 2 + hd % 4, :]
                    vc = slice(SWA_DH * kv, SWA_DH * kv + SWA_DH)
                    mm(o[:, 0:P], s_v[:, 0, vc], swt[:, hd, 0, :], True, True)
                    mm(o[:, P:T], s_v[:, 0, vc], swt[:, hd, 1, :], True, False)
                    last = mm(o[:, P:T], s_v[:, 1, vc], swt[:, hd, 2, :], False, True)
                last.then_inc(s["swo_done"], 1)
                pe.wait_ge(s["swo_ready"], l + 1)
                pe.wait_ge(s["gla_ready"], l + 1)
                pe.wait_ge(s["cv_ready"], l + 1)
                for p in range(2):
                    load_done(pe, "mix_out", p, 0, l)
                    w = slot_view(p, DC, 512)
                    for j in range(4):
                        for k in range(DC):
                            last = mm(bank[:, 4 * p + j, 0:T], w[:, k, j * P:(j + 1) * P], mix[:, k, :], k == 0, k == DC - 1)
                        last.then_inc(s["yproj"] if j < 3 else panel_done[p], 1)

            pe.wait_ge(s["cond_ready"], 1)
            modulation(0, "mod0", 0, range(10))
            pe.wait_ge(in_loaded, 32)
            turn_rows(0, 0, 40)
            mla()
            norm_mean(0, slice(0, TOK))
            modulation(0, "mod0b", 10, [0])
            norm_variance(0, TOK)
            modulation(0, "mod0b", 10, [1])
            turn_rows(0, 40, MB)
            ffn(0, "ffn0", "down0", DC)
            norm_mean(1, slice(0, SEQ))
            modulation(1, "mod1", 0, [0])
            norm_variance(1, SEQ)
            modulation(1, "mod1", 0, [1, 2])
            pe.wait_ge(s["mod_copied"], 15)
            ffn(1, "ffn0c", "down0c", 2 * DC)
            norm_mean(2, slice(SEQ, TOK))
            modulation(1, "mod1b", 3, range(3))
            norm_variance(2, SEQ)
            modulation(1, "mod1b", 3, range(3, 9))
            turn_rows(1, 0, MB)
            gdn()
            norm_mean(3, slice(0, SEQ))
            norm_variance(3, SEQ)
            ffn(2, "ffn1", "down1", U_FFN1)
            norm_mean(4, slice(0, SEQ))
            norm_variance(4, SEQ)
            with pe.Fori(0, DEPTH) as l:
                mean_square(6 * l)
                ffn(2 * l + 3, "ffnA", "downA", U_BLOCK2 + 3 * DC * l, l)
                mean_square(6 * l + 1)
                mean_square(6 * l + 2)
                mixer(l)
                mean_square(6 * l + 3)
                mean_square(6 * l + 4)
                ffn(2 * l + 4, "ffnB", "downB", U_BLOCK2 + 3 * DC * l + 2 * DC, l)
                mean_square(6 * l + 5)

        @block.scalar
        def _(act):
            act.wait_ge(par_loaded, 16)
            act.activation(cond[:], cvec, ACT.Silu).then_inc(s["cond_ready"], 1)

            def copy(o, i, scale=1.0):
                return act.activation(o, i, ACT.Copy, scale=scale)

            def mla():
                for b in range(QC + KC):
                    act.wait_ge(s["lat_copied"], b + 1)
                    act.activation(lat_sq[:, b, :], lat[:, b, :], ACT.Square).then_inc(s["lat_squared"], 1)
                for b, n in enumerate([Q_RANK, KV_RANK]):
                    act.wait_ge(s["lat_ssq"], b + 1)
                    act.activation(std[:, b, :], bank[:, b, :], ACT.Sqrt, bias=EPS_RMS, scale=1.0 / n).then_inc(s["lat_std"], 1)
                for j in range(HEADS):
                    if j < HEADS - 1:
                        act.wait_ge(s["mla_done"], MLA_Q + j + 1)
                    else:
                        panel_over(act, "mla", 2, 0)
                    copy(q_n[:, j, :], bank[:, j, :]).then_inc(s["mla_copied"], 1)
                for j in range(HEADS):
                    act.wait_ge(s["mla_done"], MLA_K + j + 1)
                    copy(k_n[:, j, :], bank[:, j, :]).then_inc(s["mla_copied"], 1)
                for n in range(8):
                    if n < 7:
                        act.wait_ge(s["mla_done"], MLA_V + n + 1)
                    else:
                        panel_over(act, "mla", 1, 1)
                    copy(v_tm[:, n // 2, n % 2 * 512:n % 2 * 512 + 512], bank[:, n, :]).then_inc(s["mla_copied"], 1)
                for hd in range(HEADS):
                    act.wait_ge(s["max_ready"], hd + 1)
                    d = hd % 2
                    for i in range(4):
                        b, cols = (i, slice(0, 512)) if i < 2 else (2, slice((i - 2) * CTX, (i - 1) * CTX))
                        last = act.activation(probs[:, d, b, cols], bank[:, b, cols], ACT.Exp, bias=negmax[:, d, i:i + 1],
                                              scale=MLA_SCALE, accum_out=rowsum[:, d, i:i + 1])
                    last.then_inc(s["exp_done"], 1)
                    if hd:
                        act.wait_ge(s["pv_done"], hd)
                    for t in range(LT_TILES):
                        act.wait_ge(s["pt_done"], 3 * hd + t + 1)
                        last = copy(probs_t[:, :, t * P:(t + 1) * P], bank[:, 3 + t, :].rearrange("p (k q) -> p k q", k=TILES))
                    last.then_inc(s["pt_lat"], 1)

            def copy_rows(l, name, first, panels):
                for i in panels:
                    panel_over(act, name, i % SLOTS, i // SLOTS)
                    copy(rows_at(l, (first + i) * 512, 512), bank[0:2, 3 + i % SLOTS, :]).then_inc(s["mod_copied"], 1)

            def norm_squares(n, cols):
                for k in range(DC):
                    act.wait_ge(s["cent_ready"], DC * n + k + 1)
                    act.activation(sq[:, k, 0:cols.stop - cols.start], h[:, k, cols], ACT.Square).then_inc(s["cent_sq"], 1)

            def warm_root():
                act.activation(warm[:], EPS_LN, ACT.Sqrt)

            def norm_root(n, T):
                warm_root()
                act.wait_ge(s["var_done"], n + 1)
                act.activation(std[:, 0, 0:T], bank[:, 1, 0:T], ACT.Sqrt, bias=EPS_LN, scale=1.0 / D).then_inc(s["var_std"], 1)

            def norm_shift(n, b, cols):
                for k in range(DC):
                    act.wait_ge(s["norm_ready"], DC * n + k + 1)
                    act.activation(h[:, k, cols], h[:, k, cols], ACT.Identity, bias=b[:, k:k + 1]).then_inc(s["h_ready"], 1)

            def layer_norm(n, b, cols, following=None, between=None):
                if following:
                    act.wait_ge(s["r_ready"], DC * (n + 1))
                    split_hi(following, 0, 0, 0, 0)
                norm_squares(n, cols)
                if between:
                    between()
                norm_root(n, cols.stop - cols.start)
                norm_shift(n, b, cols)

            def raw_part(name, slot, half):
                slot = PLAN.slot(name, slot)
                if name.startswith("down"):
                    return ring[:, slot, HALF * half:HALF * (half + 1)]
                return ring[:, slot, :].rearrange("p (k n) -> p k n", k=DC)[:, :, half * 2 * P:(half + 1) * 2 * P]

            def split_hi(name, slot, turn, half, layer, between=None):
                q = ((FC if name.startswith("down") else 0) + 2 * slot + half) % 3
                raw = raw_part(name, slot, half)
                load_done(act, name, slot, turn, layer)
                for piece in range(2):
                    if piece and between:
                        between()
                    if name.startswith("down"):
                        a = slice(piece * HALF // 2, (piece + 1) * HALF // 2)
                        act.activation(r(w_hi[:, q, a]), raw[:, a], ACT.Copy).then_inc(s["hi_ready"], 1)
                    else:
                        a = slice(piece * DC // 2, (piece + 1) * DC // 2)
                        act.activation(r(w_hi[:, q, :].rearrange("p (k n) -> p k n", k=DC)[:, a]), raw[:, a], ACT.Copy).then_inc(s["hi_ready"], 1)

            def ffn_tokens(f):
                for k in range(DC):
                    act.wait_ge(s["whole_ready"], DC * f + k + 1)
                    act.activation(r(u_parts[:, k, 0, :]), tokens[:, k, :], ACT.Copy).then_inc(s["uhi_ready"], 1)

            def ffn(f, name, down, layer=0, between=None):
                ffn_tokens(f)
                if between:
                    between()
                split_hi(name, 0, 0, 1, layer)
                split_hi(name, 1, 0, 0, layer)

                def pair(slot, turn, half, ahead, last=False):
                    i = 2 * (SLOTS * turn + slot) + half
                    if half:
                        panel_over(act, name, slot, turn, layer)
                    else:
                        act.wait_ge(s["pair_done"], HALVES * f + SLOTS * turn + slot + 1)
                    q = (2 * slot + half) % 3
                    act.activation(silu_g[:, q, :], bank[:, 2 * q, 0:SEQ], ACT.Silu).then_inc(s["silu_ready"], 1)
                    if last:
                        act.wait_ge(s["pair_free"], FC * f + i + 1 + 3)
                        act.activation(r(hidden[:, i, 0, :]), whole[:, q, :], ACT.Copy).then_inc(s["hid_hi"], 1)
                        split_hi(*ahead, layer)
                        return
                    split_hi(*ahead, layer, lambda: act.wait_ge(s["pair_free"], FC * f + i + 1 + 3))
                    act.activation(r(hidden[:, i, 0, :]), whole[:, q, :], ACT.Copy).then_inc(s["hid_hi"], 1)

                def next_part(slot, turn, half):
                    step = 1 + half
                    return (slot + step) % SLOTS, turn + (slot + step) // SLOTS, 1 - half

                with act.Fori(0, 3) as i:
                    for slot in range(SLOTS):
                        for half in range(2):
                            pair(slot, i, half, (name, *next_part(slot, i, half)))
                pair(0, 3, 0, (name, 1, 3, 1))
                pair(0, 3, 1, (down, 0, 0, 0))
                pair(1, 3, 0, (down, 0, 0, 1))
                pair(1, 3, 1, (down, 1, 0, 0), True)

                def half_over(slot, turn, half):
                    if half:
                        panel_over(act, down, slot, turn, layer)
                    else:
                        act.wait_ge(s["pair_done"], HALVES * f + FC // 2 + SLOTS * turn + slot + 1)

                with act.Fori(0, 2) as i:
                    for slot in range(SLOTS):
                        for half in range(2):
                            half_over(slot, i, half)
                            split_hi(down, *next_part(slot, i, half), layer)
                half_over(0, 2, 0)
                split_hi(down, 1, 2, 1, layer)

            def gdn_gates():
                act.wait_ge(s["gate_sums"], 1)
                ba = bank[:, 2, 0:TILES * 64].rearrange("p (t d w h) -> p t d w h", t=TILES, d=2, w=2)
                for d in range(2):
                    last = act.activation(BETA[:, d], ba[:, :, d, 0, :], ACT.Sigmoid)
                last.then_inc(s["gate_acts"], 1)
                act.activation(a_log, a_log, ACT.Exp)
                act.wait_ge(s["ax_ready"], 1)
                act.activation(soft[:, 1], soft[:, 1], ACT.Exp)
                act.drain()
                act.activation(soft[:, 1], soft[:, 1], ACT.Ln, bias=ONE).then_inc(s["gate_acts"], 1)
                act.wait_ge(s["gcum_ready"], 1)
                act.activation(EG, GCUM, ACT.Exp)
                act.activation(ED, ED, ACT.Exp)
                act.activation(ETOT, ETOT, ACT.Exp).then_inc(s["gexp_ready"], 1)

            def gdn_tokens():
                for k in range(0, DC, 2):
                    act.activation(r(gu_hi[:, k, :]), u[:, k, :], ACT.Copy).then_inc(s["parts_split"], 1)

            def gdn_group(g):
                raw = [k_fm[:, 0, :], k_fm[:, 1, :], q_fm[:, 0, :], q_fm[:, 1, :]] + [v_fm[:, j, :] for j in range(GH)]

                def silu(b):
                    act.wait_ge(s["conv_done"], 8 * g + b + 3)
                    act.activation(raw[b], raw[b], ACT.Silu).then_inc(s["act_ready"], 1)

                def split_block(n):
                    slot, j = divmod(n, 4)
                    if j == 0:
                        load_done(act, "gdn", slot, g)
                    w = ring[:, slot, :].rearrange("p (k n) -> p k n", k=DC)[:, :, j * P:(j + 1) * P]
                    act.activation(r(gw_hi[n % 4]), w, ACT.Copy).then_inc(s["parts_split"], 1)

                for n in range(4):
                    split_block(n)
                for b in range(8):
                    if b in (0, 1):
                        act.wait_ge(s["proj_done"], 7 * g + b + 1)
                    elif b == 2:
                        act.wait_ge(s["proj_done"], 7 * g + 3)
                        split_block(6)
                        panel_over(act, "gdn", 0, g)
                    elif 4 <= b < 7:
                        act.wait_ge(s["proj_done"], 7 * g + b)
                    elif b == 7:
                        panel_over(act, "gdn", 1, g)
                    if b == 2:
                        split_block(7)
                    elif b != 3:
                        split_block(b + 4)
                    act.wait_ge(s["conv_done"], 8 * g + b + 1)
                    if 2 <= b < 4:
                        i = bank[:, 2, (b - 2) * SEQ:(b - 1) * SEQ]
                        copy(cin[:, b % 2, 0, 2:2 + SEQ], i).then_inc(s["cin_ready"], 1)
                    else:
                        i = bank[:, b if b < 2 else b - 1, :].rearrange("p (s t) -> p s t", s=2)
                        copy(cin[:, b % 2, :, 2:2 + SEQ], i).then_inc(s["cin_ready"], 1)
                    if b:
                        silu(b - 1)
                    if b == 3:
                        act.drain()
                        for j in range(GKH):
                            act.activation(gdn_sq[:, j, :], k_fm[:, j, :], ACT.Square).then_inc(s["kq_sq"], 1)
                    if b == 4:
                        act.drain()
                        act.activation(gdn_sq[:, 2, :], q_fm.rearrange("p a t -> p (a t)"), ACT.Square).then_inc(s["kq_sq"], 1)
                    for j, bk in {4: [(0, 1), (1, 2)], 5: [(2, 0)]}.get(b, []):
                        act.wait_ge(s["kq_ssq"], 3 * g + j + 1)
                        act.activation(gdn_std[:, j, :], bank[:, bk, :], ACT.Sqrt, bias=EPS_RMS).then_inc(s["kq_std"], 1)
                silu(7)
                for i, b in enumerate([7, 0]):
                    if i == 0:
                        act.wait_ge(s["proj_done"], 7 * g + 7)
                    else:
                        panel_over(act, "gdn", 2, g)
                    act.activation(z_s[:, 2 * i:2 * i + 2, :], bank[:, b, :].rearrange("p (a t) -> p a t", a=2), ACT.Silu).then_inc(s["z_ready"], 1)
                heads = lambda bk: bank[:, bk, :].rearrange("p (j q) -> p j q", j=GH)

                def prepare(st):
                    for d in range(2):
                        act.wait_ge(sd["diff_ready"], 2 * (4 * g + st + 1) + d - 1)
                        act.activation(E[:, d], E[:, d], ACT.Exp).then_inc(sd["decay_ready"], 1)
                        if st >= LT_TILES:
                            act.activation(QDS[st % 2][:, d], heads(4 * d + 3), ACT.Exp).then_inc(sd["eg_ready"], 1)

                prepare(0)
                for j in range(GH):
                    act.wait_ge(s["vt_done"], GH * g + j + 1)
                    copy(gv_tm[:, :, j, :], bank[:, VT_BANK[j], :].rearrange("p (t q) -> p t q", t=TILES)).then_inc(s["vt_ready"], 1)
                for i in range(2):
                    act.wait_ge(s["kk_done"], 3 * g + i + 1)
                    copy(kk[:, 2 * i:2 * i + 2], bank[:, 4 + i, :].rearrange("p (t j q) -> p t j q", t=2, j=GKH)).then_inc(s["kk_ready"], 1)
                for st in range(4):
                    n = 4 * g + st
                    for d in range(2):
                        act.wait_ge(sd["x0_done"], 2 * (n + 1) + d - 1)
                        copy(X[:, d], heads(4 * d + 2)).then_inc(sd["x0_ready"], 1)
                    for b in range(1, LEVELS):
                        for d in range(2):
                            act.wait_ge(sd["y_done"], 2 * (6 * n + b) + d - 1)
                            copy(Y[:, d], heads(4 * d)).then_inc(sd["yc_ready"], 1)
                        for d in range(2):
                            act.wait_ge(sd["xt_done"], 2 * (6 * n + b) + d - 1)
                            copy(XT[:, d], heads(4 * d + 2)).then_inc(sd["xt_ready"], 1)
                        if b == 4 and st < 3:
                            prepare(st + 1)
                for half in range(2):
                    if half == 0:
                        act.wait_ge(sd["od_ready"], 2 * (2 * g + 2))
                    act.activation(gdn_sq[:, half, :].rearrange("p (a t) -> p a t", a=2), o_acc[:, 2 * half:2 * half + 2, :], ACT.Square).then_inc(s["oacc_sq"], 1)
                gdn_tokens()
                for half in range(2):
                    act.wait_ge(s["oacc_ssq"], 2 * g + half + 1)
                    act.activation(gdn_std[:, half, :], bank[:, 4 * half, :], ACT.Sqrt, bias=EPS_RMS, scale=1.0 / P).then_inc(s["oacc_std"], 1)

            def root(i, twice):
                warm_root()
                act.wait_ge(s["ssq_done"], i + 1)
                act.activation(std[:, 0, 0:SEQ], bank[:, 0, 0:SEQ], ACT.Sqrt, bias=EPS_RMS4 if twice else EPS_RMS,
                               scale=(4.0 if twice else 1.0) / D).then_inc(s["std_ready"], 1)

            def squares_of_x(batch):
                for k in range(DC):
                    act.wait_ge(s["x_ready"], DC * batch + k + 1)
                    act.activation(sq2[:, k, :], h[:, k, 0:SEQ], ACT.Square).then_inc(s["sq_ready"], 1)

            def squares_of_y(batch):
                for k in range(DC):
                    act.wait_ge(s["yb_ready"], DC * batch + k + 1)
                    act.activation(sq2[:, k, :], yb[:, k, :], ACT.Square).then_inc(s["sq_ready"], 1)

            def mixer(l):
                T = SEQ
                act.wait_ge(s["glr_done"], l + 1)
                copy(glr_s[0:GLA_RANK, :], bank[0:GLA_RANK, 7, T:2 * T]).then_inc(s["glr_ready"], 1)
                two = lambda b: bank[:, b, :].rearrange("p (a t) -> p a t", a=2)
                panel_over(act, "mix_in", 0, 0, l)
                act.activation(sig_g, two(3), ACT.Sigmoid).then_inc(s["sig_ready"], 1)
                act.wait_ge(s["ge_ready"], l + 1)
                act.activation(gl_e, gl_e, ACT.Exp)
                act.drain()
                act.activation(gl_e, gl_e, ACT.Ln, bias=ONE).then_inc(s["gln_ready"], 1)
                act.wait_ge(s["mixp_done"], 5 * l + 2)
                copy(gqk[:, 0, :], bank[:, 0, 0:T], scale=GLA_DK ** -0.5)
                copy(gqk[:, 1, :], bank[:, 0, T:2 * T]).then_inc(s["gqk_ready"], 1)
                panel_over(act, "mix_in", 1, 0, l)
                act.activation(gr_s, two(1), ACT.Silu).then_inc(s["gr_ready"], 1)
                act.wait_ge(s["gabs_ready"], l + 1)
                act.activation(dec, dec, ACT.Exp, scale=1.0 / GLA_TAU).then_inc(s["gdec_ready"], 1)
                act.wait_ge(s["mixp_done"], 5 * l + 3)
                copy(s_q[:, 0:2, :], two(4), scale=SWA_DH ** -0.5).then_inc(s["swq_ready"], 1)
                panel_over(act, "mix_in", 2, 0, l)
                copy(s_q[:, 2:4, :], two(5), scale=SWA_DH ** -0.5).then_inc(s["swq_ready"], 1)
                act.wait_ge(s["mixp_done"], 5 * l + 4)
                copy(s_k, bank[:, 6, 0:T]).then_inc(s["swq_ready"], 1)
                for t in range(2):
                    if t == 0:
                        act.wait_ge(s["mixp_done"], 5 * l + 5)
                    else:
                        panel_over(act, "mix_in", 0, 1, l)
                    b = 7 if t == 0 else 0
                    copy(g_v[:, t, :], bank[:, b, 0:2 * P])
                    copy(s_v[:, t, :], bank[:, b, 2 * P:3 * P]).then_inc(s["gv_ready"], 1)
                act.wait_ge(s["swm_ready"], l + 1)
                for hd in range(SWA_HEADS):
                    act.activation(swp[:, hd, 0, :], swp[:, hd, 0, :], ACT.Exp, bias=swm[:, hd, 0:1], accum_out=sws[:, hd, 0:1])
                    act.activation(swp[:, hd, 1:3, :], swp[:, hd, 1:3, :], ACT.Exp, bias=swm[:, hd, 1:2], accum_out=sws[:, hd, 1:2])
                act.activation(swe, swe, ACT.Exp).then_inc(s["swe_ready"], 1)
                act.wait_ge(s["cv_cent"], l + 1)
                act.activation(cv_sq, conv_y, ACT.Square).then_inc(s["cv_sq_ready"], 1)
                act.wait_ge(s["go_ready"], 2 * l + 2)
                act.activation(og_sq, og, ACT.Square).then_inc(s["go_sq"], 1)
                act.wait_ge(s["cv_var"], l + 1)
                act.activation(gl_e, bank[:, 7, T:2 * T], ACT.Sqrt, bias=EPS_LN, scale=1.0 / (2 * P)).then_inc(s["cv_std"], 1)
                flat = swt.rearrange("p h k q -> p (h k q)")
                for b in range(6):
                    act.wait_ge(s["swt_done"], 6 * l + b + 1)
                    copy(flat[:, 512 * b:512 * b + 512], bank[:, 2 + b, :]).then_inc(s["swt_ready"], 1)
                act.wait_ge(s["go_ssq"], l + 1)
                act.activation(std[:, 0, :], bank[:, 0, :], ACT.Sqrt, bias=EPS_RMS, scale=1.0 / GLA_DV).then_inc(s["go_std"], 1)
                act.wait_ge(s["cv_norm"], l + 1)
                for b in range(2):
                    last = act.activation(mix[:, 2 + b, :], conv_y[:, b, :], ACT.Silu, bias=conv_ln_b[:, b:b + 1])
                last.then_inc(s["cv_ready"], 1)
                act.wait_ge(s["swo_done"], l + 1)
                for b in range(4):
                    last = copy(mix[:, 4 + b, :], bank[:, 2 + b, 0:T])
                last.then_inc(s["swo_ready"], 1)

            def over_down(name, layer=0):
                return lambda e, m: panel_over(e, name, m % SLOTS, m // SLOTS, layer)

            copy_rows(0, "mod0", 0, range(10))
            act.wait_ge(s["mod_ready"], 1)
            mla()
            layer_norm(0, ln_b[0][:, 0], slice(0, TOK), None, lambda: copy_rows(0, "mod0b", 10, [0]))
            split_hi("ffn0", 0, 0, 0, 0)
            ffn(0, "ffn0", "down0", between=lambda: copy_rows(0, "mod0b", 10, [1]))
            layer_norm(1, ln_b[1][:, 0], slice(0, SEQ), None, lambda: copy_rows(1, "mod1", 0, [0]))
            split_hi("ffn0c", 0, 0, 0, 0)
            ffn(1, "ffn0c", "down0c", between=lambda: copy_rows(1, "mod1", 0, [1, 2]))
            norm_squares(2, slice(SEQ, TOK))
            copy_rows(1, "mod1b", 3, range(3))
            norm_root(2, SEQ)
            copy_rows(1, "mod1b", 3, range(3, 6))
            norm_shift(2, ln_b[1][:, 0], slice(SEQ, TOK))
            copy_rows(1, "mod1b", 3, range(6, 9))
            act.wait_ge(s["mod_ready"], 2)
            act.wait_ge(s["u_ready"], U_GDN + DC)
            gdn_tokens()
            gdn_gates()
            with act.Fori(0, GROUPS) as g:
                gdn_group(g)
            act.wait_ge(s["parts_lo"], SPLITS * GROUPS + DC // 2)
            act.wait_ge(s["odd_lo"], DC // 2 * GROUPS + DC // 2)
            layer_norm(3, ln_b[0][:, 1], slice(0, SEQ), "ffn1")
            ffn(2, "ffn1", "down1")
            layer_norm(4, ln_b[1][:, 1], slice(0, SEQ))
            with act.Fori(0, DEPTH) as l:
                act.wait_ge(lpar_loaded, 16 * l + 16)
                split_hi("ffnA", 0, 0, 0, l)
                squares_of_x(3 * l)
                root(6 * l, False)
                ffn(2 * l + 3, "ffnA", "downA", l)
                squares_of_y(3 * l)
                root(6 * l + 1, True)
                squares_of_x(3 * l + 1)
                root(6 * l + 2, False)
                mixer(l)
                squares_of_y(3 * l + 1)
                root(6 * l + 3, False)
                split_hi("ffnB", 0, 0, 0, l)
                squares_of_x(3 * l + 2)
                root(6 * l + 4, False)
                ffn(2 * l + 4, "ffnB", "downB", l)
                squares_of_y(3 * l + 2)
                root(6 * l + 5, True)

        @block.gpsimd
        def _(pool):
            def gdn_tokens(before):
                for k in range(0, DC, 2):
                    pool.wait_ge(s["parts_split"], before + k // 2 + 1)
                    pool.tensor_tensor(r(gu_lo[:, k, :]), u[:, k, :], r(gu_hi[:, k, :]), ALU.subtract).then_inc(s["parts_lo"], 1)

            def gdn_group(g):
                def split_lo(n):
                    slot, j = divmod(n, 4)
                    raw, lo = (t[:, slot, :].rearrange("p (k n) -> p k n", k=DC)[:, :, j * P:(j + 1) * P] for t in (ring, ring_lo))
                    pool.wait_ge(s["parts_split"], SPLITS * g + DC // 2 + n + 1)
                    pool.tensor_tensor(r(lo), raw, r(gw_hi[n % 4]), ALU.subtract).then_inc(s["parts_lo"], 1)

                for n in range(10):
                    split_lo(n)
                pool.wait_ge(s["gst_ready"], g + 1)
                def prepare(st):
                    for d in range(2):
                        if st:
                            pool.wait_ge(sd["gbc_done"], 2 * (4 * g + st) + d - 1)
                        t = SCAN[d][st]
                        pool.tensor_tensor(G[:, d], wide(tri[:, d, :], GH, 1), wide(S_G[:, d, t, :], P, 2), ALU.mult).then_inc(sd["gtri_ready"], 1)

                prepare(0)
                split_lo(10)
                split_lo(11)
                pool.wait_ge(s["kt_ready"], 2 * g + 2)
                pool.wait_ge(s["kq_ready"], 3 * g + 3)
                for st in range(4):
                    n = 4 * g + st
                    for b in range(LEVELS):
                        for d in range(2):
                            t = SCAN[d][st]
                            if b == 0:
                                pool.wait_ge(sd["lt_ready"], 2 * (n + 1) + d - 1)
                                if st:
                                    pool.wait_ge(sd["y_done"], 2 * (6 * n) + d - 1)
                            if b == 2:
                                pool.wait_ge(sd["xt0_ready"], 2 * (n + 1) + d - 1)
                            if b > 2:
                                pool.wait_ge(sd["y_done"], 2 * (6 * n + b - 2) + d - 1)
                            pool.tensor_tensor(ML[:, d, b % 2], LT[:, d], wide(level[:, d, b, :], GH, 1), ALU.mult).then_inc(sd["ml_ready"], 1)
                        if b == 1 and st >= LT_TILES:
                            for d in range(2):
                                t = SCAN[d][st]
                                if st == 3:
                                    pool.wait_ge(sd["od_done"], 2 * (2 * g + 1) + d - 1)
                                pair = "p (a r) q -> p a r q"
                                pool.tensor_tensor(AT[:, d].rearrange(pair, r=2), E[:, d].rearrange(pair, r=2),
                                                   wide(kq[:, d, t], 2, 2), ALU.mult).then_inc(sd["at_ready"], 1)
                        if b == 2 and st < 3:
                            prepare(st + 1)
                        if b == 4 and st < 3:
                            for d in range(2):
                                t = SCAN[d][st]
                                for j in range(GH):
                                    last = pool.tensor_scalar(KD[:, d, j, :], k_tm[:, t, j // 2, :], S_ED[:, d, t, j:j + 1], 1.0, ALU.mult, ALU.mult)
                                last.then_inc(sd["kd_ready"], 1)
                gdn_tokens(SPLITS * g + SPLITS)

            def convolution(l):
                T = SEQ
                terms = [sig_g, cv_sq]
                pool.wait_ge(s["conv_u"], l + 1)
                pool.tensor_tensor(conv_y, conv_in[:, :, 0:T], wide(conv31[:, :, 0], T, 2), ALU.mult)
                for j in range(1, CONV_W):
                    for b in range(2):
                        tap, w = conv_in[:, b, j:j + T], conv31[:, b, j:j + 1]
                        if j == 1:
                            pool.tensor_scalar(terms[j % 2][:, b, :], tap, w, conv_b[:, b:b + 1], ALU.mult, ALU.add)
                        else:
                            pool.tensor_scalar(terms[j % 2][:, b, :], tap, w, 1.0, ALU.mult, ALU.mult)
                    pool.drain()
                    last = pool.tensor_tensor(conv_y, conv_y, terms[j % 2], ALU.add)
                last.then_inc(s["cvy_ready"], 1)

            gdn_tokens(0)
            with pool.Fori(0, GROUPS) as g:
                gdn_group(g)
            with pool.Fori(0, DEPTH) as l:
                convolution(l)

        @block.vector
        def _(dve):
            dve.sem_inc(s["pair_free"], 3)
            dve.sem_inc(s["conv_done"], 2)
            dve.sem_inc(s["oacc_std"], 2)
            dve.wait_ge(par_loaded, 16)
            dve.wait_ge(in_loaded, 32)

            def modulation(l, turn, a, b):
                dve.wait_ge(s["rows_turned"], turn)
                dve.tensor_tensor(mod[:, a:b, :], bank[:, 7, 2 * a:2 * b].rearrange("p (m s) -> p m s", s=2),
                                  wide(b_mod[:, l, a:b], 2, 2), ALU.add)
                dve.drain()
                if a == 0:
                    for row in (1, 4):
                        rows = mod[:, row * DC:(row + 1) * DC, :]
                        last = dve.tensor_scalar(rows, rows, 1.0, None, ALU.add)
                    last.then_inc(s["mod_ready"], 1)
                    dve.drain()

            def shifted(o, shift, scale, k, seg):
                return dve.tensor_scalar(o, h[:, k, seg * SEQ:(seg + 1) * SEQ], mod[:, scale * DC + k, seg:seg + 1],
                                         mod[:, shift * DC + k, seg:seg + 1], ALU.mult, ALU.add)

            def scaled(segs):
                dve.drain()
                for seg in segs:
                    x = h[:, :, seg * SEQ:(seg + 1) * SEQ]
                    dve.tensor_scalar(x, x, ALPHA, None, ALU.mult)
                dve.drain()

            def modulate(shift, scale):
                for k in range(DC):
                    for seg in range(2):
                        last = shifted(u[:, k, seg * SEQ:(seg + 1) * SEQ], shift, scale, k, seg)
                    last.then_inc(s["u_ready"], 1)

            def split_tokens(f, token):
                for k in range(DC + 1):
                    if k < DC:
                        token(tokens[:, k, :], k).then_inc(s["whole_ready"], 1)
                    if k:
                        dve.wait_ge(s["uhi_ready"], DC * f + k)
                        dve.tensor_tensor(r(u_parts[:, k - 1, 1, :]), tokens[:, k - 1, :], r(u_parts[:, k - 1, 0, :]),
                                          ALU.subtract).then_inc(s["u_ready"], 1)

            def rope(o, nat, swapped):
                dve.tensor_tensor(rope_t[:, 0, :], nat, rope_cos, ALU.mult)
                dve.tensor_tensor(rope_t[:, 1, :], swapped, rope_sin, ALU.mult)
                dve.drain()
                dve.tensor_tensor(o, rope_t[:, 0, :], rope_t[:, 1, :], ALU.add)
                dve.drain()

            def mla():
                for b in range(QC + KC):
                    if b % 4 == 3:
                        panel_over(dve, "mla", 0, 0)
                    else:
                        dve.wait_ge(s["mla_done"], b + 1 - b // 4)
                    dve.tensor_copy(lat[:, b, :], bank[:, b, :]).then_inc(s["lat_copied"], 1)
                panel_over(dve, "mla", 1, 0)
                rope(krope[:, 0:SEQ], bank[:, 6, 0:SEQ], bank[:, 7, 0:SEQ])
                dve.tensor_copy(krope[:, SEQ:TOK], bank[:, 6, SEQ:TOK]).then_inc(s["krope_ready"], 1)
                for b, (a, n, g) in enumerate([(0, QC, q_norm), (QC, KC, kv_norm)]):
                    dve.wait_ge(s["lat_std"], b + 1)
                    dve.reciprocal(std[:, b, :], std[:, b, :])
                    dve.drain()
                    for k in range(n):
                        dve.scalar_tensor_tensor(lat[:, a + k, :], lat[:, a + k, :], g[:, k:k + 1], std[:, b, :],
                                                 ALU.mult, ALU.mult).then_inc(s["latn_ready"], 1)
                panel_over(dve, "mla", 0, 1)
                for j in range(HEADS // 2):
                    rope(q_r[:, j, 0:SEQ], bank[:, j, 0:SEQ], bank[:, 4 + j, 0:SEQ])
                    dve.tensor_copy(q_r[:, j, SEQ:TOK], bank[:, j, SEQ:TOK]).then_inc(s["qr_ready"], 1)

                def maxima(hd):
                    d = hd % 2
                    dve.wait_ge(s["s_done"], 2 * hd + 1)
                    for t in range(LT_TILES):
                        dve.tensor_reduce(negmax[:, d, t:t + 1], bank[:, t, :], AX_X, ALU.max, negate=True)
                    dve.wait_ge(s["s_done"], 2 * hd + 2)
                    dve.tensor_reduce(negmax[:, d, 2:4], bank[:, 2, :].rearrange("p (t k) -> p t k", t=2), AX_X, ALU.max, negate=True)
                    dve.drain()
                    dve.tensor_scalar(negmax[:, d, :], negmax[:, d, :], MLA_SCALE, None, ALU.mult).then_inc(s["max_ready"], 1)

                def normed(hd):
                    d = hd % 2
                    dve.wait_ge(s["exp_done"], hd + 1)
                    dve.reciprocal(rowsum[:, d, :], rowsum[:, d, :])
                    dve.drain()
                    for i in range(4):
                        b, cols = (i, slice(0, 512)) if i < 2 else (2, slice((i - 2) * CTX, (i - 1) * CTX))
                        p = probs[:, d, b, cols]
                        last = dve.tensor_scalar(p, p, rowsum[:, d, i:i + 1], None, ALU.mult)
                    last.then_inc(s["p_ready"], 1)

                maxima(0)
                for hd in range(HEADS):
                    normed(hd)
                    if hd + 1 < HEADS:
                        maxima(hd + 1)
                    if hd:
                        dve.wait_ge(s["pv_done"], hd)
                    dve.wait_ge(s["pt_done"], 3 * hd + 3)
                    dve.tensor_copy(probs_tc.rearrange("p k (t q) -> p t k q", t=2),
                                    bank[:, 5, :].rearrange("p (t k q) -> p t k q", t=2, k=2)).then_inc(s["pt_ctx"], 1)
                    dve.wait_ge(s["pv_done"], hd + 1)
                    dve.tensor_copy(u[:, hd, :], bank[:, 6 + hd % 2, :]).then_inc(s["o_ready"], 1)

            def layer_norm(n, l, row, over, cols, meanwhile=None):
                T = cols.stop - cols.start
                for m in range(DC):
                    over(dve, m)
                    for seg in range(cols.start // SEQ, cols.stop // SEQ):
                        x = h[:, m, seg * SEQ:(seg + 1) * SEQ]
                        a = seg * SEQ - cols.start
                        last = dve.scalar_tensor_tensor(x, bank[:, m, a:a + SEQ], mod[:, row * DC + m, seg:seg + 1], x, ALU.mult, ALU.add)
                    last.then_inc(s["r_ready"], 1)
                dve.wait_ge(s["mean_done"], n + 1)
                for k in range(DC):
                    dve.scalar_tensor_tensor(h[:, k, cols], bank[:, 0, 0:T], -1.0 / D, h[:, k, cols],
                                             ALU.mult, ALU.add).then_inc(s["cent_ready"], 1)
                if meanwhile:
                    meanwhile()
                dve.wait_ge(s["var_std"], n + 1)
                dve.reciprocal(std[:, 1, 0:T], std[:, 0, 0:T])
                dve.drain()
                for k in range(DC):
                    dve.scalar_tensor_tensor(h[:, k, cols], h[:, k, cols], ln_g[row // 3][:, l, k:k + 1], std[:, 1, 0:T],
                                             ALU.mult, ALU.mult).then_inc(s["norm_ready"], 1)

            def split_lo(f, name, slot, turn, half):
                is_down = name.startswith("down")
                i = (FC if is_down else 0) + 2 * (SLOTS * turn + slot) + half
                q = ((FC if is_down else 0) + 2 * slot + half) % 3
                for piece in range(2):
                    dve.wait_ge(s["hi_ready"], 2 * (PARTS * f + i) + piece + 1)
                    if is_down:
                        a = slice(piece * HALF // 2, (piece + 1) * HALF // 2)
                        b = slice(HALF * half + piece * HALF // 2, HALF * half + (piece + 1) * HALF // 2)
                        last = dve.tensor_tensor(r(w_lo[:, q, a]), ring[:, PLAN.slot(name, slot), b], r(w_hi[:, q, a]), ALU.subtract)
                    else:
                        a = slice(piece * DC // 2, (piece + 1) * DC // 2)
                        raw = ring[:, PLAN.slot(name, slot), :].rearrange("p (k n) -> p k n", k=DC)[:, a, half * 2 * P:(half + 1) * 2 * P]
                        hi, lo = (w[:, q, :].rearrange("p (k n) -> p k n", k=DC)[:, a] for w in (w_hi, w_lo))
                        last = dve.tensor_tensor(r(lo), raw, r(hi), ALU.subtract)
                last.then_inc(s["lo_ready"], 1)

            def ffn(f, name, down, token, between=None):
                token()
                if between:
                    between()
                split_lo(f, name, 0, 0, 1)
                split_lo(f, name, 1, 0, 0)

                def pair(slot, turn, half, ahead, last=False):
                    i = 2 * (SLOTS * turn + slot) + half
                    q = (2 * slot + half) % 3
                    dve.wait_ge(s["silu_ready"], FC * f + i + 1)
                    dve.wait_ge(s["lo_ready"], PARTS * f + i + 2)
                    dve.tensor_tensor(whole[:, q, :], silu_g[:, q, :], bank[:, 2 * q + 1, 0:SEQ], ALU.mult).then_inc(s["pair_free"], 1)
                    if not last:
                        split_lo(f, *ahead)
                    dve.wait_ge(s["hid_hi"], FC * f + i + 1)
                    dve.tensor_tensor(r(hidden[:, i, 1, :]), whole[:, q, :], r(hidden[:, i, 0, :]), ALU.subtract).then_inc(s["hid_ready"], 1)
                    if last:
                        split_lo(f, *ahead)

                def next_part(slot, turn, half):
                    step = 1 + half
                    return (slot + step) % SLOTS, turn + (slot + step) // SLOTS, 1 - half

                with dve.Fori(0, 3) as i:
                    for slot in range(SLOTS):
                        for half in range(2):
                            pair(slot, i, half, (name, *next_part(slot, i, half)))
                pair(0, 3, 0, (name, 1, 3, 1))
                pair(0, 3, 1, (down, 0, 0, 0))
                pair(1, 3, 0, (down, 0, 0, 1))
                pair(1, 3, 1, (down, 1, 0, 0), True)
                with dve.Fori(0, 2) as i:
                    for slot in range(SLOTS):
                        for half in range(2):
                            split_lo(f, down, *next_part(slot, i, half))
                split_lo(f, down, 1, 2, 1)

            def gdn_gates():
                dve.wait_ge(s["gate_acts"], 1)
                ba = bank[:, 2, 0:TILES * 64].rearrange("p (t d w h) -> p t d w h", t=TILES, d=2, w=2)
                for d in range(2):
                    dve.tensor_tensor(soft[:, 0, d], ba[:, :, d, 1, :], wide(dt_bias[:, 16 * d:16 * d + 16], TILES, 1), ALU.add)
                dve.drain()
                dve.scalar_tensor_tensor(soft[:, 1], soft[:, 0], -1.0, soft[:, 0], ALU.mult, ALU.min).then_inc(s["ax_ready"], 1)
                dve.wait_ge(s["gate_acts"], 2)
                dve.scalar_tensor_tensor(soft[:, 0], soft[:, 0], 0.0, soft[:, 1], ALU.max, ALU.add)
                dve.drain()
                for d in range(2):
                    last = dve.scalar_tensor_tensor(G_[:, d], soft[:, 0, d], -1.0, wide(a_log[:, 16 * d:16 * d + 16], TILES, 1),
                                                    ALU.mult, ALU.mult)
                last.then_inc(s["g_ready"], 1)
                dve.wait_ge(s["gate_sums"], 2)
                half = bank[:, 3, 0:256].rearrange("p (w d t h) -> p w d t h", w=2, d=2, t=TILES)
                dve.tensor_copy(GCUM, half[:, 0])
                dve.tensor_copy(ETOT, half[:, 1])
                dve.drain()
                dve.tensor_tensor(ED, ETOT, GCUM, ALU.subtract).then_inc(s["gcum_ready"], 1)

            def gdn_tokens():
                for k in range(1, DC, 2):
                    dve.tensor_copy(r(gu_hi[:, k, :]), u[:, k, :])
                dve.drain()
                for k in range(1, DC, 2):
                    dve.tensor_tensor(r(gu_lo[:, k, :]), u[:, k, :], r(gu_hi[:, k, :]), ALU.subtract).then_inc(s["odd_lo"], 1)

            def gdn_group(g):
                raw = [k_fm[:, 0, :], k_fm[:, 1, :], q_fm[:, 0, :], q_fm[:, 1, :]] + [v_fm[:, j, :] for j in range(GH)]
                dve.memset(cin[:, :, :, 0:2], 0.0)
                dve.memset(cin[:, :, :, 2 + SEQ:4 + SEQ], 0.0)
                dve.wait_ge(s["gexp_ready"], 1)
                dve.tensor_copy(gst.rearrange("p k d t h -> p (k d t) h"),
                                gates.rearrange("p k d t h -> p (k d t) h")[:, :, bass.ds(g * GH, GH)]).then_inc(s["gst_ready"], 1)
                dve.tensor_copy(cst, conv5[:, g, :])
                dve.drain()

                def lengths(blocks):
                    for j in blocks:
                        dve.wait_ge(s["kq_std"], 3 * g + j + 1)
                        dve.reciprocal(gdn_std[:, j, :], gdn_std[:, j, :])
                        dve.drain()
                        if j < 2:
                            dve.tensor_tensor(k_fm[:, j, :], k_fm[:, j, :], gdn_std[:, j, :], ALU.mult).then_inc(s["kq_ready"], 1)
                        else:
                            qf = q_fm.rearrange("p a t -> p (a t)")
                            dve.scalar_tensor_tensor(qf, qf, P ** -0.5, gdn_std[:, j, :], ALU.mult, ALU.mult).then_inc(s["kq_ready"], 1)

                for b in range(8):
                    dve.wait_ge(s["cin_ready"], 8 * g + b + 1)
                    segs = slice(0, 1) if 2 <= b < 4 else slice(0, 2)
                    o = raw[b].rearrange("p (s t) -> p s t", t=SEQ)
                    for j in range(TAPS):
                        tap, w = cin[:, b % 2, segs, j:j + SEQ], cst[:, b * TAPS + j:b * TAPS + j + 1]
                        if j == 0:
                            last = dve.tensor_scalar(o, tap, w, None, ALU.mult)
                        else:
                            last = dve.scalar_tensor_tensor(o, tap, w, o, ALU.mult, ALU.add)
                        if j < TAPS - 1:
                            dve.drain()
                    last.then_inc(s["conv_done"], 1)
                    if b in (4, 5):
                        lengths((0, 1) if b == 4 else (2,))

                def differ(st):
                    for d in range(2):
                        t = SCAN[d][st]
                        dve.wait_ge(sd["gbc_done"], 2 * (4 * g + st + 1) + d - 1)
                        if st > LT_TILES:
                            dve.wait_ge(sd["at_ready"], 2 * (2 * g + st - LT_TILES) + d - 1)
                        for j in range(GH):
                            last = dve.tensor_scalar(E[:, d, j, :], bank[:, 4 * d + 3, j * P:(j + 1) * P], S_GCUM[:, d, t, j:j + 1], 0.0,
                                                     ALU.subtract, ALU.min)
                        last.then_inc(sd["diff_ready"], 1)

                differ(0)
                for j in range(GKH):
                    dve.wait_ge(s["kt_done"], GKH * g + j + 1)
                    dve.tensor_copy(k_tm[:, :, j, :], bank[:, 1 + j, :].rearrange("p (t q) -> p t q", t=TILES)).then_inc(s["kt_ready"], 1)
                dve.wait_ge(s["kk_done"], 3 * g + 3)
                for d in range(2):
                    last = dve.tensor_tensor(kq[:, d].rearrange("p t j q -> p (t j) q"), bank[:, 6, :].rearrange("p (n q) -> p n q", n=4),
                                             wide(tri[:, d, :], 4, 1), ALU.mult)
                last.then_inc(s["kqm_ready"], 1)
                dve.wait_ge(s["kk_ready"], 2 * g + 2)
                heads = lambda b: bank[:, b, :].rearrange("p (j q) -> p j q", j=GH)
                def triangle(st):
                    for d in range(2):
                        t = SCAN[d][st]
                        n = 4 * g + st
                        dve.wait_ge(sd["decay_ready"], 2 * (n + 1) + d - 1)
                        if st:
                            dve.wait_ge(sd["ml_ready"], 2 * (LEVELS * n) + d - 1)
                        for j in range(GH):
                            last = dve.scalar_tensor_tensor(LT[:, d, j, :], E[:, d, j, :], S_BETA[:, d, t, j:j + 1], kk[:, t, j // 2, :],
                                                            ALU.mult, ALU.mult)
                        last.then_inc(sd["lt_ready"], 1)

                def pairs_of_two(st):
                    for d in range(2):
                        dve.wait_ge(sd["ml_ready"], 2 * (LEVELS * (4 * g + st) + 1) + d - 1)
                        dve.tensor_tensor(XT[:, d], wide(ident, GH, 1), ML[:, d, 0], ALU.subtract).then_inc(sd["xt0_ready"], 1)

                triangle(0)
                pairs_of_two(0)
                for st in range(4):
                    n = 4 * g + st
                    for b in range(1, LEVELS):
                        for d in range(2):
                            if b == 1:
                                dve.wait_ge(sd["x0_ready"], 2 * (n + 1) + d - 1)
                            dve.wait_ge(sd["xy_done"], 2 * (6 * n + b) + d - 1)
                            dve.tensor_tensor(X[:, d], X[:, d], heads(4 * d + 1), ALU.subtract).then_inc(sd["xs_ready"], 1)
                        if b == 2 and st >= LT_TILES:
                            for d in range(2):
                                t = SCAN[d][st]
                                dve.wait_ge(sd["eg_ready"], 2 * (2 * g + st - 1) + d - 1)
                                pair = "p (a r) q -> p a r q"
                                q = QDS[st % 2][:, d].rearrange(pair, r=2)
                                dve.tensor_tensor(q, q, wide(q_fm[:, :, t * P:(t + 1) * P], 2, 2), ALU.mult).then_inc(sd["qd_ready"], 1)
                        if b == 2 and st:
                            for d in range(2):
                                t = SCAN[d][st]
                                dve.wait_ge(sd["ks_done"], 2 * (3 * g + st) + d - 1)
                                for j in range(GH):
                                    last = dve.scalar_tensor_tensor(R[:, d, j, :], bank[:, 4 * d + 3, j * P:(j + 1) * P], S_EG[:, d, t, j:j + 1],
                                                                    gv_tm[:, t, j, :], ALU.mult, ALU.subtract)
                                last.then_inc(sd["rest_ready"], 1)
                        if b == 3 and st < 3:
                            differ(st + 1)
                        if b == 5 and st < 3:
                            triangle(st + 1)
                    for d in range(2):
                        t = SCAN[d][st]
                        dve.wait_ge(sd["vn_done"], 2 * (n + 1) + d - 1)
                        for j in range(GH):
                            last = dve.tensor_scalar(V[:, d, j, :], bank[:, 4 * d + 3, j * P:(j + 1) * P], S_BETA[:, d, t, j:j + 1],
                                                     -1.0 if st else 1.0, ALU.mult, ALU.mult)
                        last.then_inc(sd["vn_ready"], 1)
                    if st < 3:
                        pairs_of_two(st + 1)
                    for d in range(2):
                        t = SCAN[d][st]
                        if st >= LT_TILES:
                            dve.wait_ge(sd["od_done"], 2 * (2 * g + st - 1) + d - 1)
                            o = o_acc[:, :, t * P:(t + 1) * P]
                            if st == LT_TILES:
                                dve.tensor_copy(o, heads(4 * d + 1)).then_inc(sd["od_ready"], 1)
                            else:
                                dve.tensor_tensor(o, o, heads(4 * d + 1), ALU.add).then_inc(sd["od_ready"], 1)
                        if st < 3:
                            dve.wait_ge(sd["su_done"], 2 * (3 * g + st + 1) + d - 1)
                            if st == 0:
                                dve.tensor_copy(state[:, d], heads(4 * d + 3)).then_inc(sd["su_ready"], 1)
                            else:
                                for j in range(GH):
                                    last = dve.scalar_tensor_tensor(state[:, d, j, :], state[:, d, j, :], S_ETOT[:, d, t, j:j + 1],
                                                                    bank[:, 4 * d + 3, j * P:(j + 1) * P], ALU.mult, ALU.add)
                                last.then_inc(sd["su_ready"], 1)
                gdn_tokens()
                for half in range(2):
                    two = slice(2 * half, 2 * half + 2)
                    dve.wait_ge(s["oacc_std"], 2 * g + half + 3)
                    dve.reciprocal(gdn_std[:, half, :], gdn_std[:, half, :])
                    dve.drain()
                    dve.scalar_tensor_tensor(o_acc[:, two, :], o_acc[:, two, :], gdn_norm, gdn_std[:, half, :].rearrange("p (a t) -> p a t", a=2),
                                             ALU.mult, ALU.mult)
                dve.drain()
                dve.tensor_tensor(y_all[:, bass.ds(g * GH, GH), :], o_acc, z_s, ALU.mult).then_inc(s["y_ready"], 1)

            def inverse_root(i):
                dve.wait_ge(s["std_ready"], i + 1)
                dve.reciprocal(std[:, 1, 0:SEQ], std[:, 0, 0:SEQ])
                dve.drain()

            def normed_x(o, j, k):
                return dve.scalar_tensor_tensor(o, h[:, k, 0:SEQ], norm_g[:, j, k:k + 1], std[:, 1, 0:SEQ], ALU.mult, ALU.mult)

            def pre_norm(i, j):
                inverse_root(i)
                for k in range(DC):
                    normed_x(u[:, k, 0:SEQ], j, k).then_inc(s["u_ready"], 1)

            def pre_norm_split(i, j, f, name):
                split_lo(f, name, 0, 0, 0)
                inverse_root(i)
                split_tokens(f, lambda o, k: normed_x(o, j, k))

            def post_norm(i, j, over):
                for m in range(DC):
                    over(dve, m)
                    dve.tensor_copy(yb[:, m, :], bank[:, m, 0:SEQ]).then_inc(s["yb_ready"], 1)
                inverse_root(i)
                for k in range(DC):
                    dve.scalar_tensor_tensor(yb[:, k, :], yb[:, k, :], norm_g[:, j, k:k + 1], std[:, 1, 0:SEQ], ALU.mult, ALU.mult)
                dve.drain()
                for k in range(DC):
                    dve.tensor_tensor(h[:, k, 0:SEQ], h[:, k, 0:SEQ], yb[:, k, :], ALU.add).then_inc(s["x_ready"], 1)
                dve.drain()

            def mixer(l):
                T = SEQ
                two = lambda b: bank[:, b, :].rearrange("p (a t) -> p a t", a=2)
                dve.wait_ge(s["gate_done"], l + 1)
                dve.tensor_scalar(gl_y, bank[:, 7, 0:T], b_gate, None, ALU.add).then_inc(s["gy_ready"], 1)
                dve.drain()
                dve.scalar_tensor_tensor(gl_e, gl_y, -1.0, gl_y, ALU.mult, ALU.min).then_inc(s["ge_ready"], 1)
                dve.memset(conv_in[:, :, 0:CONV_W - 1], 0.0)
                dve.wait_ge(s["sig_ready"], l + 1)
                dve.tensor_tensor(conv_in[:, :, CONV_W - 1:], two(2), sig_g, ALU.mult).then_inc(s["conv_u"], 1)
                dve.wait_ge(s["gln_ready"], l + 1)
                dve.scalar_tensor_tensor(gl_y, gl_y, 0.0, gl_e, ALU.min, ALU.subtract)
                dve.drain()
                dve.tensor_tensor_scan(gl_c, gl_y, gl_y, 0.0, ALU.add, ALU.bypass)
                dve.drain()
                for lv in range(8):
                    n = 2 << lv
                    cum = gl_c.rearrange("p (b n) -> p b n", n=n)
                    mid = cum[:, :, n // 2 - 1:n // 2].to_broadcast([P, T // n, n])
                    dve.tensor_tensor(dec[:, lv, :].rearrange("p (b n) -> p b n", n=n), cum, mid, ALU.subtract)
                dve.drain()
                dve.scalar_tensor_tensor(dec, dec, -1.0, dec, ALU.mult, ALU.min).then_inc(s["gabs_ready"], 1)
                dve.wait_ge(s["gdec_ready"], l + 1)
                dve.tensor_tensor(qe, dec, wide(gqk[:, 0, :], 8, 1), ALU.mult)
                dve.tensor_tensor(ke, dec, wide(gqk[:, 1, :], 8, 1), ALU.mult).then_inc(s["gqe_ready"], 1)
                dve.wait_ge(alibi_loaded, 16)
                for hd in range(SWA_HEADS):
                    dve.wait_ge(s["sw_done"], SWA_HEADS * l + hd + 1)
                    dve.tensor_tensor(swp[:, hd, 0, :], bank[:, hd, 0:P], alibi[:, hd, P:2 * P], ALU.add)
                    dve.tensor_tensor(swp[:, hd, 1:3, :], bank[:, hd, P:3 * P].rearrange("p (a q) -> p a q", a=2),
                                      alibi[:, hd, :].rearrange("p (a q) -> p a q", a=2), ALU.add).then_inc(s["swb_ready"], 1)
                dve.drain()
                dve.tensor_reduce(swm[:, :, 0], swp[:, :, 0, :], AX_X, ALU.max)
                dve.tensor_reduce(swm[:, :, 1], swp[:, :, 1:3, :].rearrange("p h a q -> p h (a q)"), AX_X, ALU.max)
                dve.drain()
                dve.tensor_tensor(swm, swm, wide(sinks, 2, 2), ALU.max)
                dve.drain()
                dve.tensor_scalar(swm, swm, -1.0, None, ALU.mult)
                dve.drain()
                dve.tensor_tensor(swe, swm, wide(sinks, 2, 2), ALU.add).then_inc(s["swm_ready"], 1)
                for t in range(2):
                    for hd in range(GLA_HEADS):
                        dve.wait_ge(s["gs_done"], 12 * l + 4 * t + hd + 1)
                        for b in range(2):
                            dve.tensor_tensor(att_l[:, hd % 2, 4 * b:4 * b + 4, :], bank[:, 2 * hd + b, :].rearrange("p (v q) -> p v q", v=4),
                                              gmask[:, 4 * b:4 * b + 4, :], ALU.mult)
                        dve.drain()
                        dve.tensor_reduce(att[:, hd, t, :], att_l[:, hd % 2].rearrange("p v q -> p q v"), AX_X, ALU.add).then_inc(s["att_ready"], 1)
                for hd in range(GLA_HEADS):
                    dve.wait_ge(s["gs_done"], 12 * l + 8 + hd + 1)
                    dve.tensor_copy(att[:, hd, 2, :], bank[:, 2 * hd, 0:P]).then_inc(s["att_ready"], 1)
                dve.wait_ge(s["cv_mean"], l + 1)
                for b in range(2):
                    last = dve.scalar_tensor_tensor(conv_y[:, b, :], bank[:, 7, 0:T], -1.0 / (2 * P), conv_y[:, b, :], ALU.mult, ALU.add)
                last.then_inc(s["cv_cent"], 1)
                dve.wait_ge(s["swe_ready"], l + 1)
                dve.tensor_tensor(sws, sws, swe, ALU.add)
                dve.drain()
                dve.reciprocal(sws, sws)
                dve.drain()
                for hd in range(SWA_HEADS):
                    dve.tensor_scalar(swp[:, hd, 0, :], swp[:, hd, 0, :], sws[:, hd, 0:1], None, ALU.mult)
                    last = dve.tensor_scalar(swp[:, hd, 1:3, :], swp[:, hd, 1:3, :], sws[:, hd, 1:2], None, ALU.mult)
                last.then_inc(s["swp_ready"], 1)
                dve.wait_ge(s["go_done"], l + 1)
                for b in range(2):
                    dve.tensor_copy(og[:, b, :], bank[:, b, 0:T]).then_inc(s["go_ready"], 1)
                dve.wait_ge(s["go_std"], l + 1)
                dve.reciprocal(std[:, 1, :], std[:, 0, :])
                dve.drain()
                for b in range(2):
                    dve.scalar_tensor_tensor(og[:, b, :], og[:, b, :], gla_norm[:, b:b + 1], std[:, 1, b * T:(b + 1) * T], ALU.mult, ALU.mult)
                dve.drain()
                dve.tensor_tensor(mix[:, 0:2, :], og, gr_s, ALU.mult).then_inc(s["gla_ready"], 1)
                dve.wait_ge(s["cv_std"], l + 1)
                dve.reciprocal(gl_y, gl_e)
                dve.drain()
                for b in range(2):
                    last = dve.scalar_tensor_tensor(conv_y[:, b, :], conv_y[:, b, :], conv_ln_g[:, b:b + 1], gl_y, ALU.mult, ALU.mult)
                last.then_inc(s["cv_norm"], 1)

            def over_down(name, layer=0):
                return lambda e, m: panel_over(e, name, m % SLOTS, m // SLOTS, layer)

            modulation(0, 1, 0, 40)
            modulate(0, 1)
            scaled([0, 1])
            mla()
            layer_norm(0, 0, 2, mla_out_over, slice(0, TOK))

            def modulate_split(f, n, seg, name=None):
                def token(o, k):
                    dve.wait_ge(s["h_ready"], DC * n + k + 1)
                    return shifted(o, 3, 4, k, seg)
                split_tokens(f, token)
                scaled([seg])
                if name:
                    split_lo(f, name, 0, 0, 0)

            ffn(0, "ffn0", "down0", lambda: modulate_split(0, 0, 0, "ffn0"), lambda: modulation(0, 2, 40, MB))
            layer_norm(1, 0, 5, over_down("down0"), slice(0, SEQ))
            ffn(1, "ffn0c", "down0c", lambda: modulate_split(1, 0, 1, "ffn0c"))
            layer_norm(2, 0, 5, over_down("down0c"), slice(SEQ, TOK))
            modulation(1, 3, 0, MB)
            dve.wait_ge(s["h_ready"], 3 * DC)
            modulate(0, 1)
            scaled([0])
            gdn_tokens()
            gdn_gates()
            with dve.Fori(0, GROUPS) as g:
                gdn_group(g)
            dve.wait_ge(s["parts_lo"], SPLITS * GROUPS + DC // 2)
            dve.sem_inc(s["layer_done"], 1)
            layer_norm(3, 1, 2, gdn_out_over, slice(0, SEQ), lambda: split_lo(2, "ffn1", 0, 0, 0))
            ffn(2, "ffn1", "down1", lambda: modulate_split(2, 3, 0))
            layer_norm(4, 1, 5, over_down("down1"), slice(0, SEQ))
            dve.wait_ge(s["h_ready"], NORMS * DC)
            dve.sem_inc(s["x_ready"], DC)
            with dve.Fori(0, DEPTH) as l:
                dve.wait_ge(lpar_loaded, 16 * l + 16)
                ffn(2 * l + 3, "ffnA", "downA", lambda: pre_norm_split(6 * l, 0, 2 * l + 3, "ffnA"))
                post_norm(6 * l + 1, 1, over_down("downA", l))
                pre_norm(6 * l + 2, 2)
                mixer(l)
                post_norm(6 * l + 3, 3, lambda e, m: mix_out_over(e, m, l))
                ffn(2 * l + 4, "ffnB", "downB", lambda: pre_norm_split(6 * l + 4, 4, 2 * l + 4, "ffnB"))
                post_norm(6 * l + 5, 5, over_down("downB", l))
                dve.sem_inc(s["layer_done"], 1)


def chunks(w):
    k, n = w.shape
    return w.reshape(k // P, P, n).transpose(1, 0, 2)


def vec(v):
    v = v.reshape(-1, P)
    return v.T


def constants():
    t = np.arange(P)
    c = {"ones": np.ones((P, P)), "ident": np.eye(P), "ones64": (t[:, None] // 64 == t[None, :] // 64) * 1.0}
    c["tri"] = np.concatenate([t[:, None] <= t[None, :], t[:, None] >= t[None, :]], 1) * 1.0
    levels = []
    for d in range(2):
        for b in range(LEVELS):
            same = t[:, None] >> (b + 1) == t[None, :] >> (b + 1)
            first, second = (t >> b) % 2 == 0, (t >> b) % 2 == 1
            levels.append((same & first[:, None] & second[None, :]) if d == 0 else (same & second[:, None] & first[None, :]))
    c["level"] = np.concatenate(levels, 1) * 1.0
    f32 = np.float32
    tok = np.arange(SEQ)
    n_freq = ROPE // 4
    inv = f32(ROPE_THETA) ** (-(f32(2.0) * np.arange(n_freq, dtype=f32)) / f32(ROPE // 2))
    ang = np.stack([(tok // GRID_W).astype(f32)[:, None] * inv, (tok % GRID_W).astype(f32)[:, None] * inv], 1)
    cos, sin = np.cos(ang), np.sin(ang)
    f = np.arange(P) % ROPE
    axis, half, i = f // 32, f // 16 % 2, f % 16
    c["rope_cos"] = cos[:, axis, i].T
    c["rope_sin"] = (sin[:, axis, i] * np.where(half == 0, -1, 1)).T
    return np.ascontiguousarray(np.concatenate([c[n] for n, _ in CONSTS], 1), np.float32)


def slopes_and_mask():
    t = np.arange(P)
    slopes = np.exp2(-8.0 * (np.arange(SWA_HEADS) + 1.0) / SWA_HEADS)
    dist = t[:, None] - np.arange(2 * P)[None, :] + P
    valid = (dist >= 0) & (dist < P)
    return np.concatenate([np.where(valid, -sl * dist, NEG) for sl in slopes], 1).astype(np.float32)


def panel(blocks):
    w = np.concatenate(blocks, 2).reshape(P, -1)
    assert w.shape[1] == PANEL, w.shape
    return w


def ffn_panels(gate, up):
    g, v = chunks(gate), chunks(up)
    col = lambda w, b: w[:, :, b * P:(b + 1) * P]
    return [panel([col(g, 2 * p), col(v, 2 * p), col(g, 2 * p + 1), col(v, 2 * p + 1)]) for p in range(FC // 2)]


def down_panels(w):
    w = chunks(w)
    return [w[:, :, m * P:(m + 1) * P].reshape(P, -1) for m in range(DC)]


def wide_panels(w, n):
    w = chunks(w)
    return [panel([w[:, :, a:a + n]]) for a in range(0, w.shape[2], n)]


def layout(a):
    tokens = np.concatenate([a["x"][0], a["ctx"][0]], 0)
    h_in = np.ascontiguousarray(tokens.T.reshape(DC, P, TOK).transpose(1, 0, 2))

    spread = lambda v: np.broadcast_to(v.reshape(1, -1), (P, v.size))
    conv = a["gdn_conv"][0]
    def taps(g):
        heads = [2 * g, 2 * g + 1]
        starts = [D + hd * P for hd in heads] + [hd * P for hd in heads] + [2 * D + (GH * g + j) * P for j in range(GH)]
        return np.concatenate([conv[:, st:st + P].T for st in starts], 1)
    pieces = {
        "b_mod": vec(a["b_mod"]), "ln1_g": vec(a["ln1_g"]), "ln1_b": vec(a["ln1_b"]), "ln2_g": vec(a["ln2_g"]),
        "ln2_b": vec(a["ln2_b"]), "q_norm": vec(a["mla_q_norm"]), "kv_norm": vec(a["mla_kv_norm"]),
        "conv5": np.concatenate([taps(g) for g in range(GROUPS)], 1), "gdn_norm": vec(a["gdn_norm"]),
        "a_log": spread(a["gdn_a_log"]), "dt_bias": spread(a["gdn_dt_bias"]),
        "w_ba": chunks(a["gdn_w_in"][0][:, 4 * D + GDN_VW:]).reshape(P, -1),
        "cvec": np.stack([vec(a["c"]), vec(a["c_ctx"])], 2).reshape(P, -1),
        "eps": spread(np.array([RMS_EPS, LN_EPS, 4 * RMS_EPS, 1.0], np.float32)),
    }
    params = np.ascontiguousarray(np.concatenate([pieces[n] for n, _ in PARAMS], 1))
    lparams = []
    for l in range(DEPTH):
        rank = a["gla_w_gate2_2"][l]
        cw = a["conv_w_2"][l].T.reshape(2, P, CONV_W).transpose(1, 0, 2).reshape(P, -1)
        q = {
            "norm_g": vec(a["norm_g_2"][l]), "glr": chunks(a["w_in_2"][l][:, 768:768 + GLA_RANK]).reshape(P, -1),
            "gate2": np.concatenate([rank, np.zeros((P - GLA_RANK, P), rank.dtype)], 0), "b_gate": vec(a["gla_b_gate_2"][l]),
            "gla_norm": vec(a["gla_norm_g_2"][l]), "conv31": cw, "conv_b": vec(a["conv_b_2"][l]),
            "conv_ln_g": vec(a["conv_ln_g_2"][l]), "conv_ln_b": vec(a["conv_ln_b_2"][l]), "sinks": spread(a["swa_sinks_2"][l]),
        }
        lparams.append(np.concatenate([q[n] for n, _ in LPARAMS], 1))
    lparams = np.ascontiguousarray(np.stack(lparams))

    rows = {True: [], False: []}
    def add(name, more):
        rows[name.startswith("down")] += more
    swap = np.arange(ROPE).reshape(2, 2, 16)[:, ::-1].reshape(-1)
    w_in = chunks(a["mla_w_in"][0])
    kr = w_in[:, :, Q_RANK + KV_RANK:]
    krs = kr[:, :, swap]
    q_up = chunks(a["mla_w_q_up"][0]).reshape(P, QC, HEADS, NOPE + ROPE)
    q_rope = q_up[..., NOPE:]
    kv_up = chunks(a["mla_w_kv_up"][0]).reshape(P, KC, HEADS, NOPE + VDIM)
    flat = lambda w: w.reshape(w.shape[0], w.shape[1], -1)
    mods = [wide_panels(w, 512) for w in a["w_mod"]]
    add("mod0", mods[0][:10])
    add("mla", [panel([w_in[:, :, 0:512]]), panel([w_in[:, :, 512:Q_RANK + KV_RANK], kr, kr, krs, krs]),
                panel([flat(q_up[..., :NOPE])]), panel([flat(q_rope), flat(q_rope[..., swap])]),
                panel([flat(kv_up[..., :NOPE]), flat(kv_up[..., NOPE:])])] + wide_panels(a["mla_w_out"][0], 512))
    add("mod0b", mods[0][10:])
    for l in range(DEPTH):
        w = a["w_ffn_in"][l]
        if l == 1:
            add("mod1", mods[1][:3])
            add("mod1b", mods[1][3:])
            gw = chunks(a["gdn_w_in"][0])
            for g in range(GROUPS):
                two = lambda at: gw[:, :, at + 2 * P * g:at + 2 * P * g + 2 * P]
                four = lambda at: gw[:, :, at + 4 * P * g:at + 4 * P * g + 4 * P]
                add("gdn", [panel([two(D), two(0)]), panel([four(2 * D)]), panel([four(4 * D)])])
            add("gdn_out", wide_panels(a["gdn_w_out"][0], 2 * P))
        add(f"ffn{l}", ffn_panels(w[:, :D_FF], w[:, D_FF:]))
        add(f"down{l}", down_panels(a["w_ffn_out"][l]))
    for l in range(DEPTH):
        w = chunks(a["w_in_2"][l])
        swq = w[:, :, 1296:1808].reshape(P, DC, 2, 4, SWA_DH).transpose(0, 1, 3, 2, 4).reshape(P, DC, 512)
        wo = a["w_out_2"][l]
        wo = np.concatenate([wo[:512], wo[512:].reshape(2, 4, SWA_DH, D).transpose(1, 0, 2, 3).reshape(512, D)], 0)
        add("ffnA", ffn_panels(a["ffn_w_gate_2"][l, 0], a["ffn_w_up_2"][l, 0]))
        add("downA", down_panels(a["ffn_w_down_2"][l, 0]))
        add("mix_in", [panel([w[:, :, 784:1296]]), panel([w[:, :, 0:256], w[:, :, 512:768]]), panel([swq]),
                       panel([w[:, :, 1808:1936], w[:, :, 256:512], w[:, :, 1936:2064]])])
        add("mix_out", wide_panels(wo, 512))
        add("ffnB", ffn_panels(a["ffn_w_gate_2"][l, 1], a["ffn_w_up_2"][l, 1]))
        add("downB", down_panels(a["ffn_w_down_2"][l, 1]))
    panels, downs = np.stack(rows[False]), np.stack(rows[True])

    return {"h_in": h_in, "params": params, "lparams": lparams, "consts": constants(),
            "slopes": slopes_and_mask().reshape(P, SWA_HEADS, 2 * P), "panels": panels, "downs": downs}


def kernel(**inputs):
    import concourse.bacc as bacc
    from concourse.bass_utils import run_bass_kernel_spmd

    arrays = layout({k: np.asarray(v) for k, v in inputs.items()})
    nc = bacc.Bacc("TRN2", target_bir_lowering=False, num_devices=1)
    args = [nc.dram_tensor(n, v.shape, F32, kind="ExternalInput").ap() for n, v in arrays.items()]
    args.append(nc.dram_tensor("out", (P, DC, SEQ), F32, kind="ExternalOutput").ap())
    build(nc, *args)
    r = run_bass_kernel_spmd(nc, [arrays], core_ids=[0])
    got = r.results[0]["out"]
    return np.ascontiguousarray(got.transpose(2, 1, 0).reshape(1, SEQ, D))
```
